# Optimizing a Trainium2 kernel written in Bass

```python
import jax, jax.numpy as jnp
from jax import lax
import numpy as np

D_MODEL = 1024
BATCH = 1
SEQ = 512
DEPTH = 2

N_A_LAYERS = DEPTH // 2
N_B_LAYERS = DEPTH - N_A_LAYERS
SSM_EXPAND = 2
D_INNER = SSM_EXPAND * D_MODEL
SSM_HEAD_DIM = 64
SSM_HEADS = D_INNER // SSM_HEAD_DIM
SSM_GROUPS = 4
SSM_HPG = SSM_HEADS // SSM_GROUPS
D_STATE = 128
CONV_WIDTH = 4
CONV_CH = D_INNER + 2 * SSM_GROUPS * D_STATE
SSM_IN = D_INNER + CONV_CH + SSM_HEADS
CHUNK = 128
ATT_HEADS = 16
KV_HEADS = 4
HEAD_DIM = 64
Q_PER_KV = ATT_HEADS // KV_HEADS
ATT_WIDTH = ATT_HEADS * HEAD_DIM
KV_WIDTH = KV_HEADS * HEAD_DIM
WINDOW = 128
BLOCK = WINDOW
ROPE_THETA = 10000.0
PLE_DIM = 256
EPS = 1e-6


def rms_norm(x, w):
    xf = x.astype(jnp.float32)
    y = xf * lax.rsqrt(jnp.mean(xf * xf, axis=-1, keepdims=True) + EPS)
    return (y * w.astype(jnp.float32)).astype(x.dtype)

def rope(x, positions):
    half = HEAD_DIM // 2
    inv_freq = ROPE_THETA ** (-(jnp.arange(half, dtype=jnp.float32) * 2.0 / HEAD_DIM))
    ang = positions.astype(jnp.float32)[..., None] * inv_freq
    cos = jnp.cos(ang)[:, :, None, :]
    sin = jnp.sin(ang)[:, :, None, :]
    xf = x.astype(jnp.float32)
    x1, x2 = xf[..., :half], xf[..., half:]
    return jnp.concatenate([x1 * cos - x2 * sin, x2 * cos + x1 * sin], axis=-1).astype(x.dtype)

def ssd_chunked(xs, dt, a, bm, cm):
    b, s = xs.shape[:2]
    nc = s // CHUNK
    x = xs.astype(jnp.float32).reshape(b, nc, CHUNK, SSM_GROUPS, SSM_HPG, SSM_HEAD_DIM)
    dt = dt.reshape(b, nc, CHUNK, SSM_GROUPS, SSM_HPG)
    bm = bm.astype(jnp.float32).reshape(b, nc, CHUNK, SSM_GROUPS, D_STATE)
    cm = cm.astype(jnp.float32).reshape(b, nc, CHUNK, SSM_GROUPS, D_STATE)
    a_cum = jnp.cumsum(dt * a.reshape(SSM_GROUPS, SSM_HPG), axis=2)
    xdt = x * dt[..., None]
    seg = a_cum[:, :, :, None] - a_cum[:, :, None, :]
    causal = jnp.tril(jnp.ones((CHUNK, CHUNK), bool))[None, None, :, :, None, None]
    decay = jnp.exp(jnp.where(causal, seg, -jnp.inf))
    cb = jnp.einsum('bcign,bcjgn->bcijg', cm, bm)
    y_diag = jnp.einsum('bcijg,bcijgr,bcjgrp->bcigrp', cb, decay, xdt)
    decay_to_end = jnp.exp(a_cum[:, :, -1:] - a_cum)
    states = jnp.einsum('bcjgn,bcjgr,bcjgrp->bcgrpn', bm, decay_to_end, xdt)
    chunk_decay = jnp.exp(a_cum[:, :, -1])

    def step(carry, inp):
        st, dec = inp
        return carry * dec[..., None, None] + st, carry

    init = jnp.zeros((b, SSM_GROUPS, SSM_HPG, SSM_HEAD_DIM, D_STATE), jnp.float32)
    _, prev = lax.scan(step, init, (jnp.moveaxis(states, 1, 0), jnp.moveaxis(chunk_decay, 1, 0)))
    prev = jnp.moveaxis(prev, 0, 1)
    y_off = jnp.einsum('bcign,bcgrpn,bcigr->bcigrp', cm, prev, jnp.exp(a_cum))
    return (y_diag + y_off).reshape(b, s, SSM_HEADS, SSM_HEAD_DIM)

def mamba2_mixer(h, norm_w, in_w, conv_w, conv_b, dt_bias, a_log, d_skip, gnorm_w, out_w):
    b, s, _ = h.shape
    u = rms_norm(h, norm_w)
    zxbcdt = u @ in_w
    z, xbc, dt = jnp.split(zxbcdt, [D_INNER, D_INNER + CONV_CH], axis=-1)
    xbc = lax.conv_general_dilated(xbc, conv_w[:, None, :], window_strides=(1,),
                                   padding=[(CONV_WIDTH - 1, 0)],
                                   dimension_numbers=('NWC', 'WIO', 'NWC'),
                                   feature_group_count=CONV_CH) + conv_b
    xbc = jax.nn.silu(xbc)
    xs, bm, cm = jnp.split(xbc, [D_INNER, D_INNER + SSM_GROUPS * D_STATE], axis=-1)
    xs = xs.reshape(b, s, SSM_HEADS, SSM_HEAD_DIM)
    bm = bm.reshape(b, s, SSM_GROUPS, D_STATE)
    cm = cm.reshape(b, s, SSM_GROUPS, D_STATE)
    dt = jax.nn.softplus(dt.astype(jnp.float32) + dt_bias.astype(jnp.float32))
    a = -jnp.exp(a_log.astype(jnp.float32))
    y = ssd_chunked(xs, dt, a, bm, cm)
    y = y + d_skip.astype(jnp.float32)[:, None] * xs.astype(jnp.float32)
    y = y.reshape(b, s, D_INNER) * jax.nn.silu(z.astype(jnp.float32))
    yg = y.reshape(b, s, SSM_GROUPS, D_INNER // SSM_GROUPS)
    yg = yg * lax.rsqrt(jnp.mean(yg * yg, axis=-1, keepdims=True) + EPS)
    y = yg.reshape(b, s, D_INNER) * gnorm_w.astype(jnp.float32)
    return y.astype(h.dtype) @ out_w

def shared_kv(h, positions, kv_norm_w, kv_w, k_norm_w):
    b, s, _ = h.shape
    u = rms_norm(h, kv_norm_w)
    k, v = jnp.split(u @ kv_w, 2, axis=-1)
    k = k.reshape(b, s, KV_HEADS, HEAD_DIM)
    v = v.reshape(b, s, KV_HEADS, HEAD_DIM)
    k = rope(rms_norm(k, k_norm_w), positions)
    return k, v

def swa_sink_attention(q, k, v, sinks):
    b, s = q.shape[:2]
    nb = s // BLOCK
    qb = q.reshape(b, nb, BLOCK, KV_HEADS, Q_PER_KV, HEAD_DIM)

    def with_prev(t):
        t = t.reshape(b, nb, BLOCK, KV_HEADS, HEAD_DIM)
        prev = jnp.pad(t, ((0, 0), (1, 0), (0, 0), (0, 0), (0, 0)))[:, :-1]
        return jnp.concatenate([prev, t], axis=2)

    kk, vv = with_prev(k), with_prev(v)
    scores = jnp.einsum('bnqhgd,bnkhd->bnhgqk', qb, kk).astype(jnp.float32) * (HEAD_DIM ** -0.5)
    blk = jnp.arange(nb)[:, None, None] * BLOCK
    q_pos = blk + jnp.arange(BLOCK)[None, :, None]
    k_pos = blk - BLOCK + jnp.arange(2 * BLOCK)[None, None, :]
    valid = (k_pos <= q_pos) & (q_pos - k_pos < WINDOW) & (k_pos >= 0)
    scores = jnp.where(valid[None, :, None, None], scores, -jnp.inf)
    sink = sinks.astype(jnp.float32).reshape(KV_HEADS, Q_PER_KV)[None, None, :, :, None, None]
    m = jnp.maximum(jnp.max(scores, axis=-1, keepdims=True), sink)
    e = jnp.exp(scores - m)
    probs = e / (jnp.sum(e, axis=-1, keepdims=True) + jnp.exp(sink - m))
    out = jnp.einsum('bnhgqk,bnkhd->bnqhgd', probs.astype(v.dtype), vv)
    return out.reshape(b, s, ATT_WIDTH)

def swa_layer(h, k, v, positions, norm_w, in_w, q_norm_w, sinks, out_w):
    b, s, _ = h.shape
    u = rms_norm(h, norm_w)
    q, gate = jnp.split(u @ in_w, 2, axis=-1)
    q = rope(rms_norm(q.reshape(b, s, ATT_HEADS, HEAD_DIM), q_norm_w), positions)
    o = swa_sink_attention(q, k, v, sinks)
    return (o * jax.nn.silu(gate)) @ out_w

def per_layer_embedding(h, p_i, norm_w, gate_w, proj_w):
    g = jax.nn.sigmoid((rms_norm(h, norm_w) @ gate_w).astype(jnp.float32))
    return (g * (p_i @ proj_w).astype(jnp.float32)).astype(h.dtype)

def first_inputs(seed: int = 0) -> dict:
    key = jax.random.key(seed)
    ks = jax.random.split(key, 24)
    f32 = jnp.float32

    def nrm(k, shape, scale):
        return jax.random.normal(k, shape, f32) * scale

    dt0 = jnp.exp(jax.random.uniform(ks[7], (N_A_LAYERS, SSM_HEADS), f32, np.log(1e-3), np.log(1e-1)))
    offs = jax.random.randint(ks[3], (BATCH, 1), 0, 1024, jnp.int32)
    return {
        'x': nrm(ks[0], (BATCH, SEQ, D_MODEL), 1.0),
        'p': nrm(ks[1], (DEPTH, BATCH, SEQ, PLE_DIM), 1.0),
        'positions': (offs + jnp.arange(SEQ, dtype=jnp.int32)[None, :]).astype(jnp.int32),
        'ssm_norm_w': 1.0 + nrm(ks[2], (N_A_LAYERS, D_MODEL), 0.05),
        'ssm_in_w': nrm(ks[4], (N_A_LAYERS, D_MODEL, SSM_IN), D_MODEL ** -0.5),
        'ssm_conv_w': nrm(ks[5], (N_A_LAYERS, CONV_WIDTH, CONV_CH), CONV_WIDTH ** -0.5),
        'ssm_conv_b': nrm(ks[6], (N_A_LAYERS, CONV_CH), 0.02),
        'ssm_dt_bias': dt0 + jnp.log(-jnp.expm1(-dt0)),
        'ssm_a_log': jnp.log(jax.random.uniform(ks[8], (N_A_LAYERS, SSM_HEADS), f32, 1.0, 16.0)),
        'ssm_d': 1.0 + nrm(ks[9], (N_A_LAYERS, SSM_HEADS), 0.1),
        'ssm_gnorm_w': 1.0 + nrm(ks[10], (N_A_LAYERS, D_INNER), 0.05),
        'ssm_out_w': nrm(ks[11], (N_A_LAYERS, D_INNER, D_MODEL), D_INNER ** -0.5),
        'kv_norm_w': 1.0 + nrm(ks[12], (D_MODEL,), 0.05),
        'kv_w': nrm(ks[13], (D_MODEL, 2 * KV_WIDTH), D_MODEL ** -0.5),
        'k_norm_w': 1.0 + nrm(ks[14], (HEAD_DIM,), 0.05),
        'attn_norm_w': 1.0 + nrm(ks[15], (N_B_LAYERS, D_MODEL), 0.05),
        'attn_in_w': nrm(ks[16], (N_B_LAYERS, D_MODEL, 2 * ATT_WIDTH), D_MODEL ** -0.5),
        'q_norm_w': 1.0 + nrm(ks[17], (N_B_LAYERS, HEAD_DIM), 0.05),
        'attn_sinks': nrm(ks[18], (N_B_LAYERS, ATT_HEADS), 0.5),
        'attn_out_w': nrm(ks[19], (N_B_LAYERS, ATT_WIDTH, D_MODEL), ATT_WIDTH ** -0.5),
        'ple_norm_w': 1.0 + nrm(ks[20], (DEPTH, D_MODEL), 0.05),
        'ple_gate_w': nrm(ks[21], (DEPTH, D_MODEL, D_MODEL), D_MODEL ** -0.5),
        'ple_proj_w': nrm(ks[22], (DEPTH, PLE_DIM, D_MODEL), 0.5 * PLE_DIM ** -0.5),
    }

def first_block(x, p, positions, ssm_norm_w, ssm_in_w, ssm_conv_w, ssm_conv_b, ssm_dt_bias, ssm_a_log,
              ssm_d, ssm_gnorm_w, ssm_out_w, kv_norm_w, kv_w, k_norm_w, attn_norm_w, attn_in_w,
              q_norm_w, attn_sinks, attn_out_w, ple_norm_w, ple_gate_w, ple_proj_w):
    h = x
    k_sh = None
    v_sh = None
    for i in range(DEPTH):
        if i < N_A_LAYERS:
            h = h + mamba2_mixer(h, ssm_norm_w[i], ssm_in_w[i], ssm_conv_w[i], ssm_conv_b[i],
                                 ssm_dt_bias[i], ssm_a_log[i], ssm_d[i], ssm_gnorm_w[i], ssm_out_w[i])
        else:
            if i == N_A_LAYERS:
                k_sh, v_sh = shared_kv(h, positions, kv_norm_w, kv_w, k_norm_w)
            j = i - N_A_LAYERS
            h = h + swa_layer(h, k_sh, v_sh, positions, attn_norm_w[j], attn_in_w[j], q_norm_w[j],
                              attn_sinks[j], attn_out_w[j])
        h = h + per_layer_embedding(h, p[i], ple_norm_w[i], ple_gate_w[i], ple_proj_w[i])
    return h


DEPTH_2 = 1

M_HEADS = 4
M_HEAD_DIM = 128
M_WIDTH = M_HEADS * M_HEAD_DIM
M_CHUNK = 64
A_HEADS = 8
A_KV_GROUPS = 2
A_HEAD_DIM = 64
A_WIDTH = A_HEADS * A_HEAD_DIM
KV_WIDTH_2 = A_KV_GROUPS * A_HEAD_DIM
CMP_BLOCK = 32
CMP_STRIDE = 16
CMP_HIDDEN = 128
SEL_BLOCK = 64
N_SELECT = 16
WINDOW_2 = 512
A_Q_BLOCK = 32
ALIBI_MAX = 8.0
MIX_WIDTH = M_WIDTH + A_WIDTH
IN_WIDTH = 4 * M_WIDTH + 2 * M_HEADS + A_WIDTH + 6 * KV_WIDTH_2 + 3 * A_HEADS
D_FF = 2048
CONV_WIDTH_2 = 3
NEG = -1e30
BIG = 1e30


def rms_norm_2(x, g):
    xf = x.astype(jnp.float32)
    y = xf * lax.rsqrt(jnp.mean(xf * xf, axis=-1, keepdims=True) + EPS)
    return (y * g.astype(jnp.float32)).astype(x.dtype)

def alibi_slopes(n):
    return jnp.exp2(-ALIBI_MAX * jnp.arange(1, n + 1, dtype=jnp.float32) / n)

def mlstm(q, k, v, i_pre, f_pre):
    B, S, H, dh = q.shape
    L = M_CHUNK
    NC = S // L
    f32 = jnp.float32

    def chunks(t):
        t = t.astype(f32).reshape((B, NC, L, H) + t.shape[3:])
        return jnp.moveaxis(t, 3, 1)

    qc = chunks(q) * (dh ** -0.5)
    kc = chunks(k)
    vc = chunks(v)
    ig = chunks(i_pre)
    b = jnp.cumsum(jax.nn.log_sigmoid(chunks(f_pre)), axis=-1)
    bL = b[..., -1]
    a = bL[..., None] - b + ig

    def step(carry, inp):
        C, n, m = carry
        k_, v_, a_, bL_ = inp
        m_new = jnp.maximum(bL_ + m, jnp.max(a_, axis=-1))
        decay = jnp.exp(bL_ + m - m_new)
        w = jnp.exp(a_ - m_new[..., None])
        C_new = decay[..., None, None] * C + jnp.einsum('bhl,bhlk,bhlv->bhkv', w, k_, v_)
        n_new = decay[..., None] * n + jnp.einsum('bhl,bhlk->bhk', w, k_)
        return (C_new, n_new, m_new), (C, n, m)

    init = (jnp.zeros((B, H, dh, dh), f32), jnp.zeros((B, H, dh), f32), jnp.zeros((B, H), f32))
    xs = (jnp.moveaxis(kc, 2, 0), jnp.moveaxis(vc, 2, 0), jnp.moveaxis(a, 2, 0), jnp.moveaxis(bL, 2, 0))
    _, (Cs, ns, ms) = lax.scan(step, init, xs)
    Cs = jnp.moveaxis(Cs, 0, 2)
    ns = jnp.moveaxis(ns, 0, 2)
    ms = jnp.moveaxis(ms, 0, 2)

    bq = b + ms[..., None]
    causal = jnp.tril(jnp.ones((L, L), dtype=bool))
    Dm = jnp.where(causal, b[..., :, None] - b[..., None, :] + ig[..., None, :], -jnp.inf)
    m = jnp.maximum(bq, jnp.max(Dm, axis=-1))
    inter = jnp.exp(bq - m)
    Wt = jnp.exp(Dm - m[..., None]) * jnp.einsum('bhcld,bhcsd->bhcls', qc, kc)
    num = inter[..., None] * jnp.einsum('bhcld,bhcdv->bhclv', qc, Cs) + jnp.einsum('bhcls,bhcsv->bhclv', Wt, vc)
    den = inter * jnp.einsum('bhcld,bhcd->bhcl', qc, ns) + jnp.sum(Wt, axis=-1)
    h = num / jnp.maximum(jnp.abs(den), jnp.exp(-m))[..., None]
    return jnp.moveaxis(h, 1, 3).reshape(B, S, H, dh)

def nsa(q, kc_raw, vc_raw, ks_raw, vs_raw, kw_raw, vw_raw, g_pre, pe_k, pe_v, ck_w1, ck_w2, cv_w1, cv_w2):
    f32 = jnp.float32
    B, S, H, dh = q.shape
    G = A_KV_GROUPS
    R = H // G
    qg = q.astype(f32).reshape(B, S, G, R, dh).transpose(0, 2, 3, 1, 4) * (dh ** -0.5)
    gates = jax.nn.sigmoid(g_pre.astype(f32).reshape(B, S, G, R, 3)).transpose(0, 2, 3, 1, 4)
    to_g = lambda t: t.astype(f32).transpose(0, 2, 1, 3)

    Nc = (S - CMP_BLOCK) // CMP_STRIDE + 1
    cidx = jnp.arange(Nc)[:, None] * CMP_STRIDE + jnp.arange(CMP_BLOCK)[None, :]

    def compress(t, pe, w1, w2):
        blk = to_g(t)[:, :, cidx] + pe.astype(f32)
        flat = blk.reshape(B, G, Nc, CMP_BLOCK * dh)
        return jax.nn.gelu(flat @ w1.astype(f32)) @ w2.astype(f32)

    Kc = compress(kc_raw, pe_k, ck_w1, ck_w2)
    Vc = compress(vc_raw, pe_v, cv_w1, cv_w2)
    cmp_start = jnp.arange(Nc) * CMP_STRIDE
    cmp_end = cmp_start + CMP_BLOCK - 1

    Ns = S // SEL_BLOCK
    n_sel = min(N_SELECT, Ns)
    Ks = to_g(ks_raw).reshape(B, G, Ns, SEL_BLOCK, dh)
    Vs = to_g(vs_raw).reshape(B, G, Ns, SEL_BLOCK, dh)
    sel_start = jnp.arange(Ns) * SEL_BLOCK
    overlap = ((cmp_start[:, None] <= sel_start[None, :] + SEL_BLOCK - 1)
               & (cmp_end[:, None] >= sel_start[None, :])).astype(f32)

    pad = ((0, 0), (0, 0), (WINDOW_2, 0), (0, 0))
    Kw = jnp.pad(to_g(kw_raw), pad)
    Vw = jnp.pad(to_g(vw_raw), pad)

    slope = alibi_slopes(H).reshape(1, G, R, 1, 1)
    bi = jnp.arange(B)[:, None, None, None]
    gi = jnp.arange(G)[None, :, None, None]
    T = A_Q_BLOCK

    def block(qb):
        t0 = qb * T
        t = t0 + jnp.arange(T)
        qblk = lax.dynamic_slice_in_dim(qg, t0, T, axis=3)
        gblk = lax.dynamic_slice_in_dim(gates, t0, T, axis=3)

        valid_c = cmp_end[None, :] <= t[:, None]
        dist_c = (t[:, None] - cmp_end[None, :]).astype(f32)
        s_c = jnp.einsum('bgrtd,bgnd->bgrtn', qblk, Kc) - slope * dist_c
        p_c = jnp.where(valid_c, jax.nn.softmax(jnp.where(valid_c, s_c, NEG), axis=-1), 0.0)
        o_c = jnp.einsum('bgrtn,bgnd->bgrtd', p_c, Vc)

        imp = jnp.einsum('bgrtn,nj->bgtj', p_c, overlap)
        j = jnp.arange(Ns)[None, :]
        cur = (t // SEL_BLOCK)[:, None]
        forced = (j == 0) | (j == cur) | (j == cur - 1)
        causal_b = sel_start[None, :] <= t[:, None]
        score = jnp.where(causal_b, jnp.where(forced, BIG, imp), NEG)
        sel_idx = lax.top_k(score, n_sel)[1]
        Ksel = Ks[bi, gi, sel_idx]
        Vsel = Vs[bi, gi, sel_idx]
        pos_s = sel_idx[..., None] * SEL_BLOCK + jnp.arange(SEL_BLOCK)
        dist_s = (t[None, None, :, None, None] - pos_s)
        valid_s = (dist_s >= 0)[:, :, None]
        s_s = jnp.einsum('bgrtd,bgtnld->bgrtnl', qblk, Ksel) - slope[..., None] * dist_s[:, :, None].astype(f32)
        s_s = jnp.where(valid_s, s_s, NEG).reshape(B, G, R, T, n_sel * SEL_BLOCK)
        p_s = jax.nn.softmax(s_s, axis=-1).reshape(B, G, R, T, n_sel, SEL_BLOCK)
        o_s = jnp.einsum('bgrtnl,bgtnld->bgrtd', p_s, Vsel)

        kwin = lax.dynamic_slice_in_dim(Kw, t0, WINDOW_2 + T, axis=2)
        vwin = lax.dynamic_slice_in_dim(Vw, t0, WINDOW_2 + T, axis=2)
        pos_w = t0 - WINDOW_2 + jnp.arange(WINDOW_2 + T)
        dist_w = t[:, None] - pos_w[None, :]
        valid_w = (pos_w[None, :] >= 0) & (dist_w >= 0) & (dist_w < WINDOW_2)
        s_w = jnp.einsum('bgrtd,bgsd->bgrts', qblk, kwin) - slope * dist_w.astype(f32)
        p_w = jax.nn.softmax(jnp.where(valid_w, s_w, NEG), axis=-1)
        o_w = jnp.einsum('bgrts,bgsd->bgrtd', p_w, vwin)

        return gblk[..., 0:1] * o_c + gblk[..., 1:2] * o_s + gblk[..., 2:3] * o_w

    outs = lax.map(block, jnp.arange(S // T))
    return outs.transpose(1, 0, 4, 2, 3, 5).reshape(B, S, H * dh)

def conv_ffn(h, w_up, conv_w, conv_b, w_down):
    u = h @ w_up
    gate, val = jnp.split(u, 2, axis=-1)
    gate = lax.conv_general_dilated(gate, conv_w[:, None, :].astype(gate.dtype), window_strides=(1,),
                                    padding=[(CONV_WIDTH_2 - 1, 0)],
                                    dimension_numbers=('NWC', 'WIO', 'NWC'),
                                    feature_group_count=D_FF) + conv_b
    return (jax.nn.silu(gate) * val) @ w_down

def second_inputs(seed: int = 0) -> dict:
    key = jax.random.key(seed)
    ks = jax.random.split(key, 24)
    f32 = jnp.float32
    nrm = lambda k, shape, scale: jax.random.normal(k, shape, f32) * scale
    gain = lambda k, shape: 1.0 + 0.05 * jax.random.normal(k, shape, f32)
    i_bias = nrm(ks[4], (DEPTH_2, M_HEADS), 0.1)
    f_bias = jnp.linspace(3.0, 6.0, M_HEADS, dtype=f32)[None, :] + nrm(ks[5], (DEPTH_2, M_HEADS), 0.1)
    return {
        "x": nrm(ks[0], (BATCH, SEQ, D_MODEL), 1.0),
        "p": nrm(ks[1], (DEPTH_2, BATCH, SEQ, PLE_DIM), 1.0),
        "ln1_g": gain(ks[2], (DEPTH_2, D_MODEL)),
        "w_in": nrm(ks[3], (DEPTH_2, D_MODEL, IN_WIDTH), D_MODEL ** -0.5),
        "mlstm_gate_bias": jnp.concatenate([i_bias, f_bias], axis=-1),
        "mlstm_norm_g": gain(ks[6], (DEPTH_2, M_WIDTH)),
        "cmp_pos_k": nrm(ks[7], (DEPTH_2, CMP_BLOCK, A_HEAD_DIM), 0.02),
        "cmp_pos_v": nrm(ks[8], (DEPTH_2, CMP_BLOCK, A_HEAD_DIM), 0.02),
        "cmp_k_w1": nrm(ks[9], (DEPTH_2, CMP_BLOCK * A_HEAD_DIM, CMP_HIDDEN), (CMP_BLOCK * A_HEAD_DIM) ** -0.5),
        "cmp_k_w2": nrm(ks[10], (DEPTH_2, CMP_HIDDEN, A_HEAD_DIM), CMP_HIDDEN ** -0.5),
        "cmp_v_w1": nrm(ks[11], (DEPTH_2, CMP_BLOCK * A_HEAD_DIM, CMP_HIDDEN), (CMP_BLOCK * A_HEAD_DIM) ** -0.5),
        "cmp_v_w2": nrm(ks[12], (DEPTH_2, CMP_HIDDEN, A_HEAD_DIM), CMP_HIDDEN ** -0.5),
        "w_out": nrm(ks[13], (DEPTH_2, MIX_WIDTH, D_MODEL), MIX_WIDTH ** -0.5),
        "ln2_g": gain(ks[14], (DEPTH_2, D_MODEL)),
        "w_up": nrm(ks[15], (DEPTH_2, D_MODEL, 2 * D_FF), D_MODEL ** -0.5),
        "conv_w": nrm(ks[16], (DEPTH_2, CONV_WIDTH_2, D_FF), CONV_WIDTH_2 ** -0.5),
        "conv_b": nrm(ks[17], (DEPTH_2, D_FF), 0.02),
        "w_down": nrm(ks[18], (DEPTH_2, D_FF, D_MODEL), D_FF ** -0.5),
        "ple_norm_g": gain(ks[19], (DEPTH_2, D_MODEL)),
        "w_ple_gate": nrm(ks[20], (DEPTH_2, D_MODEL, D_MODEL), D_MODEL ** -0.5),
        "w_ple_proj": nrm(ks[21], (DEPTH_2, PLE_DIM, D_MODEL), PLE_DIM ** -0.5),
        "final_g": gain(ks[22], (D_MODEL,)),
    }

def second_block(x, p, ln1_g, w_in, mlstm_gate_bias, mlstm_norm_g, cmp_pos_k, cmp_pos_v, cmp_k_w1, cmp_k_w2,
              cmp_v_w1, cmp_v_w2, w_out, ln2_g, w_up, conv_w, conv_b, w_down, ple_norm_g, w_ple_gate,
              w_ple_proj, final_g):
    B, S, _ = x.shape
    sizes = [M_WIDTH] * 4 + [M_HEADS, M_HEADS, A_WIDTH] + [KV_WIDTH_2] * 6 + [3 * A_HEADS]
    offs = np.cumsum(sizes)[:-1].tolist()
    for i in range(DEPTH_2):
        h = rms_norm_2(x, ln1_g[i])
        z = h @ w_in[i]
        mq, mk, mv, mo, mi, mf, aq, akc, avc, aks, avs, akw, avw, ag = jnp.split(z, offs, axis=-1)
        mshape = (B, S, M_HEADS, M_HEAD_DIM)
        hm = mlstm(mq.reshape(mshape), mk.reshape(mshape), mv.reshape(mshape),
                   mi + mlstm_gate_bias[i, :M_HEADS], mf + mlstm_gate_bias[i, M_HEADS:])
        hm = rms_norm_2(hm, mlstm_norm_g[i].reshape(M_HEADS, M_HEAD_DIM)).reshape(B, S, M_WIDTH)
        m_out = (hm * jax.nn.sigmoid(mo.astype(jnp.float32))).astype(x.dtype)
        kvshape = (B, S, A_KV_GROUPS, A_HEAD_DIM)
        a_out = nsa(aq.reshape(B, S, A_HEADS, A_HEAD_DIM), akc.reshape(kvshape), avc.reshape(kvshape),
                    aks.reshape(kvshape), avs.reshape(kvshape), akw.reshape(kvshape), avw.reshape(kvshape),
                    ag, cmp_pos_k[i], cmp_pos_v[i], cmp_k_w1[i], cmp_k_w2[i], cmp_v_w1[i], cmp_v_w2[i]).astype(x.dtype)
        x = x + jnp.concatenate([m_out, a_out], axis=-1) @ w_out[i]
        x = x + conv_ffn(rms_norm_2(x, ln2_g[i]), w_up[i], conv_w[i], conv_b[i], w_down[i])
        gate = jax.nn.sigmoid(rms_norm_2(x, ple_norm_g[i]) @ w_ple_gate[i])
        x = x + gate * (p[i].astype(x.dtype) @ w_ple_proj[i])
    return rms_norm_2(x, final_g)


def setup_inputs(seed=0):
    out = dict(first_inputs(seed))
    for name, value in second_inputs(seed + 1).items():
        if name != "x":
            out[name + "_2"] = value
    return out


def reference(
    x, p, positions, ssm_norm_w, ssm_in_w, ssm_conv_w, ssm_conv_b, ssm_dt_bias, ssm_a_log,
    ssm_d, ssm_gnorm_w, ssm_out_w, kv_norm_w, kv_w, k_norm_w, attn_norm_w, attn_in_w, q_norm_w,
    attn_sinks, attn_out_w, ple_norm_w, ple_gate_w, ple_proj_w, p_2, ln1_g_2, w_in_2,
    mlstm_gate_bias_2, mlstm_norm_g_2, cmp_pos_k_2, cmp_pos_v_2, cmp_k_w1_2, cmp_k_w2_2,
    cmp_v_w1_2, cmp_v_w2_2, w_out_2, ln2_g_2, w_up_2, conv_w_2, conv_b_2, w_down_2,
    ple_norm_g_2, w_ple_gate_2, w_ple_proj_2, final_g_2,
):
    x = first_block(
        x, p, positions, ssm_norm_w, ssm_in_w, ssm_conv_w, ssm_conv_b, ssm_dt_bias, ssm_a_log,
        ssm_d, ssm_gnorm_w, ssm_out_w, kv_norm_w, kv_w, k_norm_w, attn_norm_w, attn_in_w,
        q_norm_w, attn_sinks, attn_out_w, ple_norm_w, ple_gate_w, ple_proj_w,
    )
    return second_block(
        x, p_2, ln1_g_2, w_in_2, mlstm_gate_bias_2, mlstm_norm_g_2, cmp_pos_k_2, cmp_pos_v_2,
        cmp_k_w1_2, cmp_k_w2_2, cmp_v_w1_2, cmp_v_w2_2, w_out_2, ln2_g_2, w_up_2, conv_w_2,
        conv_b_2, w_down_2, ple_norm_g_2, w_ple_gate_2, w_ple_proj_2, final_g_2,
    )


_drawn_inputs = setup_inputs


def setup_inputs(seed=0):
    import zlib

    import numpy as np

    out = dict(_drawn_inputs(seed))
    spreads = {}
    factors = {'kv_norm_w': 8.0,
     'k_norm_w': 8.0,
     'attn_norm_w': 8.0,
     'q_norm_w': 8.0,
     'attn_sinks': 27.468,
     'ple_norm_w': 8.0,
     'mlstm_norm_g_2': 200.0,
     'cmp_pos_k_2': 64.0,
     'cmp_pos_v_2': 64.0,
     'conv_b_2': 200.0,
     'ple_norm_g_2': 200.0,
     'p_2': 29.76,
     'ln1_g_2': 8.0,
     'cmp_k_w1_2': 8.0,
     'cmp_k_w2_2': 8.0,
     'cmp_v_w1_2': 8.0,
     'cmp_v_w2_2': 8.0,
     'ln2_g_2': 8.0,
     'w_up_2': 4.009,
     'conv_w_2': 4.366,
     'w_down_2': 4.009,
     'w_ple_gate_2': 44.512,
     'w_ple_proj_2': 29.744}
    for name, (base, spread) in spreads.items():
        noise = np.random.default_rng([zlib.crc32(name.encode()), seed]).standard_normal(out[name].shape)
        drawn = base * np.exp(spread * noise) if base else spread * noise
        out[name] = __import__('jax').numpy.asarray(drawn.astype(out[name].dtype))
    for name, factor in factors.items():
        out[name] = (out[name] * factor).astype(out[name].dtype)
    return out
```

```python
from contextlib import ExitStack

import numpy as np

import concourse.bass as bass
from concourse import mybir

F32 = mybir.dt.float32
I32 = mybir.dt.int32
ALU = mybir.AluOpType
ACT = mybir.ActivationFunctionType
AXX = mybir.AxisListType.X

P = 128
SEQ = 512
NT = SEQ // P
D = 1024
KD = D // P
EPS = 1e-6
NEG = -1e30

GROUPS = 4
HPG = 8
HEADS = GROUPS * HPG
HD = 64
D_INNER = 2048
GT = 4
D_STATE = 128
TAPS = 4
ATT_HEADS = 16
KV_HEADS = 4
M_HEADS = 4
A_HEADS = 8
NC_BLK = 31
CMP_BLOCK = 32
CMP_STRIDE = 16
D_FF = 2048
FT = D_FF // P
PLE = 256

NSLOT = 6
NROT = 6
BLK = 1024

NORMS = ["ssm", "kv", "attn", "ple0", "ple1", "ln1", "ln2", "ple2", "final"]
V_NORM = {n: 8 * i for i, n in enumerate(NORMS)}
V_CW = 72
V_CB = V_CW + TAPS * 24
V_GN = V_CB + 24
V_D = V_GN + 16
V_C2W = V_D + 16
V_C2B = V_C2W + 3 * FT
V_MN = V_C2B + FT
NV = V_MN + 4

R_DTB, R_ALOG, R_QN, R_QNS, R_KN, R_KNS, R_SINK, R_FREQ = 0, 32, 64, 128, 192, 256, 320, 336
NR = R_FREQ + 32

C_ID, C_T, C_U, C_ONE, C_SWA, C_CMP = 0, 128, 256, 384, 512, 768
C_RV = C_CMP + NT * A_HEADS * NC_BLK
C_SEL = C_RV + 1
NCON = C_SEL + 4 * P

NORM_OF = {0: ["ssm"], 1: ["ple0"], 2: ["kv", "attn"], 3: ["ple1"], 4: ["ln1"], 5: ["ln2"], 6: ["ple2"], 7: ["final"]}


def steps():
    out = [("load",), ("norm", 0)]
    proj = {g: [("proj", g, i) for i in range(10)] for g in range(GROUPS)}
    out += proj[0][:2] + [("dt",)] + proj[0][2:]
    for g in range(GROUPS):
        scan = [("ssd0", g), ("ssd1", g, 0), ("ssd1", g, 1), ("ssd2", g, 0), ("ssd1", g, 2), ("ssd2", g, 1),
                ("ssd1", g, 3), ("ssd2", g, 2), ("ssd2", g, 3), ("yt", g, 0), ("yt", g, 1), ("yt", g, 2), ("yt", g, 3),
                ("gn", g)]
        fill = proj[g + 1] if g + 1 < GROUPS else [("pp", 0, m) for m in range(KD)]
        k = 0
        for i, s in enumerate(scan):
            out.append(s)
            while k < len(fill) and k * len(scan) < (i + 1) * len(fill):
                out.append(fill[k])
                k += 1
        out += fill[k:]
    out += [("out", 1, m) for m in range(KD)] + [("norm", 1)]
    out += [("ple", 0, m) for m in range(KD)]
    out += [("norm", 2), ("rope_tables",), ("kv",), ("q", 0), ("kT",), ("q", 1), ("qT", 0)]
    out += [("gate", m) for m in range(4)] + [("qT", 1)] + [("gate", m) for m in range(4, KD)]
    units = [(n, g) for n in range(NT) for g in range(KV_HEADS)]
    out += [("aS", *units[0])]
    for a, b in zip(units, units[1:] + [None]):
        if b:
            out.append(("aS", *b))
        out.append(("aP", *a))
    out += [("out", 3, m) for m in range(KD)]
    out += [("pp", 1, m) for m in range(3)] + [("norm", 3)] + [("pp", 1, m) for m in range(3, KD)]
    out += [("ple", 1, m) for m in range(KD)]
    out += [("norm", 4), ("mif",), ("mrow",), ("cmp_in", 0), ("cmp_in", 1), ("mv",)]
    out += [("mq", m) for m in range(4)] + [("mrcol",)] + [("mk", m) for m in range(4)]
    out += [("aq", m) for m in range(4)] + [("ak", 0), ("ak", 1), ("avg",), ("mo", 0), ("mo", 1)]
    out += [("cmp", 0), ("cmp", 1), ("mo", 2), ("mo", 3), ("cmp2",)]
    out += [("mh", h) for h in range(M_HEADS)]
    out += [("mnorm", h) for h in range(M_HEADS)]
    seq = []
    for i in range(NT):
        for g in range(2):
            seq += [(i, g, "c"), (i, g, "s"), (i, g, "w")]
    out += [("nS", *seq[0])]
    for a, b in zip(seq, seq[1:] + [None]):
        if b:
            out.append(("nS", *b))
        out.append(("nP", *a))
    out += [("out", 5, m) for m in range(KD)] + [("norm", 5)]
    out += [("up", m) for m in range(FT)]
    out += [("out", 6, m) for m in range(KD)]
    out += [("pp", 2, m) for m in range(3)] + [("norm", 6)] + [("pp", 2, m) for m in range(3, KD)]
    out += [("ple", 2, m) for m in range(KD)]
    out += [("norm", 7)]
    return out


STEPS = steps()


def jobs_of(step):
    k, a = step[0], step[1:]
    if k == "norm":
        return [("ss", a[0])]
    if k == "dt":
        return [("dt",), ("cum",)]
    if k in ("proj", "pp", "out", "gate", "mq", "mk", "mo", "aq", "ak", "cmp_in", "gn", "yt"):
        return [step]
    if k == "ple":
        return [step]
    if k == "ssd0":
        return [("cb", *a), ("bt", *a)]
    if k == "ssd1":
        return [("xt", *a), ("seg", *a, 0), ("seg", *a, 1)]
    if k == "ssd2":
        g, c = a
        return [("yd", g, c)] + ([("yo", g, c)] if c else []) + ([("st", g, c)] if c < NT - 1 else [])
    if k in ("kv", "mv", "avg"):
        return [(k, t) for t in range(NT)]
    if k == "q":
        return [("q", a[0], t) for t in range(NT)]
    if k == "kT":
        return [("kT", t) for t in range(NT)]
    if k == "qT":
        return [("qT", a[0], t) for t in range(NT)]
    if k == "aS":
        return [("aS", *a, j) for j in range(1 if a[0] == 0 else 2)]
    if k == "aP":
        return [("aPT", *a, kt) for kt in range(1 if a[0] == 0 else 2)]
    if k == "mif":
        return [("mi",), ("mf",)]
    if k == "mrcol":
        return [("mrcol",)]
    if k == "mh":
        h = a[0]
        return [("Mb", h)] + [("KQ", h, s) for s in range(NT)] + [("En", h)]
    if k == "mnorm":
        return [("mss", a[0])]
    if k == "cmp":
        return [("chid", a[0], g) for g in range(2)]
    if k == "cmp2":
        return [("ckT",), ("cv",)]
    if k == "nS":
        return [("nS", *a, r) for r in range(1 if a[2] == "c" else 4)]
    if k == "nP":
        return [("nPT", *a, kt) for kt in range(1 if a[2] == "c" else a[0] + 1)]
    if k == "up":
        return [("upg", a[0]), ("upv", a[0])]
    return []


JOBS = [j for s in STEPS for j in jobs_of(s)]
JOBNO = {j: i for i, j in enumerate(JOBS)}


def accs_of(step):
    k, a = step[0], step[1:]
    if k == "aP" and a[1] % 2 == 0:
        return [("aO", a[0], a[1] // 2)]
    if k == "mh":
        return [("num", a[0]), ("den", a[0])]
    if k == "nP" and a[1:] == (0, "c"):
        return [("nO", a[0])]
    return []


ACCS = [j for s in STEPS for j in accs_of(s)]
ACCNO = {j: i for i, j in enumerate(ACCS)}


def blocks_of(step):
    k, a = step[0], step[1:]
    if k == "proj":
        g, i = a
        t = [("ssm_in", 32 + g), ("ssm_in", 36 + g)] + [("ssm_in", 16 + GT * g + m) for m in range(GT)]
        t += [("ssm_in", GT * g + m) for m in range(GT)]
        return [(*t[i], 0)]
    if k == "pp":
        return ([("p", a[0])] if a[1] == 0 else []) + ([("ple_proj", a[0], a[1] // 4)] if a[1] % 4 == 0 else [])
    if k == "out":
        w = {1: "ssm_out", 3: "attn_out", 5: "w_out", 6: "w_down"}[a[0]]
        return [(w, a[1], b) for b in range(2 if a[0] in (1, 6) else 1)]
    if k == "ple":
        return [("ple_gate", a[0], a[1])]
    if k == "kv":
        return [("kv", b) for b in range(4)]
    if k == "q":
        return [("attn_q", a[0], b) for b in range(4)]
    if k == "gate":
        return [("attn_gate", a[0], 0)]
    if k in ("mv", "avg"):
        return [(k, b) for b in range(4)]
    if k in ("mq", "mk", "mo", "aq", "ak", "cmp_in"):
        return [(k, a[0], 0)]
    if k == "cmp":
        return [("cmp_w1", a[0], b) for b in range(4)]
    if k == "up":
        return [("upg", a[0], 0), ("upv", a[0], 0)]
    return []


BLOCKS = [b for s in STEPS for b in blocks_of(s)]
BLKNO = {b: i for i, b in enumerate(BLOCKS)}


class Events:

    def __init__(self, nc, ctx, known):
        self.nc, self.ctx, self.known = nc, ctx, known
        self.sems, self.count, self.seen = {}, {}, {}

    def sem(self, name):
        if name not in self.sems:
            self.sems[name] = self.ctx.enter_context(self.nc.semaphore(name))
            self.count[name] = 0
        return self.sems[name]

    def done(self, name, *events, inc=1):
        s = self.sem(name)
        self.count[name] += inc
        for e in events:
            assert e not in self.seen, e
            self.seen[e] = (name, self.count[name])
        return s, inc

    def at(self, *event):
        if self.known is None:
            return self.sem("first_pass"), 1
        name, value = self.known[event]
        return self.sem(name), value


def build(nc, ins, out, known):
    ctx = ExitStack()
    with ctx:
        ev = Events(nc, ctx, known)
        done, at = ev.done, ev.at

        def sb(name, shape, dt=F32):
            return ctx.enter_context(nc.sbuf_tensor(name, shape, dt))

        h = sb("h", [P, KD, SEQ])
        hn = sb("hn", [P, KD, SEQ])
        ring = sb("ring", [P, NSLOT, BLK])
        con = sb("con", [P, NCON])
        vec = sb("vec", [P, NV])
        rowb = sb("rowb", [P, NR])
        wdt = sb("wdt", [P, KD, HEADS])
        wif = sb("wif", [P, KD, 8])
        w2c = sb("w2c", [P, 2, HD])
        peT = sb("peT", [P, 2, CMP_BLOCK])
        mbias = sb("mbias", [4, 2])
        pos = sb("pos", [P, NT], I32)
        eps = sb("eps", [P, 1])
        halfpi = sb("halfpi", [P, 1])
        sq = sb("sq", [P, 3, SEQ])
        ssacc = sb("ssacc", [P, SEQ])
        rt = sb("rt", [P, SEQ])
        NAR = 62
        arena = sb("arena", [P, NAR * SEQ])
        bank = [ctx.enter_context(nc.psum_tensor(f"bank{i}", [P, SEQ], F32)) for i in range(8)]

        def ar(unit, *dims):
            n = int(np.prod(dims))
            lo = int(unit * SEQ)
            assert lo + n <= NAR * SEQ
            v = arena[:, lo:lo + n]
            if len(dims) == 2:
                v = v.rearrange("p (a b) -> p a b", a=dims[0])
            if len(dims) == 3:
                v = v.rearrange("p (a b c) -> p a b c", a=dims[0], b=dims[1])
            return v

        ident, tri, upper, ones = (con[:, c:c + P] for c in (C_ID, C_T, C_U, C_ONE))
        swa = con[:, C_SWA:C_SWA + 256]
        cmpb = con[:, C_CMP:C_RV].rearrange("p (n h c) -> p n h c", n=NT, h=A_HEADS)
        rowvalid = con[:, C_RV:C_RV + 1]

        def ps(job):
            return bank[JOBNO[job] % NROT]

        def acc(job):
            return bank[NROT + ACCNO[job] % 2]

        def tok(t):
            return slice(t * P, (t + 1) * P)

        def over(ap, n, axis):
            a = ap.unsqueeze(axis)
            return a.broadcast_to([n if i == axis else d for i, d in enumerate(a.shape)])

        xs = [ar(8 * b, GT, SEQ) for b in range(2)]
        zs = [ar(8 * b + 4, GT, SEQ) for b in range(2)]
        bcT = [ar(16 + 2 * b, 2, SEQ) for b in range(2)]
        yn = ar(20, 16, SEQ)
        cva = [ar(36 + b, SEQ) for b in range(2)]
        xdt = [ar(38 + b, HPG, HD) for b in range(2)]
        xde = [ar(40 + b, HPG, HD) for b in range(2)]
        btok = ar(42, NT, P)
        cbm = ar(43, NT, P)
        dat = [ar(44 + 2 * b, HPG, P) for b in range(2)]
        dec = [ar(48 + 2 * b, HPG, P) for b in range(2)]
        ytok = ar(52, NT, SEQ)
        prev = [ar(56 + b, HPG, HD) for b in range(2)]
        yoe = ar(58, HPG, HD)
        ysq = ar(59, SEQ)
        yac = ar(60, SEQ)
        dtb = ar(61, NT, HEADS)
        da = ar(61.25, NT, HEADS)
        dtmp = ar(61.5, NT, HEADS)
        dtmp2 = ar(61.75, NT, HEADS)
        cums = sb("cums", [P, 3, NT * HEADS])
        aneg = sb("aneg", [P, HEADS])

        pp = [ar(0, KD, SEQ), ar(0, KD, SEQ), ar(32, KD, SEQ)]
        gsig = [ar(36 + b, SEQ) for b in range(2)]
        gsig2 = [ar(40 + b, SEQ) for b in range(2)]

        hnB = ar(0, KD, SEQ)
        gs = ar(0, KD, SEQ)
        vtok = ar(8, NT, 256)
        kr = ar(10, NT, 256)
        qr = ar(12, NT, 1024)
        qT = ar(20, KD, SEQ)
        kT = ar(28, 2, SEQ)
        og = ar(12, KD, SEQ)
        Sb = [ar(30 + 2 * b, 4, 256) for b in range(2)]
        PTb = [ar(34 + 2 * b, 2, SEQ) for b in range(2)]
        ctab = ar(38, 4, 256)
        qsq = [ar(40 + b, SEQ) for b in range(2)]
        qn = [ar(42 + b, SEQ) for b in range(2)]
        ra = [ar(44 + b, SEQ) for b in range(2)]
        rb = [ar(46 + b, SEQ) for b in range(2)]
        rtmp = ar(48, 8, P)
        small = sb("small", [P, 8, 16])
        negsink = sb("negsink", [P, ATT_HEADS])

        mqT = ar(0, 4, SEQ)
        mkT = ar(4, 4, SEQ)
        moT = ar(8, 4, SEQ)
        mvt = ar(12, NT, SEQ)
        mixT = ar(16, KD, SEQ)
        aqT = ar(24, 4, SEQ)
        akT = ar(28, 2, SEQ)
        avt = ar(30, NT, 256)
        ckv = ar(32, 2, SEQ)
        cblk = [ar(34 + 2 * b, CMP_BLOCK, NC_BLK) for b in range(2)]
        alibi = ar(38, A_HEADS, SEQ)
        Mneg = ar(46, SEQ)
        wt = [ar(47 + b, SEQ) for b in range(2)]
        wk = [ar(49 + b, SEQ) for b in range(2)]
        hm = ar(51, 4, SEQ)
        mtmp = [ar(55 + b, SEQ) for b in range(2)]
        nSb = [ar(0 + 4 * b, 4, SEQ) for b in range(2)]
        nPb = [ar(8 + b, SEQ) for b in range(4)]
        mrows = ar(57, 5, SEQ)
        gat = sb("gat", [P, NT, 24])
        rcol = sb("rcol", [P, NT, 4])
        chid = ar(32, 2, 64)
        ctm = ar(32.25, 3, 64)
        vct = ar(32.75, 2, HD)[0:NC_BLK]
        scb = [ar(33 + b / 4, 4, NC_BLK) for b in range(2)]
        kcT = ar(33.5, NC_BLK)
        ff = ar(0, FT, SEQ)
        fca = [ar(16 + b, SEQ) for b in range(2)]
        fsl = [ar(18 + b, SEQ) for b in range(2)]

        block = ctx.enter_context(nc.Block())

        @block.sync
        def _(sp):
            for L, b in enumerate(BLOCKS):
                if L >= NSLOT:
                    sp.wait_ge(*at("slot_free", L - NSLOT))
                sp.dma_start(ring[:, L % NSLOT, :], ins["wstream"][L]).then_inc(*done(f"loaded{L % NSLOT}", ("loaded", L), inc=16))
            for m in range(KD):
                sp.wait_ge(*at("hn", "final", m))
                sp.dma_start(out[m], hn[:, m, :]).then_inc(*done("stored", ("stored", m), inc=16))
            sp.wait_ge(*at("stored", KD - 1))

        @block.gpsimd
        def _(pool):
            nc.gpsimd.memset(eps[:, :], EPS)
            nc.gpsimd.memset(halfpi[:, :], float(np.pi / 2)).then_inc(*done("eps_set", ("eps",)))
            pool.wait_ge(*at("consts"))
            for step in STEPS:
                k, a = step[0], step[1:]
                if k == "dt":
                    pool.wait_ge(*at("da"))
                if k == "ssd1":
                    g, c = a
                    n = g * NT + c
                    if n >= 2:
                        pool.wait_ge(*at("mm", "seg", (n - 2) // NT, (n - 2) % NT, 1))
                    nc.gpsimd.tensor_tensor(dat[c % 2], over(tri, HPG, 1),
                                            over(da[:, c, g * HPG:(g + 1) * HPG], P, 2), ALU.mult)\
                        .then_inc(*done("dat", ("dat", g, c)))
                    pool.wait_ge(*at("xdt", g, c))
                    pool.wait_ge(*at("cums"))
                    if c < NT - 1:
                        nc.gpsimd.tensor_tensor(xde[c % 2], xdt[c % 2],
                                                over(cums[:, 1, c * HEADS + g * HPG:c * HEADS + (g + 1) * HPG], HD, 2),
                                                ALU.mult).then_inc(*done("xde", ("xde", g, c)))
                if k == "ssd2":
                    g, c = a
                    if 1 <= c < NT - 1:
                        pool.wait_ge(*at("prev", g, c))
                        nc.gpsimd.tensor_tensor(prev[(c + 1) % 2], prev[c % 2],
                                                over(cums[:, 2, c * HEADS + g * HPG:c * HEADS + (g + 1) * HPG], HD, 2),
                                                ALU.mult).then_inc(*done("pdec", ("pdec", g, c)))
                if k == "yt":
                    g, m = a
                    pool.wait_ge(*at("yskip", g, m))
                    pool.wait_ge(*at("zs", g, m))
                    nc.gpsimd.tensor_tensor(yn[:, GT * g + m, :], yn[:, GT * g + m, :], zs[g % 2][:, m, :], ALU.mult)\
                        .then_inc(*done("ygated", ("ygated", g, m)))
                if k == "out" and a == (1, 0):
                    pass
                if k == "rope_rest" or k == "kv" or k == "q":
                    for t in range(NT):
                        key = ("kv", t) if k == "kv" else ("q", a[0], t)
                        b = t % 2
                        nh = 4 if k == "kv" else 8
                        cs = ctab[:, 0 if k == "q" else 2, :].rearrange("p (t d) -> p t d", t=NT)[:, t, :]
                        pool.wait_ge(*at("qn", *key))
                        nc.gpsimd.tensor_tensor(ra[b][:, 0:nh * HD].rearrange("p (h d) -> p h d", h=nh),
                                                qn[b][:, 0:nh * HD].rearrange("p (h d) -> p h d", h=nh),
                                                over(cs, nh, 1), ALU.mult).then_inc(*done("ropea", ("ropea", *key)))
                        pool.wait_ge(*at("ropea", *key))
                        pool.wait_ge(*at("ropeb", *key))
                        if k == "kv":
                            dst = kr[:, t, :].rearrange("p (o h d) -> p o h d", o=1, h=4)
                            v = [x[b][:, 0:256].rearrange("p (o h d) -> p o h d", o=1, h=4) for x in (ra, rb)]
                        else:
                            dst = qr[:, t, a[0] * SEQ:(a[0] + 1) * SEQ].rearrange("p (j o d) -> p o j d", o=2, j=4)
                            v = [x[b][:, :].rearrange("p (o j d) -> p o j d", o=2, j=4) for x in (ra, rb)]
                        nc.gpsimd.tensor_tensor(dst, v[0], v[1], ALU.add).then_inc(*done("roped", ("roped", *key)))
                if k == "aS":
                    n, g = a
                    u = n * KV_HEADS + g
                    w = P if n == 0 else 256
                    pool.wait_ge(*at("arec", n, g))
                    s = Sb[u % 2][:, :, 0:w]
                    nc.gpsimd.tensor_tensor(s, s, over(small[:, 4 * (u % 2) + 3, 0:4], w, 2), ALU.mult)\
                        .then_inc(*done("aprob", ("aprob", n, g)))
                if k == "mh":
                    for s in range(NT):
                        pool.wait_ge(*at("wt", a[0], s))
                        b = (a[0] * NT + s) % 2
                        nc.gpsimd.tensor_tensor(wk[b][:, 0:P], wk[b][:, 0:P], tri, ALU.mult)\
                            .then_inc(*done("wtm", ("wtm", a[0], s)))
                if k == "mnorm":
                    h_ = a[0]
                    pool.wait_ge(*at("mnormed", h_))
                    nc.gpsimd.tensor_tensor(mixT[:, h_, :], hm[:, h_, :], moT[:, h_, :], ALU.mult)\
                        .then_inc(*done("mixm", ("mix", h_)))
                if k == "nS" and a[2] != "c":
                    u = NSEQ[a]
                    w = P * (a[0] + 1)
                    pool.wait_ge(*at("nrec", *a))
                    s = nSb[u % 2][:, :, 0:w]
                    nc.gpsimd.tensor_tensor(s, s, over(small[:, 4 * (u % 2) + 3, 0:4], w, 2), ALU.mult)\
                        .then_inc(*done("nprob", ("nprob", *a)))

        @block.scalar
        def _(act):
            for i, (dst, name) in enumerate([(con[:, :], "con"), (vec[:, :], "vec"), (rowb[:, :], "rowb"),
                                             (wdt[:, :, :], "wdt"), (wif[:, :, :], "wif"), (w2c[:, :, :], "w2c"),
                                             (peT[:, :, :], "peT"), (mbias[:, :], "mbias"), (pos[:, :], "pos")]):
                act.dma_start(dst, ins[name]).then_inc(*done("consts", *([("consts",)] if i == 8 else []), inc=16))
            for m in range(KD):
                act.dma_start(h[:, m, :], ins["xT"][m]).then_inc(*done(f"xin{m}", ("h", 0, m), inc=16))
            act.wait_ge(*at("eps"))
            act.wait_ge(*at("consts"))
            chain = [0]

            def link(ins_):
                chain[0] += 1
                ins_.then_inc(*done("act_step", ("act_step", chain[0])))
                act.wait_ge(*at("act_step", chain[0]))

            def square(ver, m):
                n = KD * ver + m
                if n >= 3:
                    v, q = divmod(n - 3, KD)
                    act.wait_ge(*at("ssadd", v, max(q, 1)))
                act.wait_ge(*at("h", ver, m))
                nc.scalar.activation(sq[:, n % 3, :], h[:, m, :], ACT.Square).then_inc(*done("sq", ("sq", ver, m)))

            for step in STEPS:
                k, a = step[0], step[1:]
                if k == "load":
                    for m in range(KD):
                        square(0, m)
                if k == "norm":
                    act.wait_ge(*at("mm", "ss", a[0]))
                    nc.scalar.activation(rt[:, :], ps(("ss", a[0]))[:, :], ACT.Sqrt, bias=eps[:, 0:1], scale=1.0 / D)\
                        .then_inc(*done("rms", ("rms", a[0]), ("free", "ss", a[0])))
                if k == "proj":
                    g, i = a
                    b = ps(step)
                    act.wait_ge(*at("mm", *step))
                    if i < 6:
                        ch = [16 + g, 20 + g][i] if i < 2 else GT * g + i - 2
                        n = g * 6 + i
                        if n >= 2:
                            act.wait_ge(*at("conv_used", n - 2))
                        nc.scalar.activation(cva[n % 2], b[:, :], ACT.Identity, bias=vec[:, V_CB + ch:V_CB + ch + 1],
                                             scale=vec[:, V_CW + 3 * 24 + ch:V_CW + 3 * 24 + ch + 1])\
                            .then_inc(*done("conv0", ("conv0", g, i)))
                        act.wait_ge(*at("conv", g, i))
                        if g >= 2:
                            if i < 2:
                                act.wait_ge(*at("mm", "yd", g - 2, 3))
                            else:
                                act.wait_ge(*at("yskip", g - 2, i - 2))
                        dst = bcT[g % 2][:, i, :] if i < 2 else xs[g % 2][:, i - 2, :]
                        nc.scalar.activation(dst, cva[n % 2], ACT.Silu)\
                            .then_inc(*done("silu", ("xbc", g, i), ("conv_used", n)))
                    else:
                        if g >= 2:
                            act.wait_ge(*at("ygated", g - 2, i - 6))
                        nc.scalar.activation(zs[g % 2][:, i - 6, :], b[:, :], ACT.Silu)\
                            .then_inc(*done("zs", ("zs", g, i - 6), ("free", *step)))
                if k == "dt":
                    nc.scalar.activation(aneg[:, :], rowb[:, R_ALOG:R_ALOG + HEADS], ACT.Exp).then_inc(*done("aexp", ("aexp",)))
                    act.wait_ge(*at("dtabs"))
                    link(nc.scalar.activation(dtmp2, dtmp2, ACT.Exp))
                    nc.scalar.activation(dtmp2, dtmp2, ACT.Ln, bias=1.0).then_inc(*done("dtln", ("dtln",)))
                    act.wait_ge(*at("mm", "cum"))
                    nc.scalar.activation(cums[:, :, :], ps(("cum",))[:, 0:3 * P].rearrange("p (a b) -> p a b", a=3), ACT.Exp)\
                        .then_inc(*done("cums", ("cums",), ("free", "cum")))
                if k == "norm" and a[0] == 4:
                    act.wait_ge(*at("h", 4, KD - 1))
                    act.dma_start(alibi, ins["alibi"]).then_inc(*done("alibi_in", ("alibi",), inc=16))
                if k == "ssd0":
                    act.wait_ge(*at("mm", "bt", *a))
                    if a[0] >= 1:
                        act.wait_ge(*at("mm", "st", a[0] - 1, 2))
                    nc.scalar.activation(btok, ps(("bt", *a))[:, :].rearrange("p (a b) -> p a b", a=NT), ACT.Copy)\
                        .then_inc(*done("btok", ("btok", *a), ("free", "bt", *a)))
                if k == "ssd1":
                    g, c = a
                    n = g * NT + c
                    for j in range(2):
                        act.wait_ge(*at("mm", "seg", g, c, j))
                        if n >= 2:
                            act.wait_ge(*at("mm", "yd", (n - 2) // NT, (n - 2) % NT))
                        nc.scalar.activation(dec[c % 2][:, 4 * j:4 * j + 4, :],
                                             ps(("seg", g, c, j))[:, :].rearrange("p (a b) -> p a b", a=4), ACT.Exp)\
                            .then_inc(*done("dec", ("dec", g, c, j), ("free", "seg", g, c, j)))
                if k == "ssd2" and a[1] == 0:
                    g, c = a
                    act.wait_ge(*at("mm", "yd", g, 0))
                    if g >= 1:
                        act.wait_ge(*at("mm", "yt", g - 1, 3))
                    nc.scalar.activation(ytok[:, 0, :], ps(("yd", g, 0))[:, :], ACT.Copy)\
                        .then_inc(*done("ytok0", ("ytok", g, 0), ("free", "yd", g, 0)))
                    act.wait_ge(*at("mm", "st", g, 0))
                    if g >= 1:
                        act.wait_ge(*at("mm", "yo", g - 1, 3))
                    nc.scalar.activation(prev[1], ps(("st", g, 0))[:, :].rearrange("p (a b) -> p a b", a=HPG), ACT.Copy)\
                        .then_inc(*done("prev1", ("prev", g, 1), ("free", "st", g, 0)))
                if k == "yt":
                    g, m = a
                    act.wait_ge(*at("ygated", g, m))
                    if (g, m) != (0, 0):
                        act.wait_ge(*at("yadd", *((g, m - 1) if m else (g - 1, 3))))
                    nc.scalar.activation(ysq if m else yac, yn[:, GT * g + m, :], ACT.Square)\
                        .then_inc(*done("ysq", ("ysq", g, m)))
                if k == "gn":
                    g = a[0]
                    act.wait_ge(*at("mm", "gn", g))
                    nc.scalar.activation(ysq, ps(step)[:, :], ACT.Sqrt, bias=eps[:, 0:1], scale=1.0 / 512)\
                        .then_inc(*done("grms", ("grms", g), ("free", *step)))
                if k == "pp":
                    i, m = a
                    act.wait_ge(*at("mm", *step))
                    if i == 0 and m == 0:
                        act.wait_ge(*at("ygated", 2, 3))
                    nc.scalar.activation(pp[i][:, m, :], ps(step)[:, :], ACT.Copy)\
                        .then_inc(*done("pp", ("pp", i, m), ("free", *step)))
                if k == "out":
                    square(*a)
                if k == "ple":
                    i, m = a
                    act.wait_ge(*at("mm", *step))
                    if m >= 2:
                        act.wait_ge(*at("h", 2 * i + 2 if i < 2 else 7, m - 2))
                    gb = gsig2 if i == 2 else gsig
                    nc.scalar.activation(gb[m % 2], ps(step)[:, :], ACT.Sigmoid)\
                        .then_inc(*done("gsig", ("gsig", i, m), ("free", *step)))
                    if m:
                        square(2 * i + 2 if i < 2 else 7, m - 1)
                    if m == KD - 1:
                        square(2 * i + 2 if i < 2 else 7, m)
                if k == "rope_tables":
                    act.wait_ge(*at("angles"))
                    nc.scalar.activation(rtmp[:, 4, :], rtmp[:, 2, :], ACT.Sin).then_inc(*done("sincos", ("sin",)))
                    nc.scalar.activation(rtmp[:, 5, :], rtmp[:, 3, :], ACT.Sin, scale=-1.0, bias=halfpi[:, 0:1])\
                        .then_inc(*done("sincos", ("cos",)))
                if k in ("kv", "q"):
                    w = 256 if k == "kv" else 512
                    for t in range(NT):
                        key = ("kv", t) if k == "kv" else ("q", a[0], t)
                        act.wait_ge(*at("mm", *key))
                        n = {"kv": 0, "q": 1 + (a[0] if a else 0)}[k] * NT + t
                        if n >= 2:
                            act.wait_ge(*at("qss", n - 2))
                        if k == "kv":
                            nc.scalar.activation(vtok[:, t, :], ps(key)[:, 256:512], ACT.Copy)
                        nc.scalar.activation(qsq[t % 2][:, 0:w], ps(key)[:, 0:w], ACT.Square)\
                            .then_inc(*done("qsq", ("qsq", *key)))
                        act.wait_ge(*at("qss", n))
                        nh = w // HD
                        nc.scalar.activation(small[:, 4 * (t % 2) + 1, 0:nh], small[:, 4 * (t % 2), 0:nh], ACT.Sqrt,
                                             bias=eps[:, 0:1], scale=1.0 / HD).then_inc(*done("qrms", ("qrms", *key)))
                if k == "kT":
                    for t in range(NT):
                        act.wait_ge(*at("mm", "kT", t))
                        nc.scalar.activation(kT[:, :, tok(t)], ps(("kT", t))[:, 0:256].rearrange("p (a b) -> p a b", a=2),
                                             ACT.Copy).then_inc(*done("kT", ("kT", t), ("free", "kT", t)))
                if k == "qT":
                    for t in range(NT):
                        key = ("qT", a[0], t)
                        act.wait_ge(*at("mm", *key))
                        nc.scalar.activation(qT[:, 4 * a[0]:4 * a[0] + 4, tok(t)],
                                             ps(key)[:, :].rearrange("p (a b) -> p a b", a=4), ACT.Copy,
                                             scale=HD ** -0.5).then_inc(*done("qT", key, ("free", *key)))
                if k == "gate":
                    act.wait_ge(*at("mm", *step))
                    act.wait_ge(*at("mm", "kv", NT - 1))
                    nc.scalar.activation(gs[:, a[0], :], ps(step)[:, :], ACT.Silu)\
                        .then_inc(*done("gs", ("gs", a[0]), ("free", *step)))
                if k == "aS":
                    n, g = a
                    u = n * KV_HEADS + g
                    w = P if n == 0 else 256
                    act.wait_ge(*at("anegm", n, g))
                    sm = small[:, 4 * (u % 2):4 * (u % 2) + 4, :]
                    for r in range(4):
                        last = nc.scalar.activation(Sb[u % 2][:, r, 0:w], Sb[u % 2][:, r, 0:w], ACT.Exp,
                                                    bias=sm[:, 1, r:r + 1], accum_out=sm[:, 2, r:r + 1])
                    last.then_inc(*done("aexpd", ("aexpd", n, g)))
                    nc.scalar.activation(sm[:, 1, 8:12], sm[:, 1, 4:8], ACT.Exp).then_inc(*done("aexpd", ("aesink", n, g)))
                if k == "aP":
                    n, g = a
                    u = n * KV_HEADS + g
                    act.wait_ge(*at("mm", "aPT", n, g, 0))
                    if u >= 2:
                        act.wait_ge(*at("pv", *divmod(u - 2, KV_HEADS)))
                    nc.scalar.activation(PTb[u % 2][:, 0, :], ps(("aPT", n, g, 0))[:, :], ACT.Copy)\
                        .then_inc(*done("aPT_act", ("aPT", n, g, 0), ("free", "aPT", n, g, 0)))
                if k == "mrow":
                    act.wait_ge(*at("mfabs"))
                    link(nc.scalar.activation(mrows[0:4, 2, :], mrows[0:4, 2, :], ACT.Exp))
                    nc.scalar.activation(mrows[0:4, 2, :], mrows[0:4, 2, :], ACT.Ln, bias=1.0)\
                        .then_inc(*done("mfln", ("mfln",)))
                    act.wait_ge(*at("mmt"))
                    nc.scalar.activation(mrows[0:4, 4, :], mrows[0:4, 2, :], ACT.Exp, scale=-1.0)\
                        .then_inc(*done("mexp", ("men",)))
                if k == "mrcol":
                    act.wait_ge(*at("mm", "mrcol"))
                    nc.scalar.activation(rcol[:, :, :], ps(("mrcol",))[:, 0:16].rearrange("p (a b) -> p a b", a=4), ACT.Copy)\
                        .then_inc(*done("rcol", ("rcol",), ("free", "mrcol")))
                if k in ("mv", "avg"):
                    for t in range(NT):
                        act.wait_ge(*at("mm", k, t))
                        if k == "mv":
                            nc.scalar.activation(mvt[:, t, :], ps((k, t))[:, :], ACT.Copy)\
                                .then_inc(*done("mv", ("mv", t), ("free", k, t)))
                        else:
                            nc.scalar.activation(avt[:, t, :], ps((k, t))[:, 0:256], ACT.Copy)
                            nc.scalar.activation(gat[:, t, :], ps((k, t))[:, 256:280], ACT.Sigmoid)\
                                .then_inc(*done("avg", ("avg", t), ("free", k, t)))
                if k in ("mq", "mk", "aq", "ak", "cmp_in", "mo"):
                    act.wait_ge(*at("mm", *step))
                    dst = {"mq": mqT, "mk": mkT, "aq": aqT, "ak": akT, "cmp_in": ckv, "mo": moT}[k][:, a[0], :]
                    f, s = (ACT.Sigmoid, 1.0) if k == "mo" else (ACT.Copy, {"mq": P ** -0.5, "aq": HD ** -0.5}.get(k, 1.0))
                    nc.scalar.activation(dst, ps(step)[:, :], f, scale=s).then_inc(*done(k, ("done", *step), ("free", *step)))
                if k == "cmp":
                    act.wait_ge(*at("gelu_in", a[0]))
                    nc.scalar.activation(ctm[:, 1, :], ctm[:, 1, :], ACT.Tanh, scale=float(np.sqrt(2 / np.pi)))\
                        .then_inc(*done("ctanh", ("ctanh", a[0])))
                if k == "cmp2":
                    act.wait_ge(*at("mm", "ckT"))
                    nc.scalar.activation(kcT[:, :], ps(("ckT",))[:, 0:NC_BLK], ACT.Copy).then_inc(*done("kcT", ("kcT",), ("free", "ckT")))
                    act.wait_ge(*at("mm", "cv"))
                    nc.scalar.activation(vct[:, :, :], ps(("cv",))[0:NC_BLK, 0:128].rearrange("p (a b) -> p a b", a=2), ACT.Copy)\
                        .then_inc(*done("vct", ("vct",), ("free", "cv")))
                if k == "mh":
                    h_ = a[0]
                    act.wait_ge(*at("mm", "Mb", h_))
                    if h_:
                        act.wait_ge(*at("marg", h_ - 1, NT - 1))
                    nc.scalar.activation(Mneg, ps(("Mb", h_))[:, :], ACT.Copy, scale=-1.0)\
                        .then_inc(*done("Mneg", ("Mneg", h_), ("free", "Mb", h_)))
                    for s in range(NT):
                        w = SEQ - P * s
                        b = (h_ * NT + s) % 2
                        act.wait_ge(*at("marg", h_, s))
                        nc.scalar.activation(wt[b][:, 0:w], wt[b][:, 0:w], ACT.Exp).then_inc(*done("mexpd", ("mexpd", h_, s)))
                    act.wait_ge(*at("mden", h_))
                    if h_:
                        act.wait_ge(*at("hm", h_ - 1))
                    nc.scalar.activation(mtmp[0], acc(("den", h_))[:, :], ACT.Abs)\
                        .then_inc(*done("mabs", ("mabs", h_), ("accfree", "den", h_)))
                    act.wait_ge(*at("hm", h_))
                    if h_ == M_HEADS - 1:
                        pass
                if k == "mnorm":
                    h_ = a[0]
                    if h_ == 0:
                        for j in range(M_HEADS):
                            nc.scalar.activation(mqT[:, j, :], hm[:, j, :], ACT.Square).then_inc(*done("msq", ("msq", j)))
                    act.wait_ge(*at("mm", "mss", h_))
                    if h_:
                        act.wait_ge(*at("mrstd", h_ - 1))
                    nc.scalar.activation(mtmp[0], ps(("mss", h_))[:, :], ACT.Sqrt, bias=eps[:, 0:1], scale=1.0 / P)\
                        .then_inc(*done("mrms", ("mrms", h_), ("free", "mss", h_)))
                if k == "nS":
                    i, g, br = a
                    u = NSEQ[a]
                    act.wait_ge(*at("nnegm", *a))
                    sm = small[:, 4 * (u % 2):4 * (u % 2) + 4, :]
                    if br == "c":
                        nc.scalar.activation(scb[g][:, :, :], scb[g][:, :, :], ACT.Exp).then_inc(*done("nexp", ("nexp", *a)))
                    else:
                        w = P * (i + 1)
                        for r in range(4):
                            last = nc.scalar.activation(nSb[u % 2][:, r, 0:w], nSb[u % 2][:, r, 0:w], ACT.Exp,
                                                        bias=sm[:, 1, r:r + 1], accum_out=sm[:, 2, r:r + 1])
                        last.then_inc(*done("nexp", ("nexp", *a)))
                if k == "nP":
                    if a == (0, 0, "c"):
                        act.wait_ge(*at("mix", M_HEADS - 1))
                    for kt in range(1 if a[2] == "c" else a[0] + 1):
                        n = NPT[(*a, kt)]
                        if n % 2 == 0:
                            act.wait_ge(*at("mm", "nPT", *a, kt))
                            if n >= 4:
                                act.wait_ge(*at("npv", n - 4))
                            rows = NC_BLK if a[2] == "c" else P
                            nc.scalar.activation(nPb[n % 4][0:rows, :], ps(("nPT", *a, kt))[0:rows, :], ACT.Copy)\
                                .then_inc(*done("nPT_act", ("nPT", *a, kt), ("free", "nPT", *a, kt)))
                if k == "up":
                    m = a[0]
                    act.wait_ge(*at("mm", "upg", m))
                    if m >= 2:
                        act.wait_ge(*at("fsilu", m - 2))
                    nc.scalar.activation(fca[m % 2], ps(("upg", m))[:, :], ACT.Identity, bias=vec[:, V_C2B + m:V_C2B + m + 1],
                                         scale=vec[:, V_C2W + 2 * FT + m:V_C2W + 2 * FT + m + 1])\
                        .then_inc(*done("fconv0", ("fconv0", m)))
                    act.wait_ge(*at("fconv", m))
                    if m >= 2:
                        act.wait_ge(*at("ff", m - 2))
                    nc.scalar.activation(fsl[m % 2], fca[m % 2], ACT.Silu).then_inc(*done("fsilu", ("fsilu", m)))

        @block.tensor
        def _(pe):
            pe.wait_ge(*at("consts"))

            def open_bank(job):
                n = JOBNO[job]
                if n >= NROT:
                    pe.wait_ge(*at("free", *JOBS[n - NROT]))
                return ps(job)

            def open_acc(job):
                n = ACCNO[job]
                if n >= 2:
                    pe.wait_ge(*at("accfree", *ACCS[n - 2]))
                return acc(job)

            def weights(name):
                L = BLKNO[name]
                pe.wait_ge(*at("loaded", L))
                return ring[:, L % NSLOT, :]

            def mm(*args, **kw):
                return nc.tensor.matmul(*args, **kw)

            def linear(job, names, src):
                b = open_bank(job)
                n = len(names)
                for j, name in enumerate(names):
                    w = weights(name)
                    for kt in range(KD):
                        last = mm(b[:, :], w[:, kt * P:(kt + 1) * P], src[:, KD * j + kt, :],
                                  start=(j + kt == 0), stop=(j == n - 1 and kt == KD - 1))
                    e = [("slot_free", BLKNO[name])] + ([("mm", *job)] if j == n - 1 else [])
                    last.then_inc(*done("mm", *e))

            def token_major(jobs, names, src, width=SEQ):
                bs = [open_bank(j) for j in jobs]
                for i, name in enumerate(names):
                    w = weights(name)
                    for k2 in range(2):
                        for t in range(NT):
                            fin = i == 3 and k2 == 1
                            last = mm(bs[t][:, 0:width], src[:, 2 * i + k2, tok(t)], w[:, k2 * SEQ:k2 * SEQ + width],
                                      start=(i + k2 == 0), stop=fin)
                            e = ([("mm", *jobs[t])] if fin else []) + \
                                ([("slot_free", BLKNO[name])] if k2 == 1 and t == NT - 1 else [])
                            if e:
                                last.then_inc(*done("mm", *e))

            def await_hn(name):
                for m in range(KD):
                    pe.wait_ge(*at("hn", name, m))

            for step in STEPS:
                k, a = step[0], step[1:]
                if k == "norm":
                    b = open_bank(("ss", a[0]))
                    pe.wait_ge(*at("ssadd", a[0], KD - 1))
                    mm(b[:, :], ones, ssacc[:, :], start=True, stop=True).then_inc(*done("mm", ("mm", "ss", a[0])))
                if k == "proj":
                    if a == (0, 0):
                        await_hn("ssm")
                    linear(step, blocks_of(step), hn)
                if k == "dt":
                    b = open_bank(("dt",))
                    for t in range(NT):
                        for kt in range(KD):
                            last = mm(b[:, t * HEADS:(t + 1) * HEADS], hn[:, kt, tok(t)], wdt[:, kt, :],
                                      start=(kt == 0), stop=(kt == KD - 1))
                    last.then_inc(*done("mm", ("mm", "dt")))
                    b = open_bank(("cum",))
                    pe.wait_ge(*at("da"))
                    daf = da.rearrange("p a b -> p (a b)")
                    mm(b[:, 0:P], tri, daf, start=True, stop=True)
                    mm(b[:, P:2 * P], upper, daf, start=True, stop=True)
                    mm(b[:, 2 * P:3 * P], ones, daf, start=True, stop=True).then_inc(*done("mm", ("mm", "cum")))
                if k == "ssd0":
                    g = a[0]
                    b = open_bank(("cb", g))
                    pe.wait_ge(*at("xbc", g, 1))
                    bc = bcT[g % 2]
                    for c in range(NT):
                        last = mm(b[:, tok(c)], bc[:, 0, tok(c)], bc[:, 1, tok(c)], start=True, stop=True)
                    last.then_inc(*done("mm", ("mm", "cb", g)))
                    b = open_bank(("bt", g))
                    for c in range(NT):
                        last = nc.tensor.transpose(b[:, tok(c)], bc[:, 0, tok(c)], ident)
                    last.then_inc(*done("mm", ("mm", "bt", g)))
                if k == "ssd1":
                    g, c = a
                    b = open_bank(("xt", g, c))
                    pe.wait_ge(*at("xbc", g, 5))
                    for m in range(GT):
                        last = nc.tensor.transpose(b[:, tok(m)], xs[g % 2][:, m, tok(c)], ident)
                    last.then_inc(*done("mm", ("mm", "xt", g, c)))
                    pe.wait_ge(*at("dat", g, c))
                    for j in range(2):
                        b = open_bank(("seg", g, c, j))
                        mm(b[:, :], upper, dat[c % 2][:, 4 * j:4 * j + 4, :], start=True, stop=True)\
                            .then_inc(*done("mm", ("mm", "seg", g, c, j)))
                if k == "ssd2":
                    g, c = a
                    b = open_bank(("yd", g, c))
                    pe.wait_ge(*at("decm", g, c))
                    for r in range(HPG):
                        last = mm(b[:, r * HD:(r + 1) * HD], dec[c % 2][:, r, :], xdt[c % 2][:, r, :], start=True, stop=True)
                    last.then_inc(*done("mm", ("mm", "yd", g, c)))
                    if c:
                        b = open_bank(("yo", g, c))
                        pe.wait_ge(*at("prev", g, c))
                        mm(b[:, :], bcT[g % 2][:, 1, tok(c)], prev[c % 2], start=True, stop=True)\
                            .then_inc(*done("mm", ("mm", "yo", g, c)))
                    if c < NT - 1:
                        b = open_bank(("st", g, c))
                        pe.wait_ge(*at("btok", g))
                        pe.wait_ge(*at("xde", g, c))
                        mm(b[:, :], btok[:, c, :], xde[c % 2], start=True, stop=True)\
                            .then_inc(*done("mm", ("mm", "st", g, c)))
                if k == "yt":
                    g, m = a
                    b = open_bank(step)
                    for c in range(NT):
                        pe.wait_ge(*at("ytok", g, c))
                        last = nc.tensor.transpose(b[:, tok(c)], ytok[:, c, tok(m)], ident)
                    last.then_inc(*done("mm", ("mm", *step)))
                if k == "gn":
                    b = open_bank(step)
                    pe.wait_ge(*at("yadd", a[0], 3))
                    mm(b[:, :], ones, yac, start=True, stop=True).then_inc(*done("mm", ("mm", *step)))
                if k == "pp":
                    i, m = a
                    b = open_bank(step)
                    pw = weights(("p", i))
                    w = weights(("ple_proj", i, m // 4))
                    for kt in range(2):
                        last = mm(b[:, :], w[:, kt * SEQ + (m % 4) * P:kt * SEQ + (m % 4 + 1) * P],
                                  pw[:, kt * SEQ:(kt + 1) * SEQ], start=(kt == 0), stop=(kt == 1))
                    e = [("mm", *step)]
                    if m % 4 == 3:
                        e.append(("slot_free", BLKNO[("ple_proj", i, m // 4)]))
                    if m == KD - 1:
                        e.append(("slot_free", BLKNO[("p", i)]))
                    last.then_inc(*done("mm", *e))
                if k == "out":
                    if a == (1, 0):
                        for g in range(GROUPS):
                            pe.wait_ge(*at("yn", g, 3))
                    if a == (3, 0):
                        pe.wait_ge(*at("og", NT - 1, 1))
                    if a == (5, 0):
                        pe.wait_ge(*at("mix", 3))
                        pe.wait_ge(*at("nog", NT - 1))
                    if a == (6, 0):
                        pe.wait_ge(*at("ff", FT - 1))
                    linear(step, blocks_of(step), {1: yn, 3: og, 5: mixT, 6: ff}[a[0]])
                if k == "ple":
                    if a[1] == 0:
                        await_hn(["ple0", "ple1", "ple2"][a[0]])
                    linear(step, blocks_of(step), hn)
                if k == "kv":
                    await_hn("kv")
                    token_major([("kv", t) for t in range(NT)], blocks_of(step), hnB)
                if k == "q":
                    if a[0] == 0:
                        await_hn("attn")
                    token_major([("q", a[0], t) for t in range(NT)], blocks_of(step), hn)
                if k == "kT":
                    for t in range(NT):
                        b = open_bank(("kT", t))
                        pe.wait_ge(*at("roped", "kv", t))
                        for j in range(2):
                            last = nc.tensor.transpose(b[:, tok(j)], kr[:, t, tok(j)], ident)
                        last.then_inc(*done("mm", ("mm", "kT", t)))
                if k == "qT":
                    for t in range(NT):
                        b = open_bank(("qT", a[0], t))
                        pe.wait_ge(*at("roped", "q", a[0], t))
                        for j in range(4):
                            last = nc.tensor.transpose(b[:, tok(j)], qr[:, t, a[0] * SEQ + j * P:a[0] * SEQ + (j + 1) * P], ident)
                        last.then_inc(*done("mm", ("mm", "qT", a[0], t)))
                if k == "gate":
                    linear(step, blocks_of(step), hn)
                if k == "aS":
                    n, g = a
                    lo = HD * (g % 2)
                    if g == 0:
                        pe.wait_ge(*at("kT", n))
                        pe.wait_ge(*at("qT", 1, n))
                    w = P if n == 0 else 256
                    keys = slice(0, P) if n == 0 else slice((n - 1) * P, (n + 1) * P)
                    per = SEQ // w
                    for j in range(4 // per):
                        b = open_bank(("aS", n, g, j))
                        for r in range(per * j, per * (j + 1)):
                            last = mm(b[:, (r % per) * w:(r % per + 1) * w], qT[lo:lo + HD, 4 * (g // 2) + r, tok(n)],
                                      kT[lo:lo + HD, g // 2, keys], start=True, stop=True)
                        last.then_inc(*done("mm", ("mm", "aS", n, g, j)))
                if k == "aP":
                    n, g = a
                    u = n * KV_HEADS + g
                    lo = HD * (g % 2)
                    nk = 1 if n == 0 else 2
                    pe.wait_ge(*at("aprob", n, g))
                    for kt in range(nk):
                        b = open_bank(("aPT", n, g, kt))
                        for r in range(4):
                            last = nc.tensor.transpose(b[:, tok(r)], Sb[u % 2][:, r, tok(kt)], ident)
                        last.then_inc(*done("mm", ("mm", "aPT", n, g, kt)))
                    o = open_acc(("aO", n, g // 2)) if g % 2 == 0 else acc(("aO", n, g // 2))
                    for kt in range(nk):
                        pe.wait_ge(*at("aPT", n, g, kt))
                        last = mm(o[lo:lo + HD, :], vtok[:, n - nk + 1 + kt, g * HD:(g + 1) * HD], PTb[u % 2][:, kt, :],
                                  start=(kt == 0), stop=(kt == nk - 1))
                    last.then_inc(*done("mm", ("pv", n, g)))
                if k == "mif":
                    await_hn("ln1")
                    for j, name in enumerate(("mi", "mf")):
                        b = open_bank((name,))
                        for kt in range(KD):
                            last = mm(b[0:4, :], wif[:, kt, 4 * j:4 * j + 4], hn[:, kt, :], start=(kt == 0), stop=(kt == KD - 1))
                        last.then_inc(*done("mm", ("mm", name)))
                if k in ("mq", "mk", "mo", "aq", "ak", "cmp_in"):
                    linear(step, blocks_of(step), hn)
                if k in ("mv", "avg"):
                    token_major([(k, t) for t in range(NT)], blocks_of(step), hn, SEQ if k == "mv" else 280)
                if k == "mrcol":
                    b = open_bank(("mrcol",))
                    pe.wait_ge(*at("mrrow"))
                    for t in range(NT):
                        last = nc.tensor.transpose(b[:, 4 * t:4 * t + 4], mrows[0:4, 0, tok(t)], ident[0:4, 0:4])
                    last.then_inc(*done("mm", ("mm", "mrcol")))
                if k == "cmp":
                    j = a[0]
                    b = [open_bank(("chid", j, g)) for g in range(2)]
                    pe.wait_ge(*at("cblk", j))
                    for q in range(4):
                        w = weights(("cmp_w1", j, q))
                        for g in range(2):
                            for l in range(8):
                                last = mm(b[g][:, 0:NC_BLK], w[HD * g:HD * (g + 1), l * P:(l + 1) * P],
                                          cblk[j][HD * g:HD * (g + 1), 8 * q + l, :],
                                          start=(q == 0 and l == 0), stop=(q == 3 and l == 7))
                            e = [("slot_free", BLKNO[("cmp_w1", j, q)])] if g else []
                            if q == 3:
                                e.append(("mm", "chid", j, g))
                            if e:
                                last.then_inc(*done("mm", *e))
                if k == "cmp2":
                    b = open_bank(("ckT",))
                    pe.wait_ge(*at("gelu", 1))
                    for g in range(2):
                        last = mm(b[HD * g:HD * (g + 1), 0:NC_BLK], w2c[:, 0, :], chid[:, 0, 32 * g:32 * g + NC_BLK],
                                  start=True, stop=True)
                    last.then_inc(*done("mm", ("mm", "ckT")))
                    b = open_bank(("cv",))
                    for g in range(2):
                        last = mm(b[0:NC_BLK, HD * g:HD * (g + 1)], chid[:, 1, 32 * g:32 * g + NC_BLK], w2c[:, 1, :],
                                  start=True, stop=True)
                    last.then_inc(*done("mm", ("mm", "cv")))
                if k == "mh":
                    h_ = a[0]
                    sel = con[0:4, C_SEL + h_ * P:C_SEL + (h_ + 1) * P]
                    pe.wait_ge(*at("mmt"))
                    pe.wait_ge(*at("men"))
                    b = open_bank(("Mb", h_))
                    mm(b[:, :], sel, mrows[0:4, 1, :], start=True, stop=True).then_inc(*done("mm", ("mm", "Mb", h_)))
                    pe.wait_ge(*at("done", "mk", h_))
                    pe.wait_ge(*at("done", "mq", h_))
                    for s in range(NT):
                        b = open_bank(("KQ", h_, s))
                        mm(b[:, 0:SEQ - P * s], mkT[:, h_, tok(s)], mqT[:, h_, P * s:SEQ], start=True, stop=True)\
                            .then_inc(*done("mm", ("mm", "KQ", h_, s)))
                    b = open_bank(("En", h_))
                    mm(b[:, :], sel, mrows[0:4, 4, :], start=True, stop=True).then_inc(*done("mm", ("mm", "En", h_)))
                    num, den = open_acc(("num", h_)), open_acc(("den", h_))
                    for s in range(NT):
                        pe.wait_ge(*at("wtm", h_, s))
                        pe.wait_ge(*at("mv", s))
                        wb = wk[(h_ * NT + s) % 2][:, 0:SEQ - P * s]
                        mm(num[:, P * s:SEQ], mvt[:, s, h_ * P:(h_ + 1) * P], wb, start=(s == 0), stop=(s == NT - 1),
                           skip_group_check=True)
                        mm(den[:, P * s:SEQ], ones, wb, start=(s == 0), stop=(s == NT - 1), skip_group_check=True)\
                            .then_inc(*done("mm", ("numden", h_, s), *([("mden", h_)] if s == NT - 1 else [])))
                if k == "mnorm":
                    b = open_bank(("mss", a[0]))
                    pe.wait_ge(*at("msq", a[0]))
                    mm(b[:, :], ones, mqT[:, a[0], :], start=True, stop=True).then_inc(*done("mm", ("mm", "mss", a[0])))
                if k == "nS":
                    i, g, br = a
                    lo = HD * g
                    pe.wait_ge(*at("kcT"))
                    pe.wait_ge(*at("done", "ak", 1))
                    if br == "c":
                        b = open_bank(("nS", *a, 0))
                        for r in range(4):
                            last = mm(b[:, 32 * r:32 * r + NC_BLK], aqT[lo:lo + HD, r, tok(i)], kcT[lo:lo + HD, :],
                                      start=True, stop=True)
                        last.then_inc(*done("mm", ("mm", "nS", *a, 0)))
                    else:
                        w = P * (i + 1)
                        for r in range(4):
                            b = open_bank(("nS", *a, r))
                            mm(b[:, 0:w], aqT[lo:lo + HD, r, tok(i)], akT[lo:lo + HD, "sw".index(br), 0:w],
                               start=True, stop=True).then_inc(*done("mm", ("mm", "nS", *a, r)))
                if k == "nP":
                    i, g, br = a
                    u = NSEQ[a]
                    lo = HD * g
                    o = open_acc(("nO", i)) if (g, br) == (0, "c") else acc(("nO", i))
                    nk = 1 if br == "c" else i + 1
                    pe.wait_ge(*at("nprob", *a))

                    def turn(kt):
                        b = open_bank(("nPT", *a, kt))
                        for r in range(4):
                            if br == "c":
                                last = nc.tensor.transpose(b[0:NC_BLK, tok(r)], scb[g][:, r, :], ident)
                            else:
                                last = nc.tensor.transpose(b[:, tok(r)], nSb[u % 2][:, r, tok(kt)], ident)
                        last.then_inc(*done("mm", ("mm", "nPT", *a, kt)))

                    turn(0)
                    for kt in range(nk):
                        if kt + 1 < nk:
                            turn(kt + 1)
                        pe.wait_ge(*at("nPT", *a, kt))
                        n = NPT[(*a, kt)]
                        if br == "c":
                            pe.wait_ge(*at("vct"))
                            last = mm(o[lo:lo + HD, :], vct[:, g, :], nPb[n % 4][0:NC_BLK, :], start=True, stop=False)
                        else:
                            v = avt[:, kt, P * "sw".index(br) + HD * g:P * "sw".index(br) + HD * (g + 1)]
                            last = mm(o[lo:lo + HD, :], v, nPb[n % 4][:, :], start=False, stop=(br == "w" and kt == nk - 1))
                        last.then_inc(*done("mm", ("npv", n), *([("nO", i)] if (g, br, kt) == (1, "w", nk - 1) else [])))
                if k == "up":
                    if a[0] == 0:
                        await_hn("ln2")
                    linear(("upg", a[0]), [("upg", a[0], 0)], hn)
                    linear(("upv", a[0]), [("upv", a[0], 0)], hn)

        @block.vector
        def _(dve):
            chain = [0]

            def link(ins_):
                chain[0] += 1
                ins_.then_inc(*done("dve_step", ("dve_step", chain[0])))
                dve.wait_ge(*at("dve_step", chain[0]))

            def ssadd(ver, m):
                dve.wait_ge(*at("sq", ver, m))
                n = KD * ver + m
                if m == 1:
                    nc.vector.tensor_tensor(ssacc[:, :], sq[:, (n - 1) % 3, :], sq[:, n % 3, :], ALU.add)\
                        .then_inc(*done("ssadd", ("ssadd", ver, m)))
                else:
                    dve.wait_ge(*at("ssadd", ver, m - 1))
                    nc.vector.tensor_tensor(ssacc[:, :], ssacc[:, :], sq[:, n % 3, :], ALU.add)\
                        .then_inc(*done("ssadd", ("ssadd", ver, m)))

            dve.wait_ge(*at("consts"))
            nc.vector.tensor_scalar(negsink[:, :], rowb[:, R_SINK:R_SINK + ATT_HEADS], -1.0, None, ALU.mult)
            for step in STEPS:
                k, a = step[0], step[1:]
                if k == "load":
                    for m in range(1, KD):
                        ssadd(0, m)
                if k == "norm":
                    ver = a[0]
                    dve.wait_ge(*at("rms", ver))
                    link(nc.vector.reciprocal(rt[:, :], rt[:, :]))
                    for name in NORM_OF[ver]:
                        dst = hnB if name == "kv" else hn
                        for m in range(KD):
                            nc.vector.scalar_tensor_tensor(dst[:, m, :], h[:, m, :],
                                                           vec[:, V_NORM[name] + m:V_NORM[name] + m + 1], rt[:, :],
                                                           ALU.mult, ALU.mult).then_inc(*done("hn", ("hn", name, m)))
                if k == "proj" and a[1] < 6:
                    g, i = a
                    ch = [16 + g, 20 + g][i] if i < 2 else GT * g + i - 2
                    c = cva[(g * 6 + i) % 2]
                    b = ps(step)
                    dve.wait_ge(*at("conv0", g, i))
                    for s in range(1, TAPS):
                        w = vec[:, V_CW + (3 - s) * 24 + ch:V_CW + (3 - s) * 24 + ch + 1]
                        x = nc.vector.scalar_tensor_tensor(c[:, s:SEQ], b[:, 0:SEQ - s], w, c[:, s:SEQ], ALU.mult, ALU.add)
                        if s < TAPS - 1:
                            link(x)
                        else:
                            x.then_inc(*done("conv", ("conv", g, i), ("free", *step)))
                if k == "dt":
                    dve.wait_ge(*at("mm", "dt"))
                    b = ps(("dt",))[:, 0:P].rearrange("p (a b) -> p a b", a=NT)
                    link(nc.vector.tensor_tensor(dtmp, b, over(rowb[:, R_DTB:R_DTB + HEADS], NT, 1), ALU.add))
                    nc.vector.scalar_tensor_tensor(dtmp2, dtmp, -1.0, dtmp, ALU.mult, ALU.min)\
                        .then_inc(*done("dtabs", ("dtabs",), ("free", "dt")))
                    dve.wait_ge(*at("dtln"))
                    link(nc.vector.scalar_tensor_tensor(dtb, dtmp, 0.0, dtmp2, ALU.max, ALU.add))
                    dve.wait_ge(*at("aexp"))
                    link(nc.vector.tensor_tensor(da, dtb, over(aneg[:, :], NT, 1), ALU.mult))
                    nc.vector.tensor_scalar(da, da, -1.0, None, ALU.mult).then_inc(*done("da", ("da",)))
                if k == "ssd0":
                    g = a[0]
                    dve.wait_ge(*at("mm", "cb", g))
                    nc.vector.tensor_tensor(cbm, ps(("cb", g))[:, :].rearrange("p (a b) -> p a b", a=NT), over(tri, NT, 1),
                                            ALU.mult).then_inc(*done("cbm", ("cbm", g), ("free", "cb", g)))
                if k == "ssd1":
                    g, c = a
                    n = g * NT + c
                    dve.wait_ge(*at("mm", "xt", g, c))
                    if n >= 2:
                        q = ((n - 2) // NT, (n - 2) % NT)
                        dve.wait_ge(*at("mm", "yd", *q))
                        if q[1] < NT - 1:
                            dve.wait_ge(*at("xde", *q))
                    nc.vector.tensor_tensor(xdt[c % 2], ps(("xt", g, c))[:, :].rearrange("p (a b) -> p a b", a=HPG),
                                            over(dtb[:, c, g * HPG:(g + 1) * HPG], HD, 2), ALU.mult)\
                        .then_inc(*done("xdt", ("xdt", g, c), ("free", "xt", g, c)))
                    dve.wait_ge(*at("dec", g, c, 1))
                    dve.wait_ge(*at("cbm", g))
                    nc.vector.tensor_tensor(dec[c % 2], dec[c % 2], over(cbm[:, c, :], HPG, 1), ALU.mult)\
                        .then_inc(*done("decm", ("decm", g, c)))
                if k == "ssd2":
                    g, c = a
                    if c:
                        dve.wait_ge(*at("mm", "yo", g, c))
                        dve.wait_ge(*at("cums"))
                        link(nc.vector.tensor_tensor(yoe, ps(("yo", g, c))[:, :].rearrange("p (a b) -> p a b", a=HPG),
                                                     over(cums[:, 0, c * HEADS + g * HPG:c * HEADS + (g + 1) * HPG], HD, 2),
                                                     ALU.mult))
                        if g >= 1:
                            dve.wait_ge(*at("mm", "yt", g - 1, 3))
                        nc.vector.tensor_tensor(ytok[:, c, :].rearrange("p (a b) -> p a b", a=HPG), yoe,
                                                ps(("yd", g, c))[:, :].rearrange("p (a b) -> p a b", a=HPG), ALU.add)\
                            .then_inc(*done("ytok", ("ytok", g, c), ("free", "yd", g, c), ("free", "yo", g, c)))
                    if 1 <= c < NT - 1:
                        dve.wait_ge(*at("mm", "st", g, c))
                        dve.wait_ge(*at("pdec", g, c))
                        pn = prev[(c + 1) % 2]
                        nc.vector.tensor_tensor(pn, pn, ps(("st", g, c))[:, :].rearrange("p (a b) -> p a b", a=HPG), ALU.add)\
                            .then_inc(*done("prev", ("prev", g, c + 1), ("free", "st", g, c)))
                if k == "yt":
                    g, m = a
                    ti = GT * g + m
                    dve.wait_ge(*at("mm", *step))
                    nc.vector.scalar_tensor_tensor(yn[:, ti, :], xs[g % 2][:, m, :], vec[:, V_D + ti:V_D + ti + 1], ps(step)[:, :],
                                                   ALU.mult, ALU.add).then_inc(*done("yskip", ("yskip", g, m), ("free", *step)))
                    if m == 0:
                        dve.wait_ge(*at("ysq", g, 0))
                        nc.vector.tensor_copy(yoe[:, 0, 0:1], yac[:, 0:1]).then_inc(*done("yadd", ("yadd", g, 0)))
                    else:
                        dve.wait_ge(*at("ysq", g, m))
                        dve.wait_ge(*at("yadd", g, m - 1))
                        nc.vector.tensor_tensor(yac, yac, ysq, ALU.add).then_inc(*done("yadd", ("yadd", g, m)))
                if k == "gn":
                    g = a[0]
                    dve.wait_ge(*at("grms", g))
                    link(nc.vector.reciprocal(ysq, ysq))
                    for m in range(GT):
                        ti = GT * g + m
                        nc.vector.scalar_tensor_tensor(yn[:, ti, :], yn[:, ti, :], vec[:, V_GN + ti:V_GN + ti + 1], ysq,
                                                       ALU.mult, ALU.mult).then_inc(*done("yn", ("yn", g, m)))
                if k == "out":
                    ver, m = a
                    dve.wait_ge(*at("mm", *step))
                    nc.vector.tensor_tensor(h[:, m, :], h[:, m, :], ps(step)[:, :], ALU.add)\
                        .then_inc(*done("h", ("h", ver, m), ("free", *step)))
                    if m >= 2:
                        ssadd(ver, m - 1)
                    if m == KD - 1:
                        ssadd(ver, m)
                if k == "ple":
                    i, m = a
                    ver = 2 * i + 2 if i < 2 else 7
                    gb = (gsig2 if i == 2 else gsig)[m % 2]
                    dve.wait_ge(*at("gsig", i, m))
                    dve.wait_ge(*at("pp", i, m))
                    link(nc.vector.tensor_tensor(gb, gb, pp[i][:, m, :], ALU.mult))
                    nc.vector.tensor_tensor(h[:, m, :], h[:, m, :], gb, ALU.add).then_inc(*done("h", ("h", ver, m)))
                    if m >= 2:
                        ssadd(ver, m - 1)
                    if m == KD - 1:
                        ssadd(ver, m)
                if k == "rope_tables":
                    posf = small[:, 0, 0:NT]
                    link(nc.vector.tensor_copy(posf, pos[:, :]))
                    ang = rtmp[:, 0, :]
                    a3 = ang.rearrange("p (t f) -> p t f", t=NT)
                    link(nc.vector.tensor_tensor(a3, over(posf, 32, 2), over(rowb[:, R_FREQ:R_FREQ + 32], NT, 1), ALU.mult))
                    big = float(1.5 * 2 ** 23)
                    link(nc.vector.tensor_scalar(rtmp[:, 1, :], ang, float(1 / (2 * np.pi)), big, ALU.mult, ALU.add))
                    link(nc.vector.tensor_scalar(rtmp[:, 1, :], rtmp[:, 1, :], -big, None, ALU.add))
                    c1 = 6.28125
                    c2 = float(np.float32(2 * np.pi - c1))
                    c3 = float(2 * np.pi - c1 - c2)
                    for c in (c1, c2, c3):
                        link(nc.vector.scalar_tensor_tensor(ang, rtmp[:, 1, :], -c, ang, ALU.mult, ALU.add))
                    pi = 3.1415925
                    link(nc.vector.tensor_scalar(rtmp[:, 2, :], ang, pi, -pi, ALU.min, ALU.max))
                    nc.vector.scalar_tensor_tensor(rtmp[:, 3, :], rtmp[:, 2, :], -1.0, rtmp[:, 2, :], ALU.mult, ALU.max)\
                        .then_inc(*done("angles", ("angles",)))
                    dve.wait_ge(*at("cos"))
                    for j, (w, ws) in enumerate(((R_QN, R_QNS), (R_KN, R_KNS))):
                        for half in range(2):
                            cd = ctab[:, 2 * j, :].rearrange("p (t d) -> p t d", t=NT)[:, :, 32 * half:32 * half + 32]
                            sd = ctab[:, 2 * j + 1, :].rearrange("p (t d) -> p t d", t=NT)[:, :, 32 * half:32 * half + 32]
                            cs = rtmp[:, 5, :].rearrange("p (t d) -> p t d", t=NT)
                            sn = rtmp[:, 4, :].rearrange("p (t d) -> p t d", t=NT)
                            link(nc.vector.tensor_tensor(cd, cs, over(rowb[:, w + 32 * half:w + 32 * half + 32], NT, 1), ALU.mult))
                            link(nc.vector.tensor_tensor(sd, sn, over(rowb[:, ws + 32 * half:ws + 32 * half + 32], NT, 1), ALU.mult))
                        link(nc.vector.tensor_scalar(
                            ctab[:, 2 * j + 1, :].rearrange("p (t d) -> p t d", t=NT)[:, :, 0:32],
                            ctab[:, 2 * j + 1, :].rearrange("p (t d) -> p t d", t=NT)[:, :, 0:32], -1.0, None, ALU.mult))
                if k in ("kv", "q"):
                    nh = 4 if k == "kv" else 8
                    w = nh * HD
                    for t in range(NT):
                        key = ("kv", t) if k == "kv" else ("q", a[0], t)
                        n = {"kv": 0, "q": 1 + (a[0] if a else 0)}[k] * NT + t
                        b = t % 2
                        dve.wait_ge(*at("qsq", *key))
                        nc.vector.tensor_reduce(small[:, 4 * b, 0:nh], qsq[b][:, 0:w].rearrange("p (h d) -> p h d", h=nh), AXX,
                                                ALU.add).then_inc(*done("qss", ("qss", n)))
                        dve.wait_ge(*at("qrms", *key))
                        link(nc.vector.reciprocal(small[:, 4 * b + 2, 0:nh], small[:, 4 * b + 1, 0:nh]))
                        if n >= 2:
                            p2 = ("kv", n - 2) if n - 2 < NT else ("q", (n - 2) // NT - 1, (n - 2) % NT)
                            dve.wait_ge(*at("roped", *p2))
                        q3 = qn[b][:, 0:w].rearrange("p (h d) -> p h d", h=nh)
                        nc.vector.tensor_tensor(q3, ps(key)[:, 0:w].rearrange("p (h d) -> p h d", h=nh),
                                                over(small[:, 4 * b + 2, 0:nh], HD, 2), ALU.mult)\
                            .then_inc(*done("qn", ("qn", *key), ("free", *key)))
                        dve.wait_ge(*at("qn", *key))
                        sn = ctab[:, 1 if k == "q" else 3, :].rearrange("p (t d) -> p t d", t=NT)[:, t, :]
                        r3 = rb[b][:, 0:w].rearrange("p (h d) -> p h d", h=nh)
                        nc.vector.tensor_tensor(r3[:, :, 0:32], q3[:, :, 32:64], over(sn[:, 0:32], nh, 1), ALU.mult)
                        nc.vector.tensor_tensor(r3[:, :, 32:64], q3[:, :, 0:32], over(sn[:, 32:64], nh, 1), ALU.mult)\
                            .then_inc(*done("ropeb", ("ropeb", *key)))
                if k == "aS":
                    n, g = a
                    u = n * KV_HEADS + g
                    w = P if n == 0 else 256
                    per = SEQ // w
                    s = Sb[u % 2]
                    mask = swa[:, P:256] if n == 0 else swa
                    sm = small[:, 4 * (u % 2):4 * (u % 2) + 4, :]
                    if u >= 2:
                        dve.wait_ge(*at("mm", "aPT", *divmod(u - 2, KV_HEADS), 0 if u - 2 < KV_HEADS else 1))
                    for j in range(4 // per):
                        dve.wait_ge(*at("mm", "aS", n, g, j))
                        nc.vector.tensor_tensor(s[:, per * j:per * (j + 1), 0:w],
                                                ps(("aS", n, g, j))[:, :].rearrange("p (a b) -> p a b", a=per),
                                                over(mask, per, 1), ALU.add)\
                            .then_inc(*done("amask", ("amask", n, g, j), ("free", "aS", n, g, j)))
                    dve.wait_ge(*at("amask", n, g, 4 // per - 1))
                    link(nc.vector.tensor_reduce(sm[:, 0, 0:4], s[:, :, 0:w], AXX, ALU.max))
                    link(nc.vector.scalar_tensor_tensor(sm[:, 1, 0:4], sm[:, 0, 0:4], -1.0, negsink[:, 4 * g:4 * g + 4],
                                                        ALU.mult, ALU.min))
                    nc.vector.tensor_tensor(sm[:, 1, 4:8], sm[:, 1, 0:4], rowb[:, R_SINK + 4 * g:R_SINK + 4 * g + 4],
                                            ALU.add).then_inc(*done("anegm", ("anegm", n, g)))
                    dve.wait_ge(*at("aesink", n, g))
                    link(nc.vector.tensor_tensor(sm[:, 3, 4:8], sm[:, 2, 0:4], sm[:, 1, 8:12], ALU.add))
                    nc.vector.reciprocal(sm[:, 3, 0:4], sm[:, 3, 4:8]).then_inc(*done("arec", ("arec", n, g)))
                if k == "aP":
                    n, g = a
                    u = n * KV_HEADS + g
                    if n:
                        dve.wait_ge(*at("mm", "aPT", n, g, 1))
                        if u >= 2:
                            dve.wait_ge(*at("pv", *divmod(u - 2, KV_HEADS)))
                        nc.vector.tensor_copy(PTb[u % 2][:, 1, :], ps(("aPT", n, g, 1))[:, :])\
                            .then_inc(*done("aPT_dve", ("aPT", n, g, 1), ("free", "aPT", n, g, 1)))
                    if g % 2 == 1:
                        G2 = g // 2
                        dve.wait_ge(*at("pv", n, g))
                        dve.wait_ge(*at("gs", KD - 1))
                        nc.vector.tensor_tensor(og[:, 4 * G2:4 * G2 + 4, tok(n)],
                                                acc(("aO", n, G2))[:, :].rearrange("p (a b) -> p a b", a=4),
                                                gs[:, 4 * G2:4 * G2 + 4, tok(n)], ALU.mult)\
                            .then_inc(*done("og", ("og", n, G2), ("accfree", "aO", n, G2)))
                if k == "mrow":
                    dve.wait_ge(*at("mm", "mi"))
                    nc.vector.tensor_scalar(mrows[0:4, 0, :], ps(("mi",))[0:4, :], mbias[:, 0:1], None, ALU.add)\
                        .then_inc(*done("mi", ("mi_row",), ("free", "mi")))
                    dve.wait_ge(*at("mm", "mf"))
                    nc.vector.tensor_scalar(mrows[0:4, 1, :], ps(("mf",))[0:4, :], mbias[:, 1:2], None, ALU.add)\
                        .then_inc(*done("mf", ("mf_row",), ("free", "mf")))
                    dve.wait_ge(*at("mf_row"))
                    nc.vector.scalar_tensor_tensor(mrows[0:4, 2, :], mrows[0:4, 1, :], -1.0, mrows[0:4, 1, :], ALU.mult, ALU.min)\
                        .then_inc(*done("mfabs", ("mfabs",)))
                    link(nc.vector.memset(mrows[0:4, 4, :], 0.0))
                    dve.wait_ge(*at("mfln"))
                    link(nc.vector.scalar_tensor_tensor(mrows[0:4, 1, :], mrows[0:4, 1, :], 0.0, mrows[0:4, 2, :],
                                                        ALU.min, ALU.subtract))
                    link(nc.vector.tensor_tensor_scan(mrows[0:4, 3, :], mrows[0:4, 1, :], mrows[0:4, 4, :], 0.0, ALU.add, ALU.add))
                    nc.vector.tensor_tensor(mrows[0:4, 0, :], mrows[0:4, 0, :], mrows[0:4, 3, :], ALU.subtract)\
                        .then_inc(*done("mrrow", ("mrrow",)))
                    dve.wait_ge(*at("mrrow"))
                    link(nc.vector.tensor_tensor_scan(mrows[0:4, 1, :], mrows[0:4, 0, :], mrows[0:4, 0, :], 0.0, ALU.max, ALU.max))
                    nc.vector.tensor_tensor(mrows[0:4, 2, :], mrows[0:4, 1, :], mrows[0:4, 3, :], ALU.add)\
                        .then_inc(*done("mmt", ("mmt",)))
                if k == "cmp_in":
                    j = a[0]
                    dve.wait_ge(*at("done", *step))
                    src = bass.AP(tensor=ckv.tensor, offset=ckv[:, j, :].offset,
                                  ap=[list(ckv[:, j, :].ap[0]), [1, CMP_BLOCK], [CMP_STRIDE, NC_BLK]])
                    nc.vector.tensor_tensor(cblk[j], src, over(peT[:, j, :], NC_BLK, 2), ALU.add)\
                        .then_inc(*done("cblk", ("cblk", j)))
                if k == "cmp":
                    j = a[0]
                    x = ctm[:, 0, :].rearrange("p (g n) -> p g n", g=2)[:, :, 0:NC_BLK]
                    y = ctm[:, 1, :].rearrange("p (g n) -> p g n", g=2)[:, :, 0:NC_BLK]
                    z = ctm[:, 2, :].rearrange("p (g n) -> p g n", g=2)[:, :, 0:NC_BLK]
                    if j == 0:
                        dve.wait_ge(*at("cblk", 1))
                        link(nc.vector.memset(ctm[:, :, :], 0.0))
                    for g in range(2):
                        dve.wait_ge(*at("mm", "chid", j, g))
                        nc.vector.tensor_copy(x[:, g, :], ps(("chid", j, g))[:, 0:NC_BLK])\
                            .then_inc(*done("chidc", ("chidc", j, g), ("free", "chid", j, g)))
                    dve.wait_ge(*at("chidc", j, 1))
                    link(nc.vector.tensor_tensor(y, x, x, ALU.mult))
                    link(nc.vector.tensor_scalar(y, y, 0.044715, 1.0, ALU.mult, ALU.add))
                    nc.vector.tensor_tensor(y, y, x, ALU.mult).then_inc(*done("gelu_in", ("gelu_in", j)))
                    dve.wait_ge(*at("ctanh", j))
                    link(nc.vector.tensor_scalar(z, y, 1.0, 0.5, ALU.add, ALU.mult))
                    nc.vector.tensor_tensor(chid[:, j, :].rearrange("p (g n) -> p g n", g=2)[:, :, 0:NC_BLK], z, x, ALU.mult)\
                        .then_inc(*done("gelu", ("gelu", j)))
                    dve.wait_ge(*at("gelu", j))
                if k == "mh":
                    h_ = a[0]
                    dve.wait_ge(*at("rcol"))
                    dve.wait_ge(*at("Mneg", h_))

                    def marg(s):
                        n = h_ * NT + s
                        if n >= 2:
                            dve.wait_ge(*at("wt", *divmod(n - 2, NT)))
                        nc.vector.tensor_scalar(wt[n % 2][:, 0:SEQ - P * s], Mneg[:, P * s:SEQ], rcol[:, s, h_:h_ + 1], 0.0,
                                                ALU.add, ALU.min).then_inc(*done("marg", ("marg", h_, s)))

                    marg(0)
                    for s in range(NT):
                        if s + 1 < NT:
                            marg(s + 1)
                        n = h_ * NT + s
                        w = SEQ - P * s
                        dve.wait_ge(*at("mexpd", h_, s))
                        dve.wait_ge(*at("mm", "KQ", h_, s))
                        if n >= 2:
                            dve.wait_ge(*at("numden", *divmod(n - 2, NT)))
                        nc.vector.tensor_tensor(wk[n % 2][:, 0:w], wt[n % 2][:, 0:w], ps(("KQ", h_, s))[:, 0:w], ALU.mult)\
                            .then_inc(*done("wt", ("wt", h_, s), ("free", "KQ", h_, s)))
                    dve.wait_ge(*at("mabs", h_))
                    dve.wait_ge(*at("mm", "En", h_))
                    dve.wait_ge(*at("mden", h_))
                    nc.vector.tensor_tensor(mtmp[1], mtmp[0], ps(("En", h_))[:, :], ALU.max)\
                        .then_inc(*done("mdmax", ("mdmax", h_), ("free", "En", h_)))
                    dve.wait_ge(*at("mdmax", h_))
                    link(nc.vector.reciprocal(mtmp[1], mtmp[1]))
                    nc.vector.tensor_tensor(hm[:, h_, :], mtmp[1], acc(("num", h_))[:, :], ALU.mult)\
                        .then_inc(*done("hm", ("hm", h_), ("accfree", "num", h_)))
                if k == "mnorm":
                    h_ = a[0]
                    dve.wait_ge(*at("mrms", h_))
                    if h_:
                        dve.wait_ge(*at("mnormed", h_ - 1))
                    nc.vector.reciprocal(mtmp[1], mtmp[0]).then_inc(*done("mrstd", ("mrstd", h_)))
                    dve.wait_ge(*at("mrstd", h_))
                    nc.vector.scalar_tensor_tensor(hm[:, h_, :], hm[:, h_, :], vec[:, V_MN + h_:V_MN + h_ + 1], mtmp[1],
                                                   ALU.mult, ALU.mult).then_inc(*done("mnormed", ("mnormed", h_)))
                if k == "nS":
                    i, g, br = a
                    u = NSEQ[a]
                    sm = small[:, 4 * (u % 2):4 * (u % 2) + 4, :]
                    h0 = 4 * g
                    gcol = gat[:, i, :].rearrange("p (h b) -> p b h", b=3)[:, "csw".index(br), h0:h0 + 4]
                    if br == "c":
                        s = scb[g]
                        if i:
                            dve.wait_ge(*at("mm", "nPT", i - 1, g, "c", 0))
                        dve.wait_ge(*at("mm", "nS", *a, 0))
                        nc.vector.tensor_tensor(s[:, :, :], ps(("nS", *a, 0))[:, 0:P].rearrange("p (r c) -> p r c", r=4)[:, :, 0:NC_BLK],
                                                cmpb[:, i, h0:h0 + 4, :], ALU.add)\
                            .then_inc(*done("nmask", ("nmask", *a), ("free", "nS", *a, 0)))
                        dve.wait_ge(*at("nmask", *a))
                        link(nc.vector.tensor_reduce(sm[:, 0, 0:4], s[:, :, :], AXX, ALU.max))
                        nc.vector.tensor_tensor(s[:, :, :], s[:, :, :], over(sm[:, 0, 0:4], NC_BLK, 2), ALU.subtract)\
                            .then_inc(*done("nnegm", ("nnegm", *a)))
                        dve.wait_ge(*at("nexp", *a))
                        link(nc.vector.tensor_reduce(sm[:, 2, 0:4], s[:, :, :], AXX, ALU.add))
                        link(nc.vector.reciprocal(sm[:, 3, 4:8], sm[:, 2, 0:4]))
                        if i == 0:
                            link(nc.vector.tensor_scalar(sm[:, 3, 4:8], sm[:, 3, 4:8], rowvalid, None, ALU.mult))
                        dve.wait_ge(*at("avg", i))
                        link(nc.vector.tensor_tensor(sm[:, 3, 0:4], sm[:, 3, 4:8], gcol, ALU.mult))
                        nc.vector.tensor_tensor(s[:, :, :], s[:, :, :], over(sm[:, 3, 0:4], NC_BLK, 2), ALU.mult)\
                            .then_inc(*done("nprobc", ("nprob", *a)))
                    else:
                        w = P * (i + 1)
                        s = nSb[u % 2]
                        if u == 0:
                            dve.wait_ge(*at("alibi"))
                        if NPREV[a] is not None:
                            dve.wait_ge(*at("mm", "nPT", *NPREV[a], NPREV[a][0]))
                        for r in range(4):
                            dve.wait_ge(*at("mm", "nS", *a, r))
                            nc.vector.tensor_tensor_reduce(out=s[:, r, 0:w], in0=ps(("nS", *a, r))[:, 0:w],
                                                           in1=alibi[:, h0 + r, SEQ - w:SEQ], scale=1.0, scalar=-3e38,
                                                           op0=ALU.add, op1=ALU.max, accum_out=sm[:, 0, r:r + 1])\
                                .then_inc(*done("nmask", ("nmask", *a, r), ("free", "nS", *a, r)))
                        dve.wait_ge(*at("nmask", *a, 3))
                        nc.vector.tensor_scalar(sm[:, 1, 0:4], sm[:, 0, 0:4], -1.0, None, ALU.mult)\
                            .then_inc(*done("nnegm", ("nnegm", *a)))
                        dve.wait_ge(*at("nexp", *a))
                        link(nc.vector.reciprocal(sm[:, 3, 4:8], sm[:, 2, 0:4]))
                        nc.vector.tensor_tensor(sm[:, 3, 0:4], sm[:, 3, 4:8], gcol, ALU.mult)\
                            .then_inc(*done("nrec", ("nrec", *a)))
                if k == "nP":
                    i, g, br = a
                    if a == (0, 0, "c"):
                        dve.wait_ge(*at("mix", M_HEADS - 1))
                    for kt in range(1 if br == "c" else i + 1):
                        n = NPT[(*a, kt)]
                        if n % 2 == 1:
                            dve.wait_ge(*at("mm", "nPT", *a, kt))
                            if n >= 4:
                                dve.wait_ge(*at("npv", n - 4))
                            rows = NC_BLK if br == "c" else P
                            nc.vector.tensor_copy(nPb[n % 4][0:rows, :], ps(("nPT", *a, kt))[0:rows, :])\
                                .then_inc(*done("nPT_dve", ("nPT", *a, kt), ("free", "nPT", *a, kt)))
                    if (g, br) == (1, "w"):
                        dve.wait_ge(*at("nO", i))
                        nc.vector.tensor_copy(mixT[:, 4:8, tok(i)], acc(("nO", i))[:, :].rearrange("p (a b) -> p a b", a=4))\
                            .then_inc(*done("nog", ("nog", i), ("accfree", "nO", i)))
                if k == "up":
                    m = a[0]
                    b = ps(("upg", m))
                    c = fca[m % 2]
                    dve.wait_ge(*at("fconv0", m))
                    for s in range(1, 3):
                        w = vec[:, V_C2W + (2 - s) * FT + m:V_C2W + (2 - s) * FT + m + 1]
                        x = nc.vector.scalar_tensor_tensor(c[:, s:SEQ], b[:, 0:SEQ - s], w, c[:, s:SEQ], ALU.mult, ALU.add)
                        if s == 1:
                            link(x)
                        else:
                            x.then_inc(*done("fconv", ("fconv", m), ("free", "upg", m)))
                    dve.wait_ge(*at("mm", "upv", m))
                    dve.wait_ge(*at("fsilu", m))
                    nc.vector.tensor_tensor(ff[:, m, :], fsl[m % 2], ps(("upv", m))[:, :], ALU.mult)\
                        .then_inc(*done("ff", ("ff", m), ("free", "upv", m)))
    return ev.seen


NSEQ, NPREV, NPT = {}, {}, {}
for _s in STEPS:
    if _s[0] == "nS":
        _a = _s[1:]
        _big = [x for x in NSEQ if x[2] != "c"]
        NSEQ[_a] = len(_big)
        if _a[2] != "c":
            NPREV[_a] = _big[-2] if len(_big) >= 2 else None
    if _s[0] == "nP":
        for _k in range(1 if _s[3] == "c" else _s[1] + 1):
            NPT[(*_s[1:], _k)] = len(NPT)


def pack(v):
    f = {k: np.asarray(x) for k, x in v.items()}

    def cols(w, order):
        return w[:, order]

    pair16 = np.concatenate([np.arange(64) + 64 * hh for G in range(2) for r in range(4) for hh in (8 * G + r, 8 * G + 4 + r)])
    pair8 = np.concatenate([np.arange(64) + 64 * hh for r in range(4) for hh in (r, 4 + r)])
    wi = f["w_in_2"][0]
    o = np.cumsum([0, 512, 512, 512, 512, 4, 4, 512] + [128] * 6 + [24])
    mq, mk, mv, mo, mi, mf, aq, akc, avc, aks, avs, akw, avw, ag = (wi[:, o[i]:o[i + 1]] for i in range(14))
    stationary = {
        "ssm_in": f["ssm_in_w"][0], "ssm_out": f["ssm_out_w"][0], "attn_out": f["attn_out_w"][0][pair16],
        "attn_gate": cols(f["attn_in_w"][0][:, 1024:], pair16),
        "w_out": np.concatenate([f["w_out_2"][0][:512], f["w_out_2"][0][512:][pair8]]), "w_down": f["w_down_2"][0],
        "mq": mq, "mk": mk, "mo": mo, "aq": cols(aq, pair8), "ak": np.concatenate([aks, akw], 1),
        "cmp_in": np.concatenate([akc, avc], 1), "upg": f["w_up_2"][0][:, :D_FF], "upv": f["w_up_2"][0][:, D_FF:],
    }
    moving = {
        "kv": f["kv_w"], "attn_q": f["attn_in_w"][0][:, :1024], "mv": mv,
        "avg": np.concatenate([avs, avw, ag, np.zeros((D, SEQ - 280), np.float32)], 1),
    }
    gates = [f["ple_gate_w"][0], f["ple_gate_w"][1], f["w_ple_gate_2"][0]]
    projs = [f["ple_proj_w"][0], f["ple_proj_w"][1], f["w_ple_proj_2"][0]]
    ps_ = [f["p"][0, 0], f["p"][1, 0], f["p_2"][0, 0]]
    w1 = [f["cmp_k_w1_2"][0], f["cmp_v_w1_2"][0]]

    def block(b):
        k = b[0]
        if k == "p":
            return ps_[b[1]].T.reshape(2, P, SEQ).transpose(1, 0, 2)
        if k == "ple_proj":
            return projs[b[1]][:, b[2] * SEQ:(b[2] + 1) * SEQ].reshape(2, P, SEQ).transpose(1, 0, 2)
        if k == "ple_gate":
            return gates[b[1]][:, b[2] * P:(b[2] + 1) * P].reshape(KD, P, P).transpose(1, 0, 2)
        if k == "cmp_w1":
            w = w1[b[1]].reshape(CMP_BLOCK, HD, P)[8 * b[2]:8 * b[2] + 8].transpose(1, 0, 2)
            return np.concatenate([w, w], 0)
        if k in moving:
            w = moving[k][:, (b[1] * SEQ if k == "attn_q" else 0):][:, :SEQ]
            return w[256 * b[-1]:256 * (b[-1] + 1)].reshape(2, P, SEQ).transpose(1, 0, 2)
        w = stationary[k][D * b[2]:D * (b[2] + 1), b[1] * P:(b[1] + 1) * P]
        return w.reshape(KD, P, P).transpose(1, 0, 2)

    res = {"wstream": np.stack([block(b).reshape(P, BLK) for b in BLOCKS])}
    res["xT"] = np.ascontiguousarray(f["x"][0].T.reshape(KD, P, SEQ))

    def tiles(x):
        return x.reshape(-1, P).T

    norms = [f["ssm_norm_w"], f["kv_norm_w"], f["attn_norm_w"], f["ple_norm_w"][0], f["ple_norm_w"][1], f["ln1_g_2"],
             f["ln2_g_2"], f["ple_norm_g_2"], f["final_g_2"]]
    vec = [tiles(x) for x in norms] + [tiles(f["ssm_conv_w"]), tiles(f["ssm_conv_b"]), tiles(f["ssm_gnorm_w"]),
                                       tiles(np.repeat(f["ssm_d"][0], HD)), tiles(f["conv_w_2"]), tiles(f["conv_b_2"]),
                                       tiles(f["mlstm_norm_g_2"])]
    res["vec"] = np.concatenate(vec, 1)
    assert res["vec"].shape == (P, NV)
    qw, kw = f["q_norm_w"][0], f["k_norm_w"]
    half = 32
    inv_freq = (10000.0 ** (-(np.arange(half, dtype=np.float32) * 2.0 / HD))).astype(np.float32)
    row = np.concatenate([f["ssm_dt_bias"][0], f["ssm_a_log"][0], qw, qw[half:], qw[:half], kw, kw[half:], kw[:half],
                          f["attn_sinks"][0], inv_freq])
    res["rowb"] = np.broadcast_to(row, (P, NR))
    res["wdt"] = f["ssm_in_w"][0][:, -HEADS:].reshape(KD, P, HEADS).transpose(1, 0, 2)
    res["wif"] = np.concatenate([mi, mf], 1).reshape(KD, P, 8).transpose(1, 0, 2)
    res["w2c"] = np.stack([f["cmp_k_w2_2"][0], f["cmp_v_w2_2"][0]], 1)
    pe = np.stack([f["cmp_pos_k_2"][0].T, f["cmp_pos_v_2"][0].T], 1)
    res["peT"] = np.concatenate([pe, pe], 0)
    res["mbias"] = f["mlstm_gate_bias_2"][0].reshape(2, 4).T
    res["pos"] = f["positions"][0].reshape(NT, P).T.astype(np.int32)
    res.update(constants())
    return {k: np.ascontiguousarray(x) for k, x in res.items()}


def constants():
    i = np.arange(P)
    con = np.zeros((P, NCON), np.float32)
    con[:, C_ID:C_ID + P] = np.eye(P)
    con[:, C_T:C_T + P] = i[:, None] <= i[None, :]
    con[:, C_U:C_U + P] = i[:, None] > i[None, :]
    con[:, C_ONE:C_ONE + P] = 1.0
    c = np.arange(256)
    con[:, C_SWA:C_SWA + 256] = np.where((c[None, :] - P <= i[:, None]) & (c[None, :] > i[:, None]), 0.0, NEG)
    slope = 2.0 ** -(np.arange(A_HEADS) + 1.0)
    t = np.arange(SEQ).reshape(NT, P).T
    end = CMP_STRIDE * np.arange(NC_BLK) + CMP_BLOCK - 1
    dist = t[:, :, None, None] - end[None, None, None, :]
    cb = np.where(dist >= 0, -slope[None, None, :, None] * dist, NEG)
    con[:, C_CMP:C_RV] = cb.reshape(P, -1)
    con[:, C_RV] = i >= CMP_BLOCK - 1
    for h in range(4):
        con[h, C_SEL + h * P:C_SEL + (h + 1) * P] = 1.0
    d = 384 + i[:, None, None] - np.arange(SEQ)[None, None, :]
    ali = np.where(d >= 0, -slope[None, :, None] * d, NEG).astype(np.float32)
    return {"con": con, "alibi": ali}


def kernel(**inputs):
    import concourse.bacc as bacc
    from concourse.bass_utils import run_bass_kernel_spmd as run

    arrays = pack(inputs)
    known = None
    for _ in range(2):
        nc = bacc.Bacc("TRN2", target_bir_lowering=False, num_devices=1)
        aps = {k: nc.dram_tensor("in_" + k, x.shape, mybir.dt.from_np(x.dtype), kind="ExternalInput").ap()
               for k, x in arrays.items()}
        out = nc.dram_tensor("outT", (KD, P, SEQ), F32, kind="ExternalOutput").ap()
        known = build(nc, aps, out, known)
    r = run(nc, [{"in_" + k: x for k, x in arrays.items()}], core_ids=[0])
    return r.results[0]["outT"].reshape(D, SEQ).T[None]
```

```python
from contextlib import ExitStack

import numpy as np

import concourse.bass as bass
from concourse import mybir

F32 = mybir.dt.float32
I32 = mybir.dt.int32
F32R = mybir.dt.float32r
ALU = mybir.AluOpType
ACT = mybir.ActivationFunctionType
AXX = mybir.AxisListType.X

P = 128
SEQ = 512
NT = SEQ // P
D = 1024
KD = D // P
EPS = 1e-6
NEG = -1e30

GROUPS = 4
HPG = 8
HEADS = GROUPS * HPG
HD = 64
D_INNER = 2048
GT = 4
D_STATE = 128
TAPS = 4
ATT_HEADS = 16
KV_HEADS = 4
M_HEADS = 4
A_HEADS = 8
NC_BLK = 31
CMP_BLOCK = 32
CMP_STRIDE = 16
D_FF = 2048
FT = D_FF // P
PLE = 256

NSLOT = 3
NSET = 2
NROT = 6
BLK = 1024

NORMS = ["ssm", "kv", "attn", "ple0", "ple1", "ln1", "ln2", "ple2", "final"]
V_NORM = {n: 8 * i for i, n in enumerate(NORMS)}
V_CW = 72
V_CB = V_CW + TAPS * 24
V_GN = V_CB + 24
V_D = V_GN + 16
V_C2W = V_D + 16
V_C2B = V_C2W + 3 * FT
V_MN = V_C2B + FT
NV = V_MN + 4

R_DTB, R_ALOG, R_QN, R_QNS, R_KN, R_KNS, R_SINK, R_FREQ = 0, 32, 64, 128, 192, 256, 320, 336
NR = R_FREQ + 32

C_ID, C_T, C_U, C_ONE, C_SWA, C_RV = 0, 128, 256, 384, 512, 768
NCON = C_RV + 1
NCMP = NT * A_HEADS * NC_BLK

NORM_OF = {0: ["ssm"], 1: ["ple0"], 2: ["kv"], 3: ["ple1"], 4: ["ln1"], 5: ["ln2"], 6: ["ple2"], 7: ["final"]}


def pipeline(x, units, closing):
    n = len(units)
    out = [(x + "S", *u) for u in units[:3]]
    for u in units[:2]:
        out += [(x + "E", *u), (x + "R", *u)]
    for i, u in enumerate(units):
        out.append((x + "T", *u))
        if i + 2 < n:
            out.append((x + "E", *units[i + 2]))
        if i and units[i - 1] in closing:
            out.append((x + "O", *units[i - 1]))
        if i + 3 < n:
            out.append((x + "S", *units[i + 3]))
        if i + 2 < n:
            out.append((x + "R", *units[i + 2]))
        out.append((x + "V", *u))
    return out + [(x + "O", *units[-1])]


def steps():
    out = [("load",), ("norm", 0)]
    proj = {g: [("proj", g, i) for i in range(10)] for g in range(GROUPS)}
    sout = {g: [("sout", g, m) for m in range(KD)] for g in range(GROUPS)}
    out += proj[0][:2] + [("dtl",), proj[0][2], ("dt",), proj[0][3], ("cum",)] + proj[0][4:]
    for g in range(GROUPS):
        scan = [("ssd0", g), ("ssd1", g, 0), ("ssd1", g, 1), ("ssd2", g, 0), ("ssd1", g, 2), ("ssd2", g, 1),
                ("ssd1", g, 3), ("ssd2", g, 2), ("ssd2", g, 3)]
        if g < 2:
            nxt = proj[g + 1]
            fill = nxt[:2] + (sout[g - 1] if g else []) + nxt[2:6]
            between, after = [[], nxt[6:7], nxt[7:8], nxt[8:9]], nxt[9:]
        elif g == 2:
            nxt, so = proj[3], sout[1]
            fill = nxt[:2] + so[:4] + nxt[2:6]
            between, after = [so[4 + m:5 + m] for m in range(GT)], nxt[6:7]
        else:
            nxt, so = proj[3], sout[2]
            fill = nxt[7:8] + so[:2] + nxt[8:9] + so[2:4] + nxt[9:] + [("psp", 0)]
            between, after = [so[4:6], [("pp", 0, 0)], [("pp", 0, 1)], [("pp", 0, 2)]], [("pp", 0, 3)] + so[6:]
        k = 0
        for i, x in enumerate(scan):
            out.append(x)
            while k < len(fill) and k * len(scan) < (i + 1) * len(fill):
                out.append(fill[k])
                k += 1
        out += fill[k:]
        for m in range(GT):
            out.append(("yt", g, m))
            out += between[m]
        out.append(("gn", g))
        out += after
    out += sout[GROUPS - 1] + [("pp", 0, 4), ("pp", 0, 5), ("norm", 1), ("pp", 0, 6), ("pp", 0, 7)]
    out += [("ple", 0, m) for m in range(KD)]
    out += [("norm", 2), ("kv", 0), ("kv", 1), ("hn2",), ("rope_tables",), ("kv", 2), ("kv", 3)]
    out += [("gate", 0), ("gate", 1)] + [("q", 0, b) for b in range(4)] + [("gate", 2), ("gate", 3), ("kT",)]
    out += [("q", 1, b) for b in range(4)] + [("gate", 4), ("qT", 0)] + [("gate", m) for m in range(5, KD)] + [("qT", 1)]
    units = [(n, g) for n in range(NT) for g in range(KV_HEADS)]
    out += pipeline("a", units, [x for x in units if x[1] % 2 == 1])
    out += [("out", 3, 0), ("out", 3, 1), ("psp", 1)] + [("out", 3, m) for m in range(2, KD)]
    out += [("pp", 1, m) for m in range(3)] + [("norm", 3)] + [("pp", 1, m) for m in range(3, KD)]
    out += [("ple", 1, m) for m in range(KD)]
    out += [("norm", 4)] + [("avg", b) for b in range(4)] + [("cmp_in", 0), ("mif",), ("mrow",), ("cmp_in", 1)]
    out += [("mv", b) for b in range(4)]
    lin = [("mq", m) for m in range(4)] + [("mk", m) for m in range(4)]
    lin += [("aq", m) for m in range(4)] + [("ak", 0), ("ak", 1)] + [("mo", m) for m in range(4)]
    for i, x in enumerate(lin):
        out.append(x)
        if i == 3:
            out.append(("mrcol",))
        if 1 <= i <= 4:
            out.append(("cmpq", 0, i - 1))
        if i == 6:
            out.append(("cmp", 0))
        if 7 <= i <= 10:
            out.append(("cmpq", 1, i - 7))
        if i == 12:
            out.append(("cmp", 1))
        if i == 15:
            out.append(("cmp2",))
    out += [("mA",)] + [("mB", h) for h in range(M_HEADS)]
    seq = [(i, g, b) for i in range(NT) for g in range(2) for b in "csw"]
    nsa = pipeline("n", seq, [x for x in seq if x[1:] == (1, "w")])
    out += nsa[:2] + [("mnorm",)] + nsa[2:]
    out += [("out", 5, m) for m in range(KD)] + [("norm", 5)]
    for m in range(FT + 4):
        if m < FT:
            out.append(("upg", m))
            if m:
                out.append(("fh", m - 1))
            out.append(("upv", m))
        if m == FT - 1:
            out.append(("fh", m))
        if m >= 4:
            out += [("dn", m // 4 - 1, 2 * (m % 4) + j) for j in range(2)]
        if m == FT - 1:
            out.append(("psp", 2))
    out += [("pp", 2, m) for m in range(3)] + [("norm", 6)] + [("pp", 2, m) for m in range(3, KD)]
    out += [("ple", 2, m) for m in range(KD)]
    out += [("norm", 7)]
    return out


STEPS = steps()


def jobs_of(step):
    k, a = step[0], step[1:]
    if k == "norm":
        return [("ss", a[0])]
    if k in ("dtl", "dt", "cum", "upg", "upv", "proj", "pp", "out", "sout", "dn", "gate", "mq", "mk", "mo", "aq", "ak", "cmp_in", "gn", "yt"):
        return [step]
    if k == "ple":
        return [step]
    if k == "ssd0":
        return [("cb", *a), ("bt", *a)]
    if k == "ssd1":
        return [("xt", *a), ("seg", *a, 0), ("seg", *a, 1)]
    if k == "ssd2":
        g, c = a
        return [("yd", g, c)] + ([("yo", g, c)] if c else []) + ([("st", g, c)] if c < NT - 1 else [])
    if k in ("kv", "mv", "avg", "q"):
        return [(k, *a[:-1], t) for t in range(NT)] if a[-1] == 0 else []
    if k == "kT":
        return [("kT", t) for t in range(NT)]
    if k == "qT":
        return [("qT", a[0], t) for t in range(NT)]
    if k == "aS":
        return [("aS", *a, j) for j in range(1 if a[0] == 0 else 2)]
    if k == "aT":
        return [("aPT", *a, kt) for kt in range(1 if a[0] == 0 else 2)]
    if k == "mif":
        return [("mi",), ("mf",)]
    if k == "mrcol":
        return [("mrcol",)]
    if k == "mA":
        return [("Mb", 0)] + [("KQ", 0, s) for s in range(NT)]
    if k == "mB":
        h = a[0]
        if h + 1 == M_HEADS:
            return [("En", h)]
        return [("Mb", h + 1)] + [("KQ", h + 1, s) for s in range(NT - 1)] + [("En", h), ("KQ", h + 1, NT - 1)]
    if k == "mnorm":
        return [("mss", h) for h in range(M_HEADS)]
    if k == "cmp2":
        return [("ckT",), ("cv",)]
    if k == "nS":
        return [("nS", *a, r) for r in range(1 if a[2] == "c" else 4)]
    if k == "nT":
        return [("nPT", *a, kt) for kt in range(1 if a[2] == "c" else a[0] + 1)]
    return []


JOBS = [j for s in STEPS for j in jobs_of(s)]
JOBNO = {j: i for i, j in enumerate(JOBS)}


def accs_of(step):
    k, a = step[0], step[1:]
    if k == "cmpq" and a[1] == 0:
        return [("chid", a[0])]
    if k == "aV" and a[1] % 2 == 0:
        return [("aO", a[0], a[1] // 2)]
    if k == "mB":
        return [("num", a[0]), ("den", a[0])]
    if k == "nV" and a[1:] == (0, "c"):
        return [("nO", a[0])]
    return []


ACCS = [j for s in STEPS for j in accs_of(s)]
ACCNO = {j: i for i, j in enumerate(ACCS)}


def blocks_of(step):
    k, a = step[0], step[1:]
    if k == "proj":
        g, i = a
        t = [("ssm_in", 32 + g), ("ssm_in", 36 + g)] + [("ssm_in", 16 + GT * g + m) for m in range(GT)]
        t += [("ssm_in", GT * g + m) for m in range(GT)]
        return [(*t[i], 0)]
    if k == "pp":
        return [("ple_proj", a[0], a[1] // 4)] if a[1] % 4 == 0 else []
    if k == "psp":
        return [("p", a[0])]
    if k == "out":
        return [({3: "attn_out", 5: "w_out"}[a[0]], a[1], 0)]
    if k in ("sout", "dn"):
        return [(k, a[0], a[1] // 2)] if a[1] % 2 == 0 else []
    if k == "dtl":
        return [("dt",)]
    if k == "ple":
        return [("ple_gate", a[0], a[1])]
    if k == "q":
        return [("attn_q", *a)]
    if k == "gate":
        return [("attn_gate", a[0], 0)]
    if k in ("kv", "mv", "avg"):
        return [step]
    if k in ("mq", "mk", "mo", "aq", "ak", "cmp_in"):
        return [(k, a[0], 0)]
    if k == "cmpq":
        return [("cmp_w1", *a)]
    if k in ("upg", "upv"):
        return [(k, a[0], 0)]
    return []


BLOCKS = [b for s in STEPS for b in blocks_of(s)]
BLKNO = {b: i for i, b in enumerate(BLOCKS)}
SPLIT = [b for b in BLOCKS if b[0] not in ("cmp_w1", "p")]
SPLITNO = {b: i for i, b in enumerate(SPLIT)}


def h_update(step):
    k, a = step[0], step[1:]
    if k == "out":
        return a[0]
    if k == "sout":
        return 1 if a[0] == GROUPS - 1 else None
    if k == "dn":
        return 6 if a[0] == 3 else None
    return None


def last_uses(step):
    k, a = step[0], step[1:]
    if k in ("sout", "dn"):
        return [(k, a[0], a[1] // 2)] if a[1] % 2 else []
    if k == "pp":
        return [("ple_proj", a[0], a[1] // 4)] if a[1] % 4 == 3 else []
    return [b for b in blocks_of(step) if b in SPLITNO]


def splits_at(step):
    if step[0] == "load":
        return [(b, SPLITNO[b]) for b in SPLIT[:NSET]]
    res = [(b, None) for b in blocks_of(step) if b[0] == "p"]
    for b in last_uses(step):
        n = SPLITNO[b] + NSET
        if n < len(SPLIT):
            res.append((SPLIT[n], n))
    return res


class Events:

    def __init__(self, nc, ctx, known):
        self.nc, self.ctx, self.known = nc, ctx, known
        self.sems, self.count, self.seen = {}, {}, {}

    def sem(self, name):
        if name not in self.sems:
            self.sems[name] = self.ctx.enter_context(self.nc.semaphore(name))
            self.count[name] = 0
        return self.sems[name]

    def done(self, name, *events, inc=1):
        s = self.sem(name)
        self.count[name] += inc
        for e in events:
            assert e not in self.seen, e
            self.seen[e] = (name, self.count[name])
        return s, inc

    def at(self, *event):
        if self.known is None:
            return self.sem("first_pass"), 1
        name, value = self.known[event]
        return self.sem(name), value


def build(nc, ins, out, known):
    ctx = ExitStack()
    with ctx:
        ev = Events(nc, ctx, known)
        done, at = ev.done, ev.at

        def sb(name, shape, dt=F32):
            return ctx.enter_context(nc.sbuf_tensor(name, shape, dt))

        h = sb("h", [P, KD, SEQ])
        hnh, hnl = sb("hnh", [P, KD, SEQ], F32R), sb("hnl", [P, KD, SEQ], F32R)
        xgh, xgl = sb("xgh", [P, KD, SEQ], F32R), sb("xgl", [P, KD, SEQ], F32R)
        wsh = [sb(f"wsh{i}", [P, BLK], F32R) for i in range(NSET)]
        wsl = [sb(f"wsl{i}", [P, BLK], F32R) for i in range(NSET)]
        ring = sb("ring", [P, NSLOT, BLK])
        con = sb("con", [P, NCON])
        vec = sb("vec", [P, NV])
        rowb = sb("rowb", [P, NR])
        w2c = sb("w2c", [P, 2, HD])
        peT = sb("peT", [P, 2, CMP_BLOCK])
        mbias = sb("mbias", [4, 2])
        pos = sb("pos", [P, NT], I32)
        eps = sb("eps", [P, 1])
        halfpi = sb("halfpi", [P, 1])
        sq = sb("sq", [P, 3, SEQ])
        ssacc = sb("ssacc", [P, SEQ])
        rt = sb("rt", [P, SEQ])
        NAR = 40
        arena = sb("arena", [P, NAR * SEQ])
        bank = [ctx.enter_context(nc.psum_tensor(f"bank{i}", [P, SEQ], F32)) for i in range(8)]

        def ar(unit, *dims):
            n = int(np.prod(dims))
            lo = int(unit * SEQ)
            assert lo + n <= NAR * SEQ
            v = arena[:, lo:lo + n]
            if len(dims) == 2:
                v = v.rearrange("p (a b) -> p a b", a=dims[0])
            if len(dims) == 3:
                v = v.rearrange("p (a b c) -> p a b c", a=dims[0], b=dims[1])
            return v

        ident, tri, upper, ones = (con[:, c:c + P] for c in (C_ID, C_T, C_U, C_ONE))
        swa = con[:, C_SWA:C_SWA + 256]
        rowvalid = con[:, C_RV:C_RV + 1]

        def ps(job):
            return bank[JOBNO[job] % NROT]

        def acc(job):
            return bank[NROT + ACCNO[job] % 2]

        def tok(t):
            return slice(t * P, (t + 1) * P)

        def over(ap, n, axis):
            a = ap.unsqueeze(axis)
            return a.broadcast_to([n if i == axis else d for i, d in enumerate(a.shape)])

        xs = [ar(8 * b, GT, SEQ) for b in range(2)]
        bcT = [ar(8 * b + 4, 2, SEQ) for b in range(2)]
        cva = [ar(6 + b, SEQ) for b in range(2)]
        btok = ar(14, NT, P)
        cbm = ar(15, NT, P)
        zs = ar(16, GT, SEQ)
        xdt = [ar(20 + b, HPG, HD) for b in range(2)]
        xde = [ar(22 + b, HPG, HD) for b in range(2)]
        dtf = ar(24, SEQ)[0:HEADS]
        dat = ar(24, HPG, P)
        dec = [ar(26 + 2 * b, HPG, P) for b in range(2)]
        ytok = ar(30, NT, SEQ)
        prev = [ar(34 + b, HPG, HD) for b in range(2)]
        yoe = ar(36, HPG, HD)
        ysq = ar(37, SEQ)
        yac = ar(38, SEQ)
        dtb = ar(39, NT, HEADS)
        da = ar(39.25, NT, HEADS)
        dtmp = ar(39.5, NT, HEADS)
        dtmp2 = ar(39.75, NT, HEADS)
        cums = sb("cums", [P, 3, NT * HEADS])
        aneg = sb("aneg", [P, HEADS])

        pp = [ar(0, KD, SEQ), ar(4, KD, SEQ), ar(8, KD, SEQ)]
        gsig = [ar(16 + b, SEQ) for b in range(2)]
        hf = [ar(20 + b, SEQ) for b in range(4)]
        hf2 = [ar(35 + b, SEQ) for b in range(4)]

        vtok = ar(0, NT, 256)
        kT = ar(2, 2, SEQ)
        qT = ar(4, KD, SEQ)
        qr = ar(12, NT, 1024)
        kr = ar(20, NT, 256)
        ctab = ar(22, 4, 256)
        rtmp = ar(24, 8, P)
        qsq = [ar(26 + b, SEQ) for b in range(2)]
        qn = [ar(28 + b, SEQ) for b in range(2)]
        ra = [ar(30 + b, SEQ) for b in range(2)]
        rb = [ar(24 + b, SEQ) for b in range(2)]
        PTb = [ar(20 + 2 * b, 2, SEQ) for b in range(2)]
        gs = ar(32, KD, SEQ)
        Sb = [ar(12 + 2 * b, 4, 256) for b in range(3)]
        ogf = [ar(18 + b, 4, P) for b in range(2)]
        small = sb("small", [P, 12, 16])
        flat = small[:, :, :].rearrange("p a b -> p (a b)")
        tiny = sb("tiny", [P, 1])
        negsink = sb("negsink", [P, ATT_HEADS])

        mqT = ar(0, 4, SEQ)
        moT = ar(4, 4, SEQ)
        mkT = ar(8, 4, SEQ)
        mvt = ar(12, NT, SEQ)
        aqT = ar(16, 4, SEQ)
        akT = ar(20, 2, SEQ)
        avt = ar(22, NT, 256)
        ckv = ar(24, 2, SEQ)
        chid = ar(24, 2, 64)
        ctm = ar(24.25, 3, 64)
        vct = ar(24.75, 2, HD)[0:NC_BLK]
        scb = [ar(25 + b / 4, 4, NC_BLK) for b in range(2)]
        kcT = ar(25.5, NC_BLK)
        cblk = [ar(26 + 4 * b, CMP_BLOCK, 2 * NC_BLK) for b in range(2)]
        wt = [ar(26 + b, SEQ) for b in range(2)]
        wk = [ar(28 + b, SEQ) for b in range(2)]
        Mneg = [ar(30, SEQ), ar(36, SEQ)]
        hm = ar(31, 4, SEQ)
        mtmp = ar(35, SEQ)
        sel = ar(37, 4, P)
        cmpbf = ar(38, NCMP)
        cmpb = cmpbf.rearrange("p (n h c) -> p n h c", n=NT, h=A_HEADS)
        alibi = ar(8, A_HEADS, SEQ)
        nSb = [ar(26, 4, SEQ), ar(0, 4, SEQ)]
        nPb = [ar(b, SEQ) for b in (30, 35, 36, 37)]
        mrow = [sq[0:4, 0, :], sq[0:4, 1, :], sq[0:4, 2, :], ssacc[0:4, :], rt[0:4, :]]
        gat = sb("gat", [P, NT, 24])
        gif = sb("gif", [P, NT, 8])
        rcol = sb("rcol", [P, NT, 4])
        fca = [ar(22 + b, SEQ) for b in range(2)]
        fsl = [ar(24 + b, SEQ) for b in range(2)]
        res = ar(0, KD, SEQ)

        block = ctx.enter_context(nc.Block())

        @block.sync
        def _(sp):
            for m in range(0, KD, 2):
                sp.dma_start(h[:, m, :], ins["xT"][m]).then_inc(*done(f"xin{m}", ("h", 0, m), inc=16))
            for L, b in enumerate(BLOCKS):
                if L >= NSLOT:
                    sp.wait_ge(*at("slot_free", L - NSLOT))
                sp.dma_start(ring[:, L % NSLOT, :], ins["wstream"][L]).then_inc(*done(f"loaded{L % NSLOT}", ("loaded", L), inc=16))
            for m in range(KD):
                sp.wait_ge(*at("result", m))
                sp.dma_start(out[m], res[:, m, :]).then_inc(*done("stored", ("stored", m), inc=16))
            sp.wait_ge(*at("stored", KD - 1))

        @block.gpsimd
        def _(pool):
            nc.gpsimd.memset(eps[:, :], EPS)
            nc.gpsimd.memset(halfpi[:, :], float(np.pi / 2)).then_inc(*done("eps_set", ("eps",)))

            def low(dst, src, hi):
                return nc.gpsimd.tensor_tensor(dst, src, hi.bitcast(F32), ALU.subtract)

            for step in STEPS:
                k, a = step[0], step[1:]
                for b, n in splits_at(step):
                    L = BLKNO[b]
                    src = ring[:, L % NSLOT, :]
                    pool.wait_ge(*at("high", L))
                    if n is None:
                        low(hnl[:, 6:8, :], src.rearrange("p (a b) -> p a b", a=2), hnh[:, 6:8, :])\
                            .then_inc(*done("split", ("split", L), ("slot_free", L)))
                    else:
                        low(wsl[n % NSET][:, :], src, wsh[n % NSET][:, :])\
                            .then_inc(*done("split", ("split", L), ("slot_free", L)))
                if k == "hn2" or k == "norm" and a[0] < 7:
                    for name in NORM_OF[a[0]] if a else ["attn"]:
                        hi, lo = (xgh, xgl) if name == "kv" else (hnh, hnl)
                        buf = hf2 if name == "ssm" else hf
                        for m in range(1, KD, 2):
                            pool.wait_ge(*at("hnhi", name, m))
                            low(lo[:, m, :], buf[m % 4], hi[:, m, :]).then_inc(*done("hn", ("hn", name, m)))
                if k == "gn":
                    g = a[0]
                    for m in range(1, GT, 2):
                        pool.wait_ge(*at("ynhi", g, m))
                        low(xgl[:, GT * (g % 2) + m, :], xs[g % 2][:, m, :], xgh[:, GT * (g % 2) + m, :]).then_inc(*done("yn", ("yn", g, m)))
                if k == "aO":
                    n, G2 = a[0], a[1] // 2
                    pool.wait_ge(*at("oghi", n, G2))
                    low(xgl[:, 4 * G2:4 * G2 + 4, tok(n)], ogf[G2], xgh[:, 4 * G2:4 * G2 + 4, tok(n)])\
                        .then_inc(*done("og", ("og", n, G2)))
                if k == "fh":
                    m = a[0]
                    pool.wait_ge(*at("ffhi", m))
                    low(xgl[:, m % 8, :], fsl[m % 2], xgh[:, m % 8, :]).then_inc(*done("ff", ("ff", m)))

                def masked(n):
                    g, c = divmod(n, NT)
                    if n >= 1:
                        pool.wait_ge(*at("mm", "seg", (n - 1) // NT, (n - 1) % NT, 1))
                    nc.gpsimd.tensor_tensor(dat, over(tri, HPG, 1),
                                            over(da[:, c, g * HPG:(g + 1) * HPG], P, 2), ALU.mult)\
                        .then_inc(*done("dat", ("dat", g, c)))

                if k == "cum":
                    pool.wait_ge(*at("consts"))
                    pool.wait_ge(*at("da"))
                    masked(0)
                if k == "ssd1":
                    g, c = a
                    pool.wait_ge(*at("xdt", g, c))
                    pool.wait_ge(*at("cums"))
                    if c < NT - 1:
                        nc.gpsimd.tensor_tensor(xde[c % 2], xdt[c % 2],
                                                over(cums[:, 1, c * HEADS + g * HPG:c * HEADS + (g + 1) * HPG], HD, 2),
                                                ALU.mult).then_inc(*done("xde", ("xde", g, c)))
                    if g * NT + c + 1 < GROUPS * NT:
                        masked(g * NT + c + 1)
                if k == "ssd2":
                    g, c = a
                    if 1 <= c < NT - 1:
                        pool.wait_ge(*at("prev", g, c))
                        nc.gpsimd.tensor_tensor(prev[(c + 1) % 2], prev[c % 2],
                                                over(cums[:, 2, c * HEADS + g * HPG:c * HEADS + (g + 1) * HPG], HD, 2),
                                                ALU.mult).then_inc(*done("pdec", ("pdec", g, c)))
                if k == "yt":
                    g, m = a
                    pool.wait_ge(*at("yskip", g, m))
                    pool.wait_ge(*at("zs", g, m))
                    nc.gpsimd.tensor_tensor(xs[g % 2][:, m, :], xs[g % 2][:, m, :], zs[:, m, :], ALU.mult)\
                        .then_inc(*done("ygated", ("ygated", g, m)))
                if k == "norm" and a[0] == 3:
                    for j in range(2):
                        nc.gpsimd.memset(cblk[j], 0.0).then_inc(*done("czero", ("czero", j)))
                if k in ("kv", "q") and a[-1] == 3:
                    for t in range(NT):
                        key = ("kv", t) if k == "kv" else ("q", a[0], t)
                        b = t % 2
                        nh = 4 if k == "kv" else 8
                        cs = ctab[:, 0 if k == "q" else 2, :].rearrange("p (t d) -> p t d", t=NT)[:, t, :]
                        pool.wait_ge(*at("qn", *key))
                        nc.gpsimd.tensor_tensor(ra[b][:, 0:nh * HD].rearrange("p (h d) -> p h d", h=nh),
                                                qn[b][:, 0:nh * HD].rearrange("p (h d) -> p h d", h=nh),
                                                over(cs, nh, 1), ALU.mult).then_inc(*done("ropea", ("ropea", *key)))
                        pool.wait_ge(*at("ropea", *key))
                        pool.wait_ge(*at("ropeb", *key))
                        if k == "kv":
                            dst = kr[:, t, :].rearrange("p (o h d) -> p o h d", o=1, h=4)
                            v = [x[b][:, 0:256].rearrange("p (o h d) -> p o h d", o=1, h=4) for x in (ra, rb)]
                        else:
                            dst = qr[:, t, a[0] * SEQ:(a[0] + 1) * SEQ].rearrange("p (j o d) -> p o j d", o=2, j=4)
                            v = [x[b][:, :].rearrange("p (o j d) -> p o j d", o=2, j=4) for x in (ra, rb)]
                        nc.gpsimd.tensor_tensor(dst, v[0], v[1], ALU.add).then_inc(*done("roped", ("roped", *key)))
                if k == "aR":
                    n, g = a
                    u = n * KV_HEADS + g
                    w = P if n == 0 else 256
                    pool.wait_ge(*at("arec", n, g))
                    s = Sb[u % 3][:, :, 0:w]
                    nc.gpsimd.tensor_tensor(s, s, over(small[:, 4 * (u % 3) + 3, 0:4], w, 2), ALU.mult)\
                        .then_inc(*done("aprob", ("aprob", n, g)))
                if k == "mB":
                    for s in range(NT):
                        pool.wait_ge(*at("wt", a[0], s))
                        b = (a[0] * NT + s) % 2
                        nc.gpsimd.tensor_tensor(wk[b][:, 0:P], wk[b][:, 0:P], tri, ALU.mult)\
                            .then_inc(*done("wtm", ("wtm", a[0], s)))
                if k == "mnorm":
                    for h_ in range(M_HEADS):
                        pool.wait_ge(*at("mixhi", h_))
                        low(xgl[:, h_, :], hm[:, h_, :], xgh[:, h_, :]).then_inc(*done("mix", ("mix", h_)))
                if k == "nR" and a[2] != "c":
                    u = NSEQ[a]
                    w = P * (a[0] + 1)
                    pool.wait_ge(*at("nrec", *a))
                    s = nSb[u % 2][:, :, 0:w]
                    nc.gpsimd.tensor_tensor(s, s, over(small[:, 4 * "csw".index(a[2]) + 3, 0:4], w, 2), ALU.mult)\
                        .then_inc(*done("nprob", ("nprob", *a)))

        @block.scalar
        def _(act):
            for m in range(1, KD, 2):
                act.dma_start(h[:, m, :], ins["xT"][m]).then_inc(*done(f"xin{m}", ("h", 0, m), inc=16))
            for i, (dst, name) in enumerate([(con[:, :], "con"), (vec[:, :], "vec"), (rowb[:, :], "rowb"),
                                             (w2c[:, :, :], "w2c"),
                                             (peT[:, :, :], "peT"), (mbias[:, :], "mbias"), (pos[:, :], "pos")]):
                act.dma_start(dst, ins[name]).then_inc(*done("consts", *([("consts",)] if i == 6 else []), inc=16))
            chain = [0]

            def link(ins_):
                chain[0] += 1
                ins_.then_inc(*done("act_step", ("act_step", chain[0])))
                act.wait_ge(*at("act_step", chain[0]))

            def square(ver, m):
                n = KD * ver + m
                if n >= 3:
                    v, q = divmod(n - 3, KD)
                    act.wait_ge(*at("ssadd", v, max(q, 1)))
                act.wait_ge(*at("h", ver, m))
                nc.scalar.activation(sq[:, n % 3, :], h[:, m, :], ACT.Square).then_inc(*done("sq", ("sq", ver, m)))

            conv_open = []

            def silu_open():
                if conv_open:
                    g, i = conv_open.pop()
                    act.wait_ge(*at("conv", g, i))
                    if g >= 2:
                        if i < 2:
                            act.wait_ge(*at("mm", "yd", g - 2, 3))
                        else:
                            act.wait_ge(*at("yn", g - 2, i - 2))
                    dst = bcT[g % 2][:, i, :] if i < 2 else xs[g % 2][:, i - 2, :]
                    nc.scalar.activation(dst, cva[(g * 6 + i) % 2], ACT.Silu)\
                        .then_inc(*done("silu", ("xbc", g, i), ("conv_used", g * 6 + i)))

            for step in STEPS:
                k, a = step[0], step[1:]
                if k == "load":
                    for m in range(2):
                        square(0, m)
                for b, n in splits_at(step):
                    L = BLKNO[b]
                    act.wait_ge(*at("loaded", L))
                    src = ring[:, L % NSLOT, :]
                    if n is None:
                        act.wait_ge(*at("mm", *[("proj", 3, 9), ("gate", KD - 1), ("upv", FT - 1)][b[1]]))
                        nc.scalar.activation(hnh[:, 6:8, :], src.rearrange("p (a b) -> p a b", a=2), ACT.Copy)\
                            .then_inc(*done("high", ("high", L)))
                    else:
                        if n >= NSET:
                            act.wait_ge(*at("set_free", n - NSET))
                        nc.scalar.activation(wsh[n % NSET][:, :], src, ACT.Copy).then_inc(*done("high", ("high", L)))
                if k == "load":
                    for m in range(2, KD):
                        square(0, m)
                    act.wait_ge(*at("eps"))
                    act.wait_ge(*at("consts"))
                if k == "norm" and a[0] == 4:
                    act.wait_ge(*at("h", 4, KD - 1))
                    act.dma_start(cmpbf, ins["cmpb"]).then_inc(*done("cmp_in_dma", inc=16))
                    act.dma_start(sel[0:4, :, :], ins["sel"]).then_inc(*done("cmp_in_dma", ("cmpb",), inc=16))
                if k == "norm":
                    link(nc.scalar.activation(tiny[:, :], eps[:, :], ACT.Sqrt))
                    act.wait_ge(*at("mm", "ss", a[0]))
                    nc.scalar.activation(rt[:, :], ps(("ss", a[0]))[:, :], ACT.Sqrt, bias=eps[:, 0:1], scale=1.0 / D)\
                        .then_inc(*done("rms", ("rms", a[0]), ("free", "ss", a[0])))
                if k == "hn2" or k == "norm" and a[0] < 7:
                    for name in NORM_OF[a[0]] if a else ["attn"]:
                        hi = xgh if name == "kv" else hnh
                        buf = hf2 if name == "ssm" else hf
                        for m in range(KD):
                            act.wait_ge(*at("hf", name, m))
                            if name in ("ple0", "ple1", "ple2") and m == 6:
                                act.wait_ge(*at("mm", "pp", int(name[3]), KD - 1))
                            nc.scalar.activation(hi[:, m, :], buf[m % 4], ACT.Copy).then_inc(*done("hnhi", ("hnhi", name, m)))
                if k == "proj":
                    g, i = a
                    b = ps(step)
                    act.wait_ge(*at("mm", *step))
                    if i < 6:
                        ch = [16 + g, 20 + g][i] if i < 2 else GT * g + i - 2
                        n = g * 6 + i
                        if n >= 2:
                            act.wait_ge(*at("conv_used", n - 2))
                        nc.scalar.activation(cva[n % 2], b[:, :], ACT.Identity, bias=vec[:, V_CB + ch:V_CB + ch + 1],
                                             scale=vec[:, V_CW + 3 * 24 + ch:V_CW + 3 * 24 + ch + 1])\
                            .then_inc(*done("conv0", ("conv0", g, i)))
                        silu_open()
                        conv_open.append((g, i))
                    else:
                        silu_open()
                        if g >= 1:
                            act.wait_ge(*at("ygated", g - 1, i - 6))
                        nc.scalar.activation(zs[:, i - 6, :], b[:, :], ACT.Silu)\
                            .then_inc(*done("zs", ("zs", g, i - 6), ("free", *step)))
                if k == "dtl":
                    act.wait_ge(*at("mm", "dtl"))
                    nc.scalar.activation(dtf, ps(step)[0:HEADS, :], ACT.Copy).then_inc(*done("dtf", ("dtf",), ("free", "dtl")))
                if k == "dt":
                    nc.scalar.activation(aneg[:, :], rowb[:, R_ALOG:R_ALOG + HEADS], ACT.Exp).then_inc(*done("aexp", ("aexp",)))
                    act.wait_ge(*at("dtabs"))
                    link(nc.scalar.activation(dtmp2, dtmp2, ACT.Exp))
                    nc.scalar.activation(dtmp2, dtmp2, ACT.Ln, bias=1.0).then_inc(*done("dtln", ("dtln",)))
                if k == "cum":
                    act.wait_ge(*at("mm", "cum"))
                    nc.scalar.activation(cums[:, :, :], ps(("cum",))[:, 0:3 * P].rearrange("p (a b) -> p a b", a=3), ACT.Exp)\
                        .then_inc(*done("cums", ("cums",), ("free", "cum")))
                if k == "ssd0":
                    act.wait_ge(*at("mm", "bt", *a))
                    if a[0] >= 1:
                        act.wait_ge(*at("mm", "st", a[0] - 1, 2))
                    nc.scalar.activation(btok, ps(("bt", *a))[:, :].rearrange("p (a b) -> p a b", a=NT), ACT.Copy)\
                        .then_inc(*done("btok", ("btok", *a), ("free", "bt", *a)))
                if k == "ssd1":
                    g, c = a
                    n = g * NT + c
                    for j in range(2):
                        act.wait_ge(*at("mm", "seg", g, c, j))
                        if n >= 2:
                            act.wait_ge(*at("mm", "yd", (n - 2) // NT, (n - 2) % NT))
                        nc.scalar.activation(dec[c % 2][:, 4 * j:4 * j + 4, :],
                                             ps(("seg", g, c, j))[:, :].rearrange("p (a b) -> p a b", a=4), ACT.Exp)\
                            .then_inc(*done("dec", ("dec", g, c, j), ("free", "seg", g, c, j)))
                if k == "ssd2" and a[1] == 0:
                    g, c = a
                    act.wait_ge(*at("mm", "yd", g, 0))
                    if g >= 1:
                        act.wait_ge(*at("mm", "yt", g - 1, 3))
                    nc.scalar.activation(ytok[:, 0, :], ps(("yd", g, 0))[:, :], ACT.Copy)\
                        .then_inc(*done("ytok0", ("ytok", g, 0), ("free", "yd", g, 0)))
                    act.wait_ge(*at("mm", "st", g, 0))
                    if g >= 1:
                        act.wait_ge(*at("mm", "yo", g - 1, 3))
                    nc.scalar.activation(prev[1], ps(("st", g, 0))[:, :].rearrange("p (a b) -> p a b", a=HPG), ACT.Copy)\
                        .then_inc(*done("prev1", ("prev", g, 1), ("free", "st", g, 0)))
                if k == "yt":
                    g, m = a
                    act.wait_ge(*at("ygated", g, m))
                    if (g, m) != (0, 0):
                        act.wait_ge(*at("yadd", *((g, m - 1) if m else (g - 1, 3))))
                    nc.scalar.activation(ysq if m else yac, xs[g % 2][:, m, :], ACT.Square)\
                        .then_inc(*done("ysq", ("ysq", g, m)))
                if k == "gn":
                    g = a[0]
                    act.wait_ge(*at("mm", "gn", g))
                    nc.scalar.activation(ysq, ps(step)[:, :], ACT.Sqrt, bias=eps[:, 0:1], scale=1.0 / 512)\
                        .then_inc(*done("grms", ("grms", g), ("free", *step)))
                    if g >= 2:
                        act.wait_ge(*at("mm", "sout", g - 2, KD - 1))
                    for m in range(GT):
                        act.wait_ge(*at("ynf", g, m))
                        nc.scalar.activation(xgh[:, GT * (g % 2) + m, :], xs[g % 2][:, m, :], ACT.Copy).then_inc(*done("ynhi", ("ynhi", g, m)))
                if k == "pp":
                    i, m = a
                    act.wait_ge(*at("mm", *step))
                    if i == 0 and m == 0:
                        act.wait_ge(*at("yn", 2, 3))
                    nc.scalar.activation(pp[i][:, m, :], ps(step)[:, :], ACT.Copy)\
                        .then_inc(*done("pp", ("pp", i, m), ("free", *step)))
                if h_update(step):
                    square(h_update(step), a[1])
                if k == "ple":
                    i, m = a
                    act.wait_ge(*at("mm", *step))
                    if m >= 2:
                        act.wait_ge(*at("h", 2 * i + 2 if i < 2 else 7, m - 2))
                    nc.scalar.activation(gsig[m % 2], ps(step)[:, :], ACT.Sigmoid)\
                        .then_inc(*done("gsig", ("gsig", i, m), ("free", *step)))
                    if m:
                        square(2 * i + 2 if i < 2 else 7, m - 1)
                    if m == KD - 1:
                        square(2 * i + 2 if i < 2 else 7, m)
                if k == "rope_tables":
                    act.wait_ge(*at("angles"))
                    nc.scalar.activation(rtmp[:, 4, :], rtmp[:, 2, :], ACT.Sin).then_inc(*done("sincos", ("sin",)))
                    nc.scalar.activation(rtmp[:, 5, :], rtmp[:, 3, :], ACT.Sin, scale=-1.0, bias=halfpi[:, 0:1])\
                        .then_inc(*done("sincos", ("cos",)))
                if k in ("kv", "q") and a[-1] == 3:
                    w = 256 if k == "kv" else 512
                    stage = 0 if k == "kv" else 1 + a[0]
                    for t in range(NT):
                        key = (k, *a[:-1], t)
                        act.wait_ge(*at("mm", *key))
                        n = stage * NT + t
                        if n >= 2:
                            act.wait_ge(*at("qss", n - 2))
                        if k == "kv":
                            nc.scalar.activation(vtok[:, t, :], ps(key)[:, 256:512], ACT.Copy)
                        nc.scalar.activation(qsq[t % 2][:, 0:w], ps(key)[:, 0:w], ACT.Square)\
                            .then_inc(*done("qsq", ("qsq", *key)))
                    act.wait_ge(*at("qss", stage * NT + NT - 1))
                    lo, nh = 96 * (stage % 2), NT * w // HD
                    nc.scalar.activation(flat[:, lo + 32:lo + 32 + nh], flat[:, lo:lo + nh], ACT.Sqrt,
                                         bias=eps[:, 0:1], scale=1.0 / HD).then_inc(*done("qrms", ("qrms", stage)))
                if k == "kT":
                    for t in range(NT):
                        act.wait_ge(*at("mm", "kT", t))
                        nc.scalar.activation(kT[:, :, tok(t)], ps(("kT", t))[:, 0:256].rearrange("p (a b) -> p a b", a=2),
                                             ACT.Copy).then_inc(*done("kT", ("kT", t), ("free", "kT", t)))
                if k == "qT":
                    for t in range(NT):
                        key = ("qT", a[0], t)
                        act.wait_ge(*at("mm", *key))
                        nc.scalar.activation(qT[:, 4 * a[0]:4 * a[0] + 4, tok(t)],
                                             ps(key)[:, :].rearrange("p (a b) -> p a b", a=4), ACT.Copy,
                                             scale=HD ** -0.5).then_inc(*done("qT", key, ("free", *key)))
                if k == "gate":
                    act.wait_ge(*at("mm", *step))
                    nc.scalar.activation(gs[:, a[0], :], ps(step)[:, :], ACT.Silu)\
                        .then_inc(*done("gs", ("gs", a[0]), ("free", *step)))
                if k == "aE":
                    n, g = a
                    u = n * KV_HEADS + g
                    w = P if n == 0 else 256
                    act.wait_ge(*at("anegm", n, g))
                    sm = small[:, 4 * (u % 3):4 * (u % 3) + 4, :]
                    for r in range(4):
                        last = nc.scalar.activation(Sb[u % 3][:, r, 0:w], Sb[u % 3][:, r, 0:w], ACT.Exp,
                                                    bias=sm[:, 1, r:r + 1], accum_out=sm[:, 2, r:r + 1])
                    last.then_inc(*done("aexpd", ("aexpd", n, g)))
                    nc.scalar.activation(sm[:, 1, 8:12], sm[:, 1, 4:8], ACT.Exp).then_inc(*done("aexpd", ("aesink", n, g)))
                if k == "aT":
                    n, g = a
                    u = n * KV_HEADS + g
                    act.wait_ge(*at("mm", "aPT", n, g, 0))
                    if u >= 2:
                        act.wait_ge(*at("pv", *divmod(u - 2, KV_HEADS)))
                    nc.scalar.activation(PTb[u % 2][:, 0, :], ps(("aPT", n, g, 0))[:, :], ACT.Copy)\
                        .then_inc(*done("aPT_act", ("aPT", n, g, 0), ("free", "aPT", n, g, 0)))
                if k == "aO":
                    n, G2 = a[0], a[1] // 2
                    act.wait_ge(*at("ogf", n, G2))
                    nc.scalar.activation(xgh[:, 4 * G2:4 * G2 + 4, tok(n)], ogf[G2], ACT.Copy)\
                        .then_inc(*done("oghi", ("oghi", n, G2)))
                if k == "mrow":
                    act.wait_ge(*at("mfabs"))
                    link(nc.scalar.activation(mrow[2], mrow[2], ACT.Exp))
                    nc.scalar.activation(mrow[2], mrow[2], ACT.Ln, bias=1.0)\
                        .then_inc(*done("mfln", ("mfln",)))
                    act.wait_ge(*at("mmt"))
                    nc.scalar.activation(mrow[4], mrow[2], ACT.Exp, scale=-1.0)\
                        .then_inc(*done("mexp", ("men",)))
                if k == "mrcol":
                    act.wait_ge(*at("mm", "mrcol"))
                    nc.scalar.activation(rcol[:, :, :], ps(("mrcol",))[:, 0:16].rearrange("p (a b) -> p a b", a=4), ACT.Copy)\
                        .then_inc(*done("rcol", ("rcol",), ("free", "mrcol")))
                if k in ("mv", "avg") and a[0] == 3:
                    for t in range(NT):
                        act.wait_ge(*at("mm", k, t))
                        if k == "mv":
                            nc.scalar.activation(mvt[:, t, :], ps((k, t))[:, :], ACT.Copy)\
                                .then_inc(*done("mv", ("mv", t), ("free", k, t)))
                        else:
                            nc.scalar.activation(avt[:, t, :], ps((k, t))[:, 0:256], ACT.Copy)
                            nc.scalar.activation(gif[:, t, :], ps((k, t))[:, 280:288], ACT.Copy)
                            nc.scalar.activation(gat[:, t, :], ps((k, t))[:, 256:280], ACT.Sigmoid)\
                                .then_inc(*done("avg", ("avg", t), ("free", k, t)))
                if k in ("mq", "mk", "aq", "ak", "cmp_in", "mo"):
                    act.wait_ge(*at("mm", *step))
                    dst = {"mq": mqT, "mk": mkT, "aq": aqT, "ak": akT, "cmp_in": ckv, "mo": moT}[k][:, a[0], :]
                    f, s = (ACT.Sigmoid, 1.0) if k == "mo" else (ACT.Copy, {"mq": P ** -0.5, "aq": HD ** -0.5}.get(k, 1.0))
                    nc.scalar.activation(dst, ps(step)[:, :], f, scale=s).then_inc(*done(k, ("done", *step), ("free", *step)))
                if k == "cmp":
                    act.wait_ge(*at("gelu_in", a[0]))
                    nc.scalar.activation(ctm[:, 1, :], ctm[:, 1, :], ACT.Tanh, scale=float(np.sqrt(2 / np.pi)))\
                        .then_inc(*done("ctanh", ("ctanh", a[0])))
                if k == "cmp2":
                    act.wait_ge(*at("mm", "ckT"))
                    nc.scalar.activation(kcT[:, :], ps(("ckT",))[:, 0:NC_BLK], ACT.Copy).then_inc(*done("kcT", ("kcT",), ("free", "ckT")))
                    act.wait_ge(*at("mm", "cv"))
                    nc.scalar.activation(vct[:, :, :], ps(("cv",))[0:NC_BLK, 0:128].rearrange("p (a b) -> p a b", a=2), ACT.Copy)\
                        .then_inc(*done("vct", ("vct",), ("free", "cv")))

                def negated(h_):
                    act.wait_ge(*at("mm", "Mb", h_))
                    if h_ >= 2:
                        act.wait_ge(*at("marg", h_ - 2, NT - 1))
                    nc.scalar.activation(Mneg[h_ % 2], ps(("Mb", h_))[:, :], ACT.Copy, scale=-1.0)\
                        .then_inc(*done("Mneg", ("Mneg", h_), ("free", "Mb", h_)))

                def mexp(n):
                    h_, s = divmod(n, NT)
                    if h_ < M_HEADS:
                        act.wait_ge(*at("marg", h_, s))
                        nc.scalar.activation(wt[n % 2][:, 0:SEQ - P * s], wt[n % 2][:, 0:SEQ - P * s], ACT.Exp)\
                            .then_inc(*done("mexpd", ("mexpd", h_, s)))

                if k == "mA":
                    negated(0)
                    mexp(0)
                if k == "mB":
                    h_ = a[0]
                    if h_ + 1 < M_HEADS:
                        negated(h_ + 1)
                    for s in range(NT):
                        mexp(h_ * NT + s + 1)
                    if h_ == M_HEADS - 1:
                        act.wait_ge(*at("mm", "KQ", h_, NT - 1))
                        act.dma_start(alibi[:, 0:4, :], ins["alibi"][:, 0:4, :]).then_inc(*done("alibi_in0", ("alibi", 0), inc=16))
                    act.wait_ge(*at("mden", h_))
                    if h_ == M_HEADS - 1:
                        act.dma_start(alibi[:, 4:8, :], ins["alibi"][:, 4:8, :]).then_inc(*done("alibi_in1", ("alibi", 1), inc=16))
                    if h_:
                        act.wait_ge(*at("hm", h_ - 1))
                    nc.scalar.activation(mtmp, acc(("den", h_))[:, :], ACT.Abs)\
                        .then_inc(*done("mabs", ("mabs", h_), ("accfree", "den", h_)))
                if k == "mnorm":
                    for h_ in range(M_HEADS):
                        act.wait_ge(*at("hm", h_))
                        nc.scalar.activation(mqT[:, h_, :], hm[:, h_, :], ACT.Square).then_inc(*done("msq", ("msq", h_)))
                    for h_ in range(M_HEADS):
                        act.wait_ge(*at("mm", "mss", h_))
                        nc.scalar.activation(mqT[:, h_, :], ps(("mss", h_))[:, :], ACT.Sqrt, bias=eps[:, 0:1], scale=1.0 / P)\
                            .then_inc(*done("mrms", ("mrms", h_), ("free", "mss", h_)))
                    for h_ in range(M_HEADS):
                        act.wait_ge(*at("mgated", h_))
                        nc.scalar.activation(xgh[:, h_, :], hm[:, h_, :], ACT.Copy).then_inc(*done("mixhi", ("mixhi", h_)))
                if k == "nE":
                    i, g, br = a
                    u = NSEQ[a]
                    act.wait_ge(*at("nnegm", *a))
                    q = 4 * "csw".index(br)
                    sm = small[:, q:q + 4, :]
                    if br == "c":
                        nc.scalar.activation(scb[g][:, :, :], scb[g][:, :, :], ACT.Exp).then_inc(*done("nexp", ("nexp", *a)))
                    else:
                        w = P * (i + 1)
                        for r in range(4):
                            last = nc.scalar.activation(nSb[u % 2][:, r, 0:w], nSb[u % 2][:, r, 0:w], ACT.Exp,
                                                        bias=sm[:, 1, r:r + 1], accum_out=sm[:, 2, r:r + 1])
                        last.then_inc(*done("nexp", ("nexp", *a)))
                if k == "nT":
                    for kt in range(1 if a[2] == "c" else a[0] + 1):
                        n = NPT[(*a, kt)]
                        if n % 2 == 0:
                            act.wait_ge(*at("mm", "nPT", *a, kt))
                            if n >= 4:
                                act.wait_ge(*at("npv", n - 4))
                            rows = NC_BLK if a[2] == "c" else P
                            nc.scalar.activation(nPb[n % 4][0:rows, :], ps(("nPT", *a, kt))[0:rows, :], ACT.Copy)\
                                .then_inc(*done("nPT_act", ("nPT", *a, kt), ("free", "nPT", *a, kt)))
                if k == "nO":
                    act.wait_ge(*at("nO", a[0]))
                    nc.scalar.activation(xgh[:, 4:8, tok(a[0])], acc(("nO", a[0]))[:, :].rearrange("p (a b) -> p a b", a=4),
                                         ACT.Copy).then_inc(*done("noghi", ("noghi", a[0])))
                if k == "upg":
                    m = a[0]
                    act.wait_ge(*at("mm", "upg", m))
                    if m >= 2:
                        act.wait_ge(*at("fsilu", m - 2))
                    nc.scalar.activation(fca[m % 2], ps(("upg", m))[:, :], ACT.Identity, bias=vec[:, V_C2B + m:V_C2B + m + 1],
                                         scale=vec[:, V_C2W + 2 * FT + m:V_C2W + 2 * FT + m + 1])\
                        .then_inc(*done("fconv0", ("fconv0", m)))
                if k == "upv":
                    m = a[0]
                    act.wait_ge(*at("fconv", m))
                    if m >= 2:
                        act.wait_ge(*at("ff", m - 2))
                    nc.scalar.activation(fsl[m % 2], fca[m % 2], ACT.Silu).then_inc(*done("fsilu", ("fsilu", m)))
                if k == "fh":
                    m = a[0]
                    act.wait_ge(*at("fff", m))
                    if m >= 8:
                        act.wait_ge(*at("mm", "dn", m // 4 - 2, KD - 1))
                    nc.scalar.activation(xgh[:, m % 8, :], fsl[m % 2], ACT.Copy).then_inc(*done("ffhi", ("ffhi", m)))

        @block.tensor
        def _(pe):
            pe.wait_ge(*at("consts"))

            def open_bank(job):
                n = JOBNO[job]
                if n >= NROT:
                    pe.wait_ge(*at("free", *JOBS[n - NROT]))
                return ps(job)

            def open_acc(job):
                n = ACCNO[job]
                if n >= 2:
                    pe.wait_ge(*at("accfree", *ACCS[n - 2]))
                return acc(job)

            def weights(name):
                pe.wait_ge(*at("split", BLKNO[name]))
                n = SPLITNO[name] % NSET
                return wsh[n], wsl[n]

            def used(name, *more):
                return done("mm", ("set_free", SPLITNO[name]), *more)

            def mm(*args, **kw):
                return nc.tensor.matmul(*args, **kw)

            def mm3(o, w, x, start, stop):
                mm(o, w[0], x[0], start=start, stop=False)
                mm(o, w[0], x[1], start=False, stop=False)
                return mm(o, w[1], x[0], start=False, stop=stop)

            def linear(job, name, src, normed=None):
                b = open_bank(job)
                w = weights(name)
                for kt in range(KD):
                    if normed:
                        pe.wait_ge(*at("hn", normed, kt))
                    last = mm3(b[:, :], [q[:, tok(kt)] for q in w], [q[:, kt, :] for q in src], kt == 0, kt == KD - 1)
                last.then_inc(*used(name, ("mm", *job)))

            def quarter(job, name, src, lo, m):
                b = open_bank(job)
                w = weights(name)
                for kt in range(4):
                    last = mm3(b[:, :], [q[:, kt * 256 + (m % 2) * P:kt * 256 + (m % 2 + 1) * P] for q in w],
                               [q[:, lo + kt, :] for q in src], kt == 0, kt == 3)
                if m % 2:
                    last.then_inc(*used(name, ("mm", *job)))
                else:
                    last.then_inc(*done("mm", ("mm", *job)))

            def token_major(jobs, i, name, src, width=SEQ, normed=None):
                bs = [open_bank(j) if i == 0 else ps(j) for j in jobs]
                w = weights(name)
                for k2 in range(2):
                    if normed:
                        pe.wait_ge(*at("hn", normed, 2 * i + k2))
                    for t in range(NT):
                        fin = i == 3 and k2 == 1
                        last = mm3(bs[t][:, 0:width], [q[:, 2 * i + k2, tok(t)] for q in src],
                                   [q[:, k2 * SEQ:k2 * SEQ + width] for q in w], i + k2 == 0, fin)
                        free = k2 == 1 and t == NT - 1
                        if free:
                            last.then_inc(*used(name, *([("mm", *jobs[t])] if fin else [])))
                        elif fin:
                            last.then_inc(*done("mm", ("mm", *jobs[t])))

            hn, xg = (hnh, hnl), (xgh, xgl)
            for step in STEPS:
                k, a = step[0], step[1:]
                if k == "norm":
                    b = open_bank(("ss", a[0]))
                    pe.wait_ge(*at("ssadd", a[0], KD - 1))
                    mm(b[:, :], ones, ssacc[:, :], start=True, stop=True).then_inc(*done("mm", ("mm", "ss", a[0])))
                if k == "proj":
                    linear(step, blocks_of(step)[0], hn, "ssm" if a == (0, 0) else None)
                if k == "dtl":
                    linear(step, ("dt",), hn)
                if k == "dt":
                    b = open_bank(("dt",))
                    pe.wait_ge(*at("dtf"))
                    for t in range(NT):
                        last = nc.tensor.transpose(b[:, t * HEADS:(t + 1) * HEADS], dtf[:, tok(t)], ident[0:HEADS, 0:HEADS])
                    last.then_inc(*done("mm", ("mm", "dt")))
                if k == "cum":
                    b = open_bank(("cum",))
                    pe.wait_ge(*at("da"))
                    daf = da.rearrange("p a b -> p (a b)")
                    mm(b[:, 0:P], tri, daf, start=True, stop=True)
                    mm(b[:, P:2 * P], upper, daf, start=True, stop=True)
                    mm(b[:, 2 * P:3 * P], ones, daf, start=True, stop=True).then_inc(*done("mm", ("mm", "cum")))
                if k == "ssd0":
                    g = a[0]
                    b = open_bank(("cb", g))
                    pe.wait_ge(*at("xbc", g, 1))
                    bc = bcT[g % 2]
                    for c in range(NT):
                        last = mm(b[:, tok(c)], bc[:, 0, tok(c)], bc[:, 1, tok(c)], start=True, stop=True)
                    last.then_inc(*done("mm", ("mm", "cb", g)))
                    b = open_bank(("bt", g))
                    for c in range(NT):
                        last = nc.tensor.transpose(b[:, tok(c)], bc[:, 0, tok(c)], ident)
                    last.then_inc(*done("mm", ("mm", "bt", g)))
                if k == "ssd1":
                    g, c = a
                    b = open_bank(("xt", g, c))
                    pe.wait_ge(*at("xbc", g, 5))
                    for m in range(GT):
                        last = nc.tensor.transpose(b[:, tok(m)], xs[g % 2][:, m, tok(c)], ident)
                    last.then_inc(*done("mm", ("mm", "xt", g, c)))
                    pe.wait_ge(*at("dat", g, c))
                    for j in range(2):
                        b = open_bank(("seg", g, c, j))
                        mm(b[:, :], upper, dat[:, 4 * j:4 * j + 4, :], start=True, stop=True)\
                            .then_inc(*done("mm", ("mm", "seg", g, c, j)))
                if k == "ssd2":
                    g, c = a
                    b = open_bank(("yd", g, c))
                    pe.wait_ge(*at("decm", g, c))
                    for r in range(HPG):
                        last = mm(b[:, r * HD:(r + 1) * HD], dec[c % 2][:, r, :], xdt[c % 2][:, r, :], start=True, stop=True)
                    last.then_inc(*done("mm", ("mm", "yd", g, c)))
                    if c:
                        b = open_bank(("yo", g, c))
                        pe.wait_ge(*at("prev", g, c))
                        mm(b[:, :], bcT[g % 2][:, 1, tok(c)], prev[c % 2], start=True, stop=True)\
                            .then_inc(*done("mm", ("mm", "yo", g, c)))
                    if c < NT - 1:
                        b = open_bank(("st", g, c))
                        pe.wait_ge(*at("btok", g))
                        pe.wait_ge(*at("xde", g, c))
                        mm(b[:, :], btok[:, c, :], xde[c % 2], start=True, stop=True)\
                            .then_inc(*done("mm", ("mm", "st", g, c)))
                if k == "yt":
                    g, m = a
                    b = open_bank(step)
                    for c in range(NT):
                        pe.wait_ge(*at("ytok", g, c))
                        last = nc.tensor.transpose(b[:, tok(c)], ytok[:, c, tok(m)], ident)
                    last.then_inc(*done("mm", ("mm", *step)))
                if k == "gn":
                    b = open_bank(step)
                    pe.wait_ge(*at("yadd", a[0], 3))
                    mm(b[:, :], ones, yac, start=True, stop=True).then_inc(*done("mm", ("mm", *step)))
                if k == "pp":
                    i, m = a
                    b = open_bank(step)
                    if m == 0:
                        pe.wait_ge(*at("split", BLKNO[("p", i)]))
                    w = weights(("ple_proj", i, m // 4))
                    for kt in range(2):
                        last = mm3(b[:, :], [q[:, kt * SEQ + (m % 4) * P:kt * SEQ + (m % 4 + 1) * P] for q in w],
                                   [q[:, 6 + kt, :] for q in hn], kt == 0, kt == 1)
                    if m % 4 == 3:
                        last.then_inc(*used(("ple_proj", i, m // 4), ("mm", *step)))
                    else:
                        last.then_inc(*done("mm", ("mm", *step)))
                if k == "sout":
                    g, m = a
                    if m == 0:
                        for q in range(GT):
                            pe.wait_ge(*at("yn", g, q))
                    quarter(step, ("sout", g, m // 2), xg, GT * (g % 2), m)
                if k == "dn":
                    q, m = a
                    if m == 0:
                        pe.wait_ge(*at("ff", 4 * q + 3))
                    quarter(step, ("dn", q, m // 2), xg, 4 * (q % 2), m)
                if k == "out":
                    if a == (3, 0):
                        pe.wait_ge(*at("og", NT - 1, 1))
                    if a == (5, 0):
                        pe.wait_ge(*at("mix", 3))
                        pe.wait_ge(*at("nog", NT - 1))
                    linear(step, blocks_of(step)[0], xg)
                if k == "ple":
                    linear(step, blocks_of(step)[0], hn, ["ple0", "ple1", "ple2"][a[0]] if a[1] == 0 else None)
                if k == "kv":
                    token_major([("kv", t) for t in range(NT)], a[0], step, xg, SEQ, "kv")
                if k == "q":
                    token_major([("q", a[0], t) for t in range(NT)], a[1], blocks_of(step)[0], hn)
                if k == "kT":
                    for t in range(NT):
                        b = open_bank(("kT", t))
                        pe.wait_ge(*at("roped", "kv", t))
                        for j in range(2):
                            last = nc.tensor.transpose(b[:, tok(j)], kr[:, t, tok(j)], ident)
                        last.then_inc(*done("mm", ("mm", "kT", t)))
                if k == "qT":
                    for t in range(NT):
                        b = open_bank(("qT", a[0], t))
                        pe.wait_ge(*at("roped", "q", a[0], t))
                        for j in range(4):
                            last = nc.tensor.transpose(b[:, tok(j)], qr[:, t, a[0] * SEQ + j * P:a[0] * SEQ + (j + 1) * P], ident)
                        last.then_inc(*done("mm", ("mm", "qT", a[0], t)))
                if k == "gate":
                    linear(step, blocks_of(step)[0], hn, None if a[0] else "attn")
                if k == "aS":
                    n, g = a
                    lo = HD * (g % 2)
                    if g == 0:
                        pe.wait_ge(*at("kT", n))
                        pe.wait_ge(*at("qT", 1, n))
                    w = P if n == 0 else 256
                    keys = slice(0, P) if n == 0 else slice((n - 1) * P, (n + 1) * P)
                    per = SEQ // w
                    for j in range(4 // per):
                        b = open_bank(("aS", n, g, j))
                        for r in range(per * j, per * (j + 1)):
                            last = mm(b[:, (r % per) * w:(r % per + 1) * w], qT[lo:lo + HD, 4 * (g // 2) + r, tok(n)],
                                      kT[lo:lo + HD, g // 2, keys], start=True, stop=True)
                        last.then_inc(*done("mm", ("mm", "aS", n, g, j)))
                if k == "aT":
                    n, g = a
                    u = n * KV_HEADS + g
                    nk = 1 if n == 0 else 2
                    pe.wait_ge(*at("aprob", n, g))
                    for kt in range(nk):
                        b = open_bank(("aPT", n, g, kt))
                        for r in range(4):
                            last = nc.tensor.transpose(b[:, tok(r)], Sb[u % 3][:, r, tok(kt)], ident)
                        last.then_inc(*done("mm", ("mm", "aPT", n, g, kt)))
                if k == "aV":
                    n, g = a
                    u = n * KV_HEADS + g
                    lo = HD * (g % 2)
                    nk = 1 if n == 0 else 2
                    o = open_acc(("aO", n, g // 2)) if g % 2 == 0 else acc(("aO", n, g // 2))
                    for kt in range(nk):
                        pe.wait_ge(*at("aPT", n, g, kt))
                        last = mm(o[lo:lo + HD, :], vtok[:, n - nk + 1 + kt, g * HD:(g + 1) * HD], PTb[u % 2][:, kt, :],
                                  start=(kt == 0), stop=(kt == nk - 1))
                    last.then_inc(*done("mm", ("pv", n, g)))
                if k == "mif":
                    pe.wait_ge(*at("avg", NT - 1))
                    for j, name in enumerate(("mi", "mf")):
                        b = open_bank((name,))
                        for t in range(NT):
                            last = nc.tensor.transpose(b[0:4, tok(t)], gif[:, t, 4 * j:4 * j + 4], ident)
                        last.then_inc(*done("mm", ("mm", name)))
                if k in ("mq", "mk", "mo", "aq", "ak", "cmp_in"):
                    linear(step, blocks_of(step)[0], hn)
                if k in ("mv", "avg"):
                    token_major([(k, t) for t in range(NT)], a[0], step, hn, SEQ if k == "mv" else 288,
                                "ln1" if k == "avg" else None)
                if k == "mrcol":
                    b = open_bank(("mrcol",))
                    pe.wait_ge(*at("mrrow"))
                    for t in range(NT):
                        last = nc.tensor.transpose(b[:, 4 * t:4 * t + 4], sq[0:4, 0, tok(t)], ident[0:4, 0:4])
                    last.then_inc(*done("mm", ("mm", "mrcol")))
                if k == "cmpq":
                    j, q = a
                    b = open_acc(("chid", j)) if q == 0 else acc(("chid", j))
                    pe.wait_ge(*at("cblk", j))
                    L = BLKNO[("cmp_w1", j, q)]
                    pe.wait_ge(*at("loaded", L))
                    w = ring[:, L % NSLOT, :]
                    for l in range(8):
                        last = mm(b[:, 0:2 * NC_BLK], w[:, l * P:(l + 1) * P], cblk[j][:, 8 * q + l, :],
                                  start=(q == 0 and l == 0), stop=(q == 3 and l == 7))
                    last.then_inc(*done("mm", ("slot_free", L), *([("mm", "chid", j)] if q == 3 else [])))
                if k == "cmp2":
                    b = open_bank(("ckT",))
                    pe.wait_ge(*at("gelu", 1))
                    for g in range(2):
                        last = mm(b[HD * g:HD * (g + 1), 0:NC_BLK], w2c[:, 0, :], chid[:, 0, 32 * g:32 * g + NC_BLK],
                                  start=True, stop=True)
                    last.then_inc(*done("mm", ("mm", "ckT")))
                    b = open_bank(("cv",))
                    for g in range(2):
                        last = mm(b[0:NC_BLK, HD * g:HD * (g + 1)], chid[:, 1, 32 * g:32 * g + NC_BLK], w2c[:, 1, :],
                                  start=True, stop=True)
                    last.then_inc(*done("mm", ("mm", "cv")))

                def stab(h_):
                    mm(open_bank(("Mb", h_))[:, :], sel[0:4, h_, :], mrow[1], start=True, stop=True)\
                        .then_inc(*done("mm", ("mm", "Mb", h_)))

                def keyquery(h_, s):
                    b = open_bank(("KQ", h_, s))
                    if s == 0:
                        pe.wait_ge(*at("done", "mk", h_))
                        pe.wait_ge(*at("done", "mq", h_))
                    mm(b[:, 0:SEQ - P * s], mkT[:, h_, tok(s)], mqT[:, h_, P * s:SEQ], start=True, stop=True)\
                        .then_inc(*done("mm", ("mm", "KQ", h_, s)))

                if k == "mA":
                    pe.wait_ge(*at("cmpb"))
                    pe.wait_ge(*at("mmt"))
                    pe.wait_ge(*at("men"))
                    stab(0)
                    for s in range(NT):
                        keyquery(0, s)
                if k == "mB":
                    h_ = a[0]
                    more = h_ + 1 < M_HEADS
                    if more:
                        stab(h_ + 1)
                    num, den = open_acc(("num", h_)), open_acc(("den", h_))
                    for s in range(NT):
                        if s == NT - 1:
                            mm(open_bank(("En", h_))[:, :], sel[0:4, h_, :], mrow[4], start=True, stop=True)\
                                .then_inc(*done("mm", ("mm", "En", h_)))
                        pe.wait_ge(*at("wtm", h_, s))
                        pe.wait_ge(*at("mv", s))
                        wb = wk[(h_ * NT + s) % 2][:, 0:SEQ - P * s]
                        mm(num[:, P * s:SEQ], mvt[:, s, h_ * P:(h_ + 1) * P], wb, start=(s == 0), stop=(s == NT - 1),
                           skip_group_check=True)
                        mm(den[:, P * s:SEQ], ones, wb, start=(s == 0), stop=(s == NT - 1), skip_group_check=True)\
                            .then_inc(*done("mm", ("numden", h_, s), *([("mden", h_)] if s == NT - 1 else [])))
                        if more:
                            keyquery(h_ + 1, s)
                if k == "mnorm":
                    for h_ in range(M_HEADS):
                        b = open_bank(("mss", h_))
                        pe.wait_ge(*at("msq", h_))
                        mm(b[:, :], ones, mqT[:, h_, :], start=True, stop=True).then_inc(*done("mm", ("mm", "mss", h_)))
                if k == "nS":
                    i, g, br = a
                    lo = HD * g
                    pe.wait_ge(*at("kcT"))
                    pe.wait_ge(*at("done", "ak", 1))
                    if br == "c":
                        b = open_bank(("nS", *a, 0))
                        for r in range(4):
                            last = mm(b[:, 32 * r:32 * r + NC_BLK], aqT[lo:lo + HD, r, tok(i)], kcT[lo:lo + HD, :],
                                      start=True, stop=True)
                        last.then_inc(*done("mm", ("mm", "nS", *a, 0)))
                    else:
                        w = P * (i + 1)
                        for r in range(4):
                            b = open_bank(("nS", *a, r))
                            mm(b[:, 0:w], aqT[lo:lo + HD, r, tok(i)], akT[lo:lo + HD, "sw".index(br), 0:w],
                               start=True, stop=True).then_inc(*done("mm", ("mm", "nS", *a, r)))
                if k == "nT":
                    i, g, br = a
                    u = NSEQ[a]
                    pe.wait_ge(*at("nprob", *a))
                    for kt in range(1 if br == "c" else i + 1):
                        b = open_bank(("nPT", *a, kt))
                        for r in range(4):
                            if br == "c":
                                last = nc.tensor.transpose(b[0:NC_BLK, tok(r)], scb[g][:, r, :], ident)
                            else:
                                last = nc.tensor.transpose(b[:, tok(r)], nSb[u % 2][:, r, tok(kt)], ident)
                        last.then_inc(*done("mm", ("mm", "nPT", *a, kt)))
                if k == "nV":
                    i, g, br = a
                    lo = HD * g
                    o = open_acc(("nO", i)) if (g, br) == (0, "c") else acc(("nO", i))
                    nk = 1 if br == "c" else i + 1
                    for kt in range(nk):
                        pe.wait_ge(*at("nPT", *a, kt))
                        n = NPT[(*a, kt)]
                        if br == "c":
                            pe.wait_ge(*at("vct"))
                            last = mm(o[lo:lo + HD, :], vct[:, g, :], nPb[n % 4][0:NC_BLK, :], start=True, stop=False)
                        else:
                            v = avt[:, kt, P * "sw".index(br) + HD * g:P * "sw".index(br) + HD * (g + 1)]
                            last = mm(o[lo:lo + HD, :], v, nPb[n % 4][:, :], start=False, stop=(br == "w" and kt == nk - 1))
                        last.then_inc(*done("mm", ("npv", n), *([("nO", i)] if (g, br, kt) == (1, "w", nk - 1) else [])))
                if k in ("upg", "upv"):
                    linear(step, blocks_of(step)[0], hn, "ln2" if step == ("upg", 0) else None)

        @block.vector
        def _(dve):
            chain = [0]

            def link(ins_):
                chain[0] += 1
                ins_.then_inc(*done("dve_step", ("dve_step", chain[0])))
                dve.wait_ge(*at("dve_step", chain[0]))

            def ssadd(ver, m):
                dve.wait_ge(*at("sq", ver, m))
                n = KD * ver + m
                if m == 1:
                    nc.vector.tensor_tensor(ssacc[:, :], sq[:, (n - 1) % 3, :], sq[:, n % 3, :], ALU.add)\
                        .then_inc(*done("ssadd", ("ssadd", ver, m)))
                else:
                    dve.wait_ge(*at("ssadd", ver, m - 1))
                    nc.vector.tensor_tensor(ssacc[:, :], ssacc[:, :], sq[:, n % 3, :], ALU.add)\
                        .then_inc(*done("ssadd", ("ssadd", ver, m)))

            def low(dst, src, hi):
                return nc.vector.tensor_tensor(dst, src, hi.bitcast(F32), ALU.subtract)

            for step in STEPS:
                k, a = step[0], step[1:]
                if k == "load":
                    for m in range(1, KD):
                        ssadd(0, m)
                    dve.wait_ge(*at("consts"))
                    nc.vector.tensor_scalar(negsink[:, :], rowb[:, R_SINK:R_SINK + ATT_HEADS], -1.0, None, ALU.mult)
                if k in ("norm", "hn2"):
                    ver = a[0] if a else 2
                    if a:
                        dve.wait_ge(*at("rms", ver))
                        link(nc.vector.reciprocal(rt[:, :], rt[:, :]))
                    for name in NORM_OF[ver] if a else ["attn"]:
                        hi, lo = (xgh, xgl) if name == "kv" else (hnh, hnl)
                        buf = hf2 if name == "ssm" else hf
                        for m in range(KD):
                            if m >= 4 and ver < 7:
                                dve.wait_ge(*at("hn", name, m - 4))
                            elif name == "attn":
                                dve.wait_ge(*at("hn", "kv", KD - 4 + m))
                            dst = res[:, m, :] if ver == 7 else buf[m % 4]
                            nc.vector.scalar_tensor_tensor(dst, h[:, m, :],
                                                           vec[:, V_NORM[name] + m:V_NORM[name] + m + 1], rt[:, :],
                                                           ALU.mult, ALU.mult)\
                                .then_inc(*done("hf", ("result", m) if ver == 7 else ("hf", name, m)))
                            if ver < 7 and m % 2:
                                dve.wait_ge(*at("hnhi", name, m - 1))
                                low(lo[:, m - 1, :], buf[(m - 1) % 4], hi[:, m - 1, :])\
                                    .then_inc(*done("hn_dve", ("hn", name, m - 1)))
                if k == "proj" and a[1] < 6:
                    g, i = a
                    ch = [16 + g, 20 + g][i] if i < 2 else GT * g + i - 2
                    c = cva[(g * 6 + i) % 2]
                    b = ps(step)
                    dve.wait_ge(*at("conv0", g, i))
                    for s in range(1, TAPS):
                        w = vec[:, V_CW + (3 - s) * 24 + ch:V_CW + (3 - s) * 24 + ch + 1]
                        x = nc.vector.scalar_tensor_tensor(c[:, s:SEQ], b[:, 0:SEQ - s], w, c[:, s:SEQ], ALU.mult, ALU.add)
                        if s < TAPS - 1:
                            link(x)
                        else:
                            x.then_inc(*done("conv", ("conv", g, i), ("free", *step)))
                if k == "dt":
                    dve.wait_ge(*at("mm", "dt"))
                    b = ps(("dt",))[:, 0:P].rearrange("p (a b) -> p a b", a=NT)
                    link(nc.vector.tensor_tensor(dtmp, b, over(rowb[:, R_DTB:R_DTB + HEADS], NT, 1), ALU.add))
                    nc.vector.scalar_tensor_tensor(dtmp2, dtmp, -1.0, dtmp, ALU.mult, ALU.min)\
                        .then_inc(*done("dtabs", ("dtabs",), ("free", "dt")))
                    dve.wait_ge(*at("dtln"))
                    link(nc.vector.scalar_tensor_tensor(dtb, dtmp, 0.0, dtmp2, ALU.max, ALU.add))
                    dve.wait_ge(*at("aexp"))
                    link(nc.vector.tensor_tensor(da, dtb, over(aneg[:, :], NT, 1), ALU.mult))
                    nc.vector.tensor_scalar(da, da, -1.0, None, ALU.mult).then_inc(*done("da", ("da",)))
                if k == "ssd0":
                    g = a[0]
                    dve.wait_ge(*at("mm", "cb", g))
                    nc.vector.tensor_tensor(cbm, ps(("cb", g))[:, :].rearrange("p (a b) -> p a b", a=NT), over(tri, NT, 1),
                                            ALU.mult).then_inc(*done("cbm", ("cbm", g), ("free", "cb", g)))
                if k == "ssd1":
                    g, c = a
                    n = g * NT + c
                    dve.wait_ge(*at("mm", "xt", g, c))
                    if n >= 2:
                        q = ((n - 2) // NT, (n - 2) % NT)
                        dve.wait_ge(*at("mm", "yd", *q))
                        if q[1] < NT - 1:
                            dve.wait_ge(*at("xde", *q))
                    nc.vector.tensor_tensor(xdt[c % 2], ps(("xt", g, c))[:, :].rearrange("p (a b) -> p a b", a=HPG),
                                            over(dtb[:, c, g * HPG:(g + 1) * HPG], HD, 2), ALU.mult)\
                        .then_inc(*done("xdt", ("xdt", g, c), ("free", "xt", g, c)))
                    dve.wait_ge(*at("dec", g, c, 1))
                    dve.wait_ge(*at("cbm", g))
                    nc.vector.tensor_tensor(dec[c % 2], dec[c % 2], over(cbm[:, c, :], HPG, 1), ALU.mult)\
                        .then_inc(*done("decm", ("decm", g, c)))
                if k == "ssd2":
                    g, c = a
                    if c:
                        dve.wait_ge(*at("mm", "yo", g, c))
                        dve.wait_ge(*at("cums"))
                        link(nc.vector.tensor_tensor(yoe, ps(("yo", g, c))[:, :].rearrange("p (a b) -> p a b", a=HPG),
                                                     over(cums[:, 0, c * HEADS + g * HPG:c * HEADS + (g + 1) * HPG], HD, 2),
                                                     ALU.mult))
                        if g >= 1:
                            dve.wait_ge(*at("mm", "yt", g - 1, 3))
                        nc.vector.tensor_tensor(ytok[:, c, :].rearrange("p (a b) -> p a b", a=HPG), yoe,
                                                ps(("yd", g, c))[:, :].rearrange("p (a b) -> p a b", a=HPG), ALU.add)\
                            .then_inc(*done("ytok", ("ytok", g, c), ("free", "yd", g, c), ("free", "yo", g, c)))
                    if 1 <= c < NT - 1:
                        dve.wait_ge(*at("mm", "st", g, c))
                        dve.wait_ge(*at("pdec", g, c))
                        pn = prev[(c + 1) % 2]
                        nc.vector.tensor_tensor(pn, pn, ps(("st", g, c))[:, :].rearrange("p (a b) -> p a b", a=HPG), ALU.add)\
                            .then_inc(*done("prev", ("prev", g, c + 1), ("free", "st", g, c)))
                if k == "yt":
                    g, m = a
                    ti = GT * g + m
                    dve.wait_ge(*at("mm", *step))
                    nc.vector.scalar_tensor_tensor(xs[g % 2][:, m, :], xs[g % 2][:, m, :], vec[:, V_D + ti:V_D + ti + 1], ps(step)[:, :],
                                                   ALU.mult, ALU.add).then_inc(*done("yskip", ("yskip", g, m), ("free", *step)))
                    if m == 0:
                        dve.wait_ge(*at("ysq", g, 0))
                        nc.vector.tensor_copy(yoe[:, 0, 0:1], yac[:, 0:1]).then_inc(*done("yadd", ("yadd", g, 0)))
                    else:
                        dve.wait_ge(*at("ysq", g, m))
                        dve.wait_ge(*at("yadd", g, m - 1))
                        nc.vector.tensor_tensor(yac, yac, ysq, ALU.add).then_inc(*done("yadd", ("yadd", g, m)))
                if k == "gn":
                    g = a[0]
                    dve.wait_ge(*at("grms", g))
                    link(nc.vector.reciprocal(ysq, ysq))
                    for m in range(GT):
                        ti = GT * g + m
                        nc.vector.scalar_tensor_tensor(xs[g % 2][:, m, :], xs[g % 2][:, m, :], vec[:, V_GN + ti:V_GN + ti + 1],
                                                       ysq, ALU.mult, ALU.mult).then_inc(*done("ynf", ("ynf", g, m)))
                        if m >= 2:
                            q = 2 * (m - 2)
                            dve.wait_ge(*at("ynhi", g, q))
                            x = GT * (g % 2) + q
                            low(xgl[:, x, :], xs[g % 2][:, q, :], xgh[:, x, :]).then_inc(*done("yn_dve", ("yn", g, q)))
                if k in ("sout", "dn") and a[0] < 3:
                    m = a[1]
                    dve.wait_ge(*at("mm", *step))
                    if a[0]:
                        dve.wait_ge(*at("hadd", k, a[0] - 1, m))
                    nc.vector.tensor_tensor(h[:, m, :], h[:, m, :], ps(step)[:, :], ALU.add)\
                        .then_inc(*done("hadd", ("hadd", *step), ("free", *step)))
                if h_update(step):
                    ver, m = h_update(step), a[1]
                    dve.wait_ge(*at("mm", *step))
                    if k != "out":
                        dve.wait_ge(*at("hadd", k, 2, m))
                    nc.vector.tensor_tensor(h[:, m, :], h[:, m, :], ps(step)[:, :], ALU.add)\
                        .then_inc(*done("h", ("h", ver, m), ("free", *step)))
                    if m >= 2:
                        ssadd(ver, m - 1)
                    if m == KD - 1:
                        ssadd(ver, m)
                if k == "ple":
                    i, m = a
                    ver = 2 * i + 2 if i < 2 else 7
                    gb = gsig[m % 2]
                    dve.wait_ge(*at("gsig", i, m))
                    dve.wait_ge(*at("pp", i, m))
                    link(nc.vector.tensor_tensor(gb, gb, pp[i][:, m, :], ALU.mult))
                    nc.vector.tensor_tensor(h[:, m, :], h[:, m, :], gb, ALU.add).then_inc(*done("h", ("h", ver, m)))
                    if m >= 2:
                        ssadd(ver, m - 1)
                    if m == KD - 1:
                        ssadd(ver, m)
                if k == "rope_tables":
                    for m in range(KD - 4, KD):
                        dve.wait_ge(*at("hn", "attn", m))
                    posf = small[:, 0, 0:NT]
                    link(nc.vector.tensor_copy(posf, pos[:, :]))
                    ang = rtmp[:, 0, :]
                    a3 = ang.rearrange("p (t f) -> p t f", t=NT)
                    link(nc.vector.tensor_tensor(a3, over(posf, 32, 2), over(rowb[:, R_FREQ:R_FREQ + 32], NT, 1), ALU.mult))
                    big = float(1.5 * 2 ** 23)
                    link(nc.vector.tensor_scalar(rtmp[:, 1, :], ang, float(1 / (2 * np.pi)), big, ALU.mult, ALU.add))
                    link(nc.vector.tensor_scalar(rtmp[:, 1, :], rtmp[:, 1, :], -big, None, ALU.add))
                    c1 = 6.28125
                    c2 = float(np.float32(2 * np.pi - c1))
                    c3 = float(2 * np.pi - c1 - c2)
                    for c in (c1, c2, c3):
                        link(nc.vector.scalar_tensor_tensor(ang, rtmp[:, 1, :], -c, ang, ALU.mult, ALU.add))
                    pi = 3.1415925
                    link(nc.vector.tensor_scalar(rtmp[:, 2, :], ang, pi, -pi, ALU.min, ALU.max))
                    nc.vector.scalar_tensor_tensor(rtmp[:, 3, :], rtmp[:, 2, :], -1.0, rtmp[:, 2, :], ALU.mult, ALU.max)\
                        .then_inc(*done("angles", ("angles",)))
                    dve.wait_ge(*at("cos"))
                    for j, (w, ws) in enumerate(((R_QN, R_QNS), (R_KN, R_KNS))):
                        for half in range(2):
                            cd = ctab[:, 2 * j, :].rearrange("p (t d) -> p t d", t=NT)[:, :, 32 * half:32 * half + 32]
                            sd = ctab[:, 2 * j + 1, :].rearrange("p (t d) -> p t d", t=NT)[:, :, 32 * half:32 * half + 32]
                            cs = rtmp[:, 5, :].rearrange("p (t d) -> p t d", t=NT)
                            sn = rtmp[:, 4, :].rearrange("p (t d) -> p t d", t=NT)
                            link(nc.vector.tensor_tensor(cd, cs, over(rowb[:, w + 32 * half:w + 32 * half + 32], NT, 1), ALU.mult))
                            link(nc.vector.tensor_tensor(sd, sn, over(rowb[:, ws + 32 * half:ws + 32 * half + 32], NT, 1), ALU.mult))
                        link(nc.vector.tensor_scalar(
                            ctab[:, 2 * j + 1, :].rearrange("p (t d) -> p t d", t=NT)[:, :, 0:32],
                            ctab[:, 2 * j + 1, :].rearrange("p (t d) -> p t d", t=NT)[:, :, 0:32], -1.0, None, ALU.mult))
                if k in ("kv", "q") and a[-1] == 3:
                    nh = 4 if k == "kv" else 8
                    w = nh * HD
                    stage = 0 if k == "kv" else 1 + a[0]
                    lo = 96 * (stage % 2)
                    for t in range(NT):
                        key = (k, *a[:-1], t)
                        dve.wait_ge(*at("qsq", *key))
                        nc.vector.tensor_reduce(flat[:, lo + t * nh:lo + (t + 1) * nh],
                                                qsq[t % 2][:, 0:w].rearrange("p (h d) -> p h d", h=nh), AXX,
                                                ALU.add).then_inc(*done("qss", ("qss", stage * NT + t)))
                    dve.wait_ge(*at("qrms", stage))
                    link(nc.vector.reciprocal(flat[:, lo + 64:lo + 64 + NT * nh], flat[:, lo + 32:lo + 32 + NT * nh]))
                    for t in range(NT):
                        key = (k, *a[:-1], t)
                        n = stage * NT + t
                        b = t % 2
                        if n >= 2:
                            p2 = ("kv", n - 2) if n - 2 < NT else ("q", (n - 2) // NT - 1, (n - 2) % NT)
                            dve.wait_ge(*at("roped", *p2))
                        q3 = qn[b][:, 0:w].rearrange("p (h d) -> p h d", h=nh)
                        nc.vector.tensor_tensor(q3, ps(key)[:, 0:w].rearrange("p (h d) -> p h d", h=nh),
                                                over(flat[:, lo + 64 + t * nh:lo + 64 + (t + 1) * nh], HD, 2), ALU.mult)\
                            .then_inc(*done("qn", ("qn", *key), ("free", *key)))
                        dve.wait_ge(*at("qn", *key))
                        sn = ctab[:, 1 if k == "q" else 3, :].rearrange("p (t d) -> p t d", t=NT)[:, t, :]
                        r3 = rb[b][:, 0:w].rearrange("p (h d) -> p h d", h=nh)
                        nc.vector.tensor_tensor(r3[:, :, 0:32], q3[:, :, 32:64], over(sn[:, 0:32], nh, 1), ALU.mult)
                        nc.vector.tensor_tensor(r3[:, :, 32:64], q3[:, :, 0:32], over(sn[:, 32:64], nh, 1), ALU.mult)\
                            .then_inc(*done("ropeb", ("ropeb", *key)))
                if k == "aS":
                    n, g = a
                    u = n * KV_HEADS + g
                    w = P if n == 0 else 256
                    per = SEQ // w
                    s = Sb[u % 3]
                    mask = swa[:, P:256] if n == 0 else swa
                    sm = small[:, 4 * (u % 3):4 * (u % 3) + 4, :]
                    if u >= 3:
                        dve.wait_ge(*at("mm", "aPT", *divmod(u - 3, KV_HEADS), 0 if u - 3 < KV_HEADS else 1))
                    for j in range(4 // per):
                        dve.wait_ge(*at("mm", "aS", n, g, j))
                        nc.vector.tensor_tensor(s[:, per * j:per * (j + 1), 0:w],
                                                ps(("aS", n, g, j))[:, :].rearrange("p (a b) -> p a b", a=per),
                                                over(mask, per, 1), ALU.add)\
                            .then_inc(*done("amask", ("amask", n, g, j), ("free", "aS", n, g, j)))
                    dve.wait_ge(*at("amask", n, g, 4 // per - 1))
                    link(nc.vector.tensor_reduce(sm[:, 0, 0:4], s[:, :, 0:w], AXX, ALU.max))
                    link(nc.vector.scalar_tensor_tensor(sm[:, 1, 0:4], sm[:, 0, 0:4], -1.0, negsink[:, 4 * g:4 * g + 4],
                                                        ALU.mult, ALU.min))
                    nc.vector.tensor_tensor(sm[:, 1, 4:8], sm[:, 1, 0:4], rowb[:, R_SINK + 4 * g:R_SINK + 4 * g + 4],
                                            ALU.add).then_inc(*done("anegm", ("anegm", n, g)))
                if k == "aR":
                    n, g = a
                    u = n * KV_HEADS + g
                    sm = small[:, 4 * (u % 3):4 * (u % 3) + 4, :]
                    dve.wait_ge(*at("aesink", n, g))
                    link(nc.vector.tensor_tensor(sm[:, 3, 4:8], sm[:, 2, 0:4], sm[:, 1, 8:12], ALU.add))
                    nc.vector.reciprocal(sm[:, 3, 0:4], sm[:, 3, 4:8]).then_inc(*done("arec", ("arec", n, g)))
                if k == "aT":
                    n, g = a
                    u = n * KV_HEADS + g
                    if n:
                        dve.wait_ge(*at("mm", "aPT", n, g, 1))
                        if u >= 2:
                            dve.wait_ge(*at("pv", *divmod(u - 2, KV_HEADS)))
                        nc.vector.tensor_copy(PTb[u % 2][:, 1, :], ps(("aPT", n, g, 1))[:, :])\
                            .then_inc(*done("aPT_dve", ("aPT", n, g, 1), ("free", "aPT", n, g, 1)))
                if k == "aO":
                    n, g = a
                    G2 = g // 2
                    dve.wait_ge(*at("pv", n, g))
                    dve.wait_ge(*at("gs", KD - 1))
                    if n:
                        dve.wait_ge(*at("og", n - 1, G2))
                    nc.vector.tensor_tensor(ogf[G2],
                                            acc(("aO", n, G2))[:, :].rearrange("p (a b) -> p a b", a=4),
                                            gs[:, 4 * G2:4 * G2 + 4, tok(n)], ALU.mult)\
                        .then_inc(*done("ogf", ("ogf", n, G2), ("accfree", "aO", n, G2)))
                if k == "mrow":
                    dve.wait_ge(*at("mm", "mi"))
                    nc.vector.tensor_scalar(mrow[0], ps(("mi",))[0:4, :], mbias[:, 0:1], None, ALU.add)\
                        .then_inc(*done("mi", ("mi_row",), ("free", "mi")))
                    dve.wait_ge(*at("mm", "mf"))
                    nc.vector.tensor_scalar(mrow[1], ps(("mf",))[0:4, :], mbias[:, 1:2], None, ALU.add)\
                        .then_inc(*done("mf", ("mf_row",), ("free", "mf")))
                    dve.wait_ge(*at("mf_row"))
                    nc.vector.scalar_tensor_tensor(mrow[2], mrow[1], -1.0, mrow[1], ALU.mult, ALU.min)\
                        .then_inc(*done("mfabs", ("mfabs",)))
                    link(nc.vector.memset(mrow[4], 0.0))
                    dve.wait_ge(*at("mfln"))
                    link(nc.vector.scalar_tensor_tensor(mrow[1], mrow[1], 0.0, mrow[2],
                                                        ALU.min, ALU.subtract))
                    link(nc.vector.tensor_tensor_scan(mrow[3], mrow[1], mrow[4], 0.0, ALU.add, ALU.add))
                    nc.vector.tensor_tensor(mrow[0], mrow[0], mrow[3], ALU.subtract)\
                        .then_inc(*done("mrrow", ("mrrow",)))
                    dve.wait_ge(*at("mrrow"))
                    link(nc.vector.tensor_tensor_scan(mrow[1], mrow[0], mrow[0], 0.0, ALU.max, ALU.max))
                    nc.vector.tensor_tensor(mrow[2], mrow[1], mrow[3], ALU.add)\
                        .then_inc(*done("mmt", ("mmt",)))
                if k == "cmp_in":
                    j = a[0]
                    dve.wait_ge(*at("done", *step))
                    dve.wait_ge(*at("czero", j))
                    for g in range(2):
                        rows = slice(HD * g, HD * (g + 1))
                        raw = ckv[rows, j, :]
                        src = bass.AP(tensor=ckv.tensor, offset=raw.offset,
                                      ap=[list(raw.ap[0]), [1, CMP_BLOCK], [CMP_STRIDE, NC_BLK]])
                        last = nc.vector.tensor_tensor(cblk[j][rows, :, NC_BLK * g:NC_BLK * (g + 1)], src,
                                                       over(peT[rows, j, :], NC_BLK, 2), ALU.add)
                    last.then_inc(*done("cblk", ("cblk", j)))
                if k == "cmp":
                    j = a[0]
                    x = ctm[:, 0, :].rearrange("p (g n) -> p g n", g=2)[:, :, 0:NC_BLK]
                    y = ctm[:, 1, :].rearrange("p (g n) -> p g n", g=2)[:, :, 0:NC_BLK]
                    z = ctm[:, 2, :].rearrange("p (g n) -> p g n", g=2)[:, :, 0:NC_BLK]
                    if j == 0:
                        dve.wait_ge(*at("cblk", 1))
                        link(nc.vector.memset(ctm[:, :, :], 0.0))
                    dve.wait_ge(*at("mm", "chid", j))
                    nc.vector.tensor_copy(x, acc(("chid", j))[:, 0:2 * NC_BLK].rearrange("p (g n) -> p g n", g=2))\
                        .then_inc(*done("chidc", ("chidc", j), ("accfree", "chid", j)))
                    dve.wait_ge(*at("chidc", j))
                    link(nc.vector.tensor_tensor(y, x, x, ALU.mult))
                    link(nc.vector.tensor_scalar(y, y, 0.044715, 1.0, ALU.mult, ALU.add))
                    nc.vector.tensor_tensor(y, y, x, ALU.mult).then_inc(*done("gelu_in", ("gelu_in", j)))
                    dve.wait_ge(*at("ctanh", j))
                    link(nc.vector.tensor_scalar(z, y, 1.0, 0.5, ALU.add, ALU.mult))
                    nc.vector.tensor_tensor(chid[:, j, :].rearrange("p (g n) -> p g n", g=2)[:, :, 0:NC_BLK], z, x, ALU.mult)\
                        .then_inc(*done("gelu", ("gelu", j)))
                    dve.wait_ge(*at("gelu", j))

                def marg(n):
                    h_, s = divmod(n, NT)
                    if h_ == M_HEADS:
                        return
                    if s == 0:
                        dve.wait_ge(*at("Mneg", h_))
                    if n >= 2:
                        dve.wait_ge(*at("wt", *divmod(n - 2, NT)))
                    nc.vector.tensor_scalar(wt[n % 2][:, 0:SEQ - P * s], Mneg[h_ % 2][:, P * s:SEQ], rcol[:, s, h_:h_ + 1], 0.0,
                                            ALU.add, ALU.min).then_inc(*done("marg", ("marg", h_, s)))

                if k == "mA":
                    dve.wait_ge(*at("rcol"))
                    marg(0)
                if k == "mB":
                    h_ = a[0]
                    for s in range(NT):
                        n = h_ * NT + s
                        marg(n + 1)
                        w = SEQ - P * s
                        dve.wait_ge(*at("mexpd", h_, s))
                        dve.wait_ge(*at("mm", "KQ", h_, s))
                        if n >= 2:
                            dve.wait_ge(*at("numden", *divmod(n - 2, NT)))
                        nc.vector.tensor_tensor(wk[n % 2][:, 0:w], wt[n % 2][:, 0:w], ps(("KQ", h_, s))[:, 0:w], ALU.mult)\
                            .then_inc(*done("wt", ("wt", h_, s), ("free", "KQ", h_, s)))
                    dve.wait_ge(*at("mabs", h_))
                    dve.wait_ge(*at("mm", "En", h_))
                    dve.wait_ge(*at("mden", h_))
                    nc.vector.tensor_tensor(mtmp, mtmp, ps(("En", h_))[:, :], ALU.max)\
                        .then_inc(*done("mdmax", ("mdmax", h_), ("free", "En", h_)))
                    dve.wait_ge(*at("mdmax", h_))
                    link(nc.vector.reciprocal(mtmp, mtmp))
                    nc.vector.tensor_tensor(hm[:, h_, :], mtmp, acc(("num", h_))[:, :], ALU.mult)\
                        .then_inc(*done("hm", ("hm", h_), ("accfree", "num", h_)))
                if k == "mnorm":
                    for h_ in range(M_HEADS):
                        dve.wait_ge(*at("mrms", h_))
                        link(nc.vector.reciprocal(mqT[:, h_, :], mqT[:, h_, :]))
                        link(nc.vector.scalar_tensor_tensor(hm[:, h_, :], hm[:, h_, :], vec[:, V_MN + h_:V_MN + h_ + 1],
                                                            mqT[:, h_, :], ALU.mult, ALU.mult))
                        nc.vector.tensor_tensor(hm[:, h_, :], hm[:, h_, :], moT[:, h_, :], ALU.mult)\
                            .then_inc(*done("mgated", ("mgated", h_)))
                if k == "nS":
                    i, g, br = a
                    u = NSEQ[a]
                    q = 4 * "csw".index(br)
                    sm = small[:, q:q + 4, :]
                    h0 = 4 * g
                    if br == "c":
                        s = scb[g]
                        dve.wait_ge(*at("cmpb"))
                        if i:
                            dve.wait_ge(*at("mm", "nPT", i - 1, g, "c", 0))
                        dve.wait_ge(*at("mm", "nS", *a, 0))
                        nc.vector.tensor_tensor(s[:, :, :], ps(("nS", *a, 0))[:, 0:P].rearrange("p (r c) -> p r c", r=4)[:, :, 0:NC_BLK],
                                                cmpb[:, i, h0:h0 + 4, :], ALU.add)\
                            .then_inc(*done("nmask", ("nmask", *a), ("free", "nS", *a, 0)))
                        dve.wait_ge(*at("nmask", *a))
                        link(nc.vector.tensor_reduce(sm[:, 0, 0:4], s[:, :, :], AXX, ALU.max))
                        nc.vector.tensor_tensor(s[:, :, :], s[:, :, :], over(sm[:, 0, 0:4], NC_BLK, 2), ALU.subtract)\
                            .then_inc(*done("nnegm", ("nnegm", *a)))
                    else:
                        w = P * (i + 1)
                        s = nSb[u % 2]
                        if i == 0:
                            dve.wait_ge(*at("alibi", g))
                        if NPREV[a] is not None:
                            dve.wait_ge(*at("mm", "nPT", *NPREV[a], NPREV[a][0]))
                        for r in range(4):
                            dve.wait_ge(*at("mm", "nS", *a, r))
                            nc.vector.tensor_tensor_reduce(out=s[:, r, 0:w], in0=ps(("nS", *a, r))[:, 0:w],
                                                           in1=alibi[:, h0 + r, SEQ - w:SEQ], scale=1.0, scalar=-3e38,
                                                           op0=ALU.add, op1=ALU.max, accum_out=sm[:, 0, r:r + 1])\
                                .then_inc(*done("nmask", ("nmask", *a, r), ("free", "nS", *a, r)))
                        dve.wait_ge(*at("nmask", *a, 3))
                        nc.vector.tensor_scalar(sm[:, 1, 0:4], sm[:, 0, 0:4], -1.0, None, ALU.mult)\
                            .then_inc(*done("nnegm", ("nnegm", *a)))
                if k == "nR":
                    i, g, br = a
                    q = 4 * "csw".index(br)
                    sm = small[:, q:q + 4, :]
                    h0 = 4 * g
                    gcol = gat[:, i, :].rearrange("p (h b) -> p b h", b=3)[:, "csw".index(br), h0:h0 + 4]
                    dve.wait_ge(*at("nexp", *a))
                    if br == "c":
                        s = scb[g]
                        link(nc.vector.tensor_reduce(sm[:, 2, 0:4], s[:, :, :], AXX, ALU.add))
                        link(nc.vector.reciprocal(sm[:, 3, 4:8], sm[:, 2, 0:4]))
                        if i == 0:
                            link(nc.vector.tensor_scalar(sm[:, 3, 4:8], sm[:, 3, 4:8], rowvalid, None, ALU.mult))
                        dve.wait_ge(*at("avg", i))
                        link(nc.vector.tensor_tensor(sm[:, 3, 0:4], sm[:, 3, 4:8], gcol, ALU.mult))
                        nc.vector.tensor_tensor(s[:, :, :], s[:, :, :], over(sm[:, 3, 0:4], NC_BLK, 2), ALU.mult)\
                            .then_inc(*done("nprobc", ("nprob", *a)))
                    else:
                        link(nc.vector.reciprocal(sm[:, 3, 4:8], sm[:, 2, 0:4]))
                        nc.vector.tensor_tensor(sm[:, 3, 0:4], sm[:, 3, 4:8], gcol, ALU.mult)\
                            .then_inc(*done("nrec", ("nrec", *a)))
                if k == "nT":
                    i, g, br = a
                    for kt in range(1 if br == "c" else i + 1):
                        n = NPT[(*a, kt)]
                        if n % 2 == 1:
                            dve.wait_ge(*at("mm", "nPT", *a, kt))
                            if n >= 4:
                                dve.wait_ge(*at("npv", n - 4))
                            rows = NC_BLK if br == "c" else P
                            nc.vector.tensor_copy(nPb[n % 4][0:rows, :], ps(("nPT", *a, kt))[0:rows, :])\
                                .then_inc(*done("nPT_dve", ("nPT", *a, kt), ("free", "nPT", *a, kt)))
                if k == "nO":
                    i = a[0]
                    dve.wait_ge(*at("noghi", i))
                    nc.vector.tensor_tensor(xgl[:, 4:8, tok(i)], acc(("nO", i))[:, :].rearrange("p (a b) -> p a b", a=4),
                                            xgh[:, 4:8, tok(i)].bitcast(F32), ALU.subtract)\
                        .then_inc(*done("nog", ("nog", i), ("accfree", "nO", i)))
                if k == "upg":
                    m = a[0]
                    b = ps(step)
                    c = fca[m % 2]
                    dve.wait_ge(*at("fconv0", m))
                    for s in range(1, 3):
                        w = vec[:, V_C2W + (2 - s) * FT + m:V_C2W + (2 - s) * FT + m + 1]
                        x = nc.vector.scalar_tensor_tensor(c[:, s:SEQ], b[:, 0:SEQ - s], w, c[:, s:SEQ], ALU.mult, ALU.add)
                        if s == 1:
                            link(x)
                        else:
                            x.then_inc(*done("fconv", ("fconv", m), ("free", "upg", m)))
                if k == "upv":
                    m = a[0]
                    dve.wait_ge(*at("mm", "upv", m))
                    dve.wait_ge(*at("fsilu", m))
                    nc.vector.tensor_tensor(fsl[m % 2], fsl[m % 2], ps(("upv", m))[:, :], ALU.mult)\
                        .then_inc(*done("fff", ("fff", m), ("free", "upv", m)))
    return ev.seen


NSEQ, NPREV, NPT = {}, {}, {}
for _s in STEPS:
    if _s[0] == "nS":
        _a = _s[1:]
        _big = [x for x in NSEQ if x[2] != "c"]
        NSEQ[_a] = len(_big)
        if _a[2] != "c":
            NPREV[_a] = _big[-2] if len(_big) >= 2 else None
    if _s[0] == "nT":
        for _k in range(1 if _s[3] == "c" else _s[1] + 1):
            NPT[(*_s[1:], _k)] = len(NPT)


def pack(v):
    f = {k: np.asarray(x) for k, x in v.items()}

    def cols(w, order):
        return w[:, order]

    pair16 = np.concatenate([np.arange(64) + 64 * hh for G in range(2) for r in range(4) for hh in (8 * G + r, 8 * G + 4 + r)])
    pair8 = np.concatenate([np.arange(64) + 64 * hh for r in range(4) for hh in (r, 4 + r)])
    wi = f["w_in_2"][0]
    o = np.cumsum([0, 512, 512, 512, 512, 4, 4, 512] + [128] * 6 + [24])
    mq, mk, mv, mo, mi, mf, aq, akc, avc, aks, avs, akw, avw, ag = (wi[:, o[i]:o[i + 1]] for i in range(14))
    stationary = {
        "ssm_in": f["ssm_in_w"][0], "attn_out": f["attn_out_w"][0][pair16],
        "attn_gate": cols(f["attn_in_w"][0][:, 1024:], pair16),
        "w_out": np.concatenate([f["w_out_2"][0][:512], f["w_out_2"][0][512:][pair8]]),
        "mq": mq, "mk": mk, "mo": mo, "aq": cols(aq, pair8), "ak": np.concatenate([aks, akw], 1),
        "cmp_in": np.concatenate([akc, avc], 1), "upg": f["w_up_2"][0][:, :D_FF], "upv": f["w_up_2"][0][:, D_FF:],
    }
    moving = {
        "kv": f["kv_w"], "attn_q": f["attn_in_w"][0][:, :1024], "mv": mv,
        "avg": np.concatenate([avs, avw, ag, mi, mf, np.zeros((D, SEQ - 288), np.float32)], 1),
    }
    gates = [f["ple_gate_w"][0], f["ple_gate_w"][1], f["w_ple_gate_2"][0]]
    projs = [f["ple_proj_w"][0], f["ple_proj_w"][1], f["w_ple_proj_2"][0]]
    ps_ = [f["p"][0, 0], f["p"][1, 0], f["p_2"][0, 0]]
    w1 = [f["cmp_k_w1_2"][0], f["cmp_v_w1_2"][0]]

    def block(b):
        k = b[0]
        if k == "p":
            return ps_[b[1]].T.reshape(2, P, SEQ).transpose(1, 0, 2)
        if k == "ple_proj":
            return projs[b[1]][:, b[2] * SEQ:(b[2] + 1) * SEQ].reshape(2, P, SEQ).transpose(1, 0, 2)
        if k == "ple_gate":
            return gates[b[1]][:, b[2] * P:(b[2] + 1) * P].reshape(KD, P, P).transpose(1, 0, 2)
        if k == "cmp_w1":
            w = w1[b[1]].reshape(CMP_BLOCK, HD, P)[8 * b[2]:8 * b[2] + 8].transpose(1, 0, 2)
            return np.concatenate([w, w], 0)
        if k == "dt":
            w = np.concatenate([f["ssm_in_w"][0][:, -HEADS:], np.zeros((D, P - HEADS), np.float32)], 1)
            return w.reshape(KD, P, P).transpose(1, 0, 2)
        if k in ("sout", "dn"):
            w = {"sout": f["ssm_out_w"][0], "dn": f["w_down_2"][0]}[k][512 * b[1]:512 * (b[1] + 1), 256 * b[2]:256 * (b[2] + 1)]
            return w.reshape(4, P, 256).transpose(1, 0, 2)
        if k in moving:
            w = moving[k][:, (b[1] * SEQ if k == "attn_q" else 0):][:, :SEQ]
            return w[256 * b[-1]:256 * (b[-1] + 1)].reshape(2, P, SEQ).transpose(1, 0, 2)
        w = stationary[k][D * b[2]:D * (b[2] + 1), b[1] * P:(b[1] + 1) * P]
        return w.reshape(KD, P, P).transpose(1, 0, 2)

    res = {"wstream": np.stack([block(b).reshape(P, BLK) for b in BLOCKS])}
    res["xT"] = np.ascontiguousarray(f["x"][0].T.reshape(KD, P, SEQ))

    def tiles(x):
        return x.reshape(-1, P).T

    norms = [f["ssm_norm_w"], f["kv_norm_w"], f["attn_norm_w"], f["ple_norm_w"][0], f["ple_norm_w"][1], f["ln1_g_2"],
             f["ln2_g_2"], f["ple_norm_g_2"], f["final_g_2"]]
    vec = [tiles(x) for x in norms] + [tiles(f["ssm_conv_w"]), tiles(f["ssm_conv_b"]), tiles(f["ssm_gnorm_w"]),
                                       tiles(np.repeat(f["ssm_d"][0], HD)), tiles(f["conv_w_2"]), tiles(f["conv_b_2"]),
                                       tiles(f["mlstm_norm_g_2"])]
    res["vec"] = np.concatenate(vec, 1)
    assert res["vec"].shape == (P, NV)
    qw, kw = f["q_norm_w"][0], f["k_norm_w"]
    half = 32
    inv_freq = (10000.0 ** (-(np.arange(half, dtype=np.float32) * 2.0 / HD))).astype(np.float32)
    row = np.concatenate([f["ssm_dt_bias"][0], f["ssm_a_log"][0], qw, qw[half:], qw[:half], kw, kw[half:], kw[:half],
                          f["attn_sinks"][0], inv_freq])
    res["rowb"] = np.broadcast_to(row, (P, NR))
    res["w2c"] = np.stack([f["cmp_k_w2_2"][0], f["cmp_v_w2_2"][0]], 1)
    pe = np.stack([f["cmp_pos_k_2"][0].T, f["cmp_pos_v_2"][0].T], 1)
    res["peT"] = np.concatenate([pe, pe], 0)
    res["mbias"] = f["mlstm_gate_bias_2"][0].reshape(2, 4).T
    res["pos"] = f["positions"][0].reshape(NT, P).T.astype(np.int32)
    res.update(constants())
    return {k: np.ascontiguousarray(x) for k, x in res.items()}


def constants():
    i = np.arange(P)
    con = np.zeros((P, NCON), np.float32)
    con[:, C_ID:C_ID + P] = np.eye(P)
    con[:, C_T:C_T + P] = i[:, None] <= i[None, :]
    con[:, C_U:C_U + P] = i[:, None] > i[None, :]
    con[:, C_ONE:C_ONE + P] = 1.0
    c = np.arange(256)
    con[:, C_SWA:C_SWA + 256] = np.where((c[None, :] - P <= i[:, None]) & (c[None, :] > i[:, None]), 0.0, NEG)
    slope = 2.0 ** -(np.arange(A_HEADS) + 1.0)
    t = np.arange(SEQ).reshape(NT, P).T
    end = CMP_STRIDE * np.arange(NC_BLK) + CMP_BLOCK - 1
    dist = t[:, :, None, None] - end[None, None, None, :]
    cb = np.where(dist >= 0, -slope[None, None, :, None] * dist, NEG)
    con[:, C_RV] = i >= CMP_BLOCK - 1
    sel = np.zeros((4, 4, P), np.float32)
    for h in range(4):
        sel[h, h] = 1.0
    d = 384 + i[:, None, None] - np.arange(SEQ)[None, None, :]
    ali = np.where(d >= 0, -slope[None, :, None] * d, NEG).astype(np.float32)
    return {"con": con, "alibi": ali, "cmpb": cb.reshape(P, -1).astype(np.float32), "sel": sel}


def kernel(**inputs):
    import concourse.bacc as bacc
    from concourse.bass_utils import run_bass_kernel_spmd as run

    arrays = pack(inputs)
    known = None
    for _ in range(2):
        nc = bacc.Bacc("TRN2", target_bir_lowering=False, num_devices=1)
        aps = {k: nc.dram_tensor("in_" + k, x.shape, mybir.dt.from_np(x.dtype), kind="ExternalInput").ap()
               for k, x in arrays.items()}
        out = nc.dram_tensor("outT", (KD, P, SEQ), F32, kind="ExternalOutput").ap()
        known = build(nc, aps, out, known)
    r = run(nc, [{"in_" + k: x for k, x in arrays.items()}], core_ids=[0])
    return r.results[0]["outT"].reshape(D, SEQ).T[None]
```

```python
from contextlib import ExitStack

import numpy as np

import concourse.bass as bass
from concourse import mybir

F32 = mybir.dt.float32
I32 = mybir.dt.int32
F32R = mybir.dt.float32r
ALU = mybir.AluOpType
ACT = mybir.ActivationFunctionType
AXX = mybir.AxisListType.X

P = 128
SEQ = 512
NT = SEQ // P
D = 1024
KD = D // P
EPS = 1e-6
NEG = -1e30

GROUPS = 4
HPG = 8
HEADS = GROUPS * HPG
HD = 64
D_INNER = 2048
GT = 4
D_STATE = 128
TAPS = 4
ATT_HEADS = 16
KV_HEADS = 4
M_HEADS = 4
A_HEADS = 8
NC_BLK = 31
CMP_BLOCK = 32
CMP_STRIDE = 16
D_FF = 2048
FT = D_FF // P
PLE = 256

NSLOT = 3
NSET = 2
NROT = 6
BLK = 1024

NORMS = ["ssm", "kv", "attn", "ple0", "ple1", "ln1", "ln2", "ple2", "final"]
V_NORM = {n: 8 * i for i, n in enumerate(NORMS)}
V_CW = 72
V_CB = V_CW + TAPS * 24
V_GN = V_CB + 24
V_D = V_GN + 16
V_C2W = V_D + 16
V_C2B = V_C2W + 3 * FT
V_MN = V_C2B + FT
NV = V_MN + 4

R_DTB, R_ALOG, R_QN, R_QNS, R_KN, R_KNS, R_SINK, R_FREQ = 0, 32, 64, 128, 192, 256, 320, 336
NR = R_FREQ + 32

C_ID, C_T, C_U, C_ONE, C_SWA, C_RV = 0, 128, 256, 384, 512, 768
NCON = C_RV + 1
NCMP = NT * A_HEADS * NC_BLK

VERSION_OF = {"ssm": 0, "ple0": 1, "kv": 2, "attn": 2, "ple1": 3, "ln1": 4, "ln2": 5, "ple2": 6, "final": 7}


def pipeline(x, units, closing):
    n = len(units)
    out = [(x + "S", *u) for u in units[:3]]
    for u in units[:2]:
        out += [(x + "E", *u), (x + "R", *u)]
    for i, u in enumerate(units):
        out.append((x + "T", *u))
        if i + 2 < n:
            out.append((x + "E", *units[i + 2]))
        if i and units[i - 1] in closing:
            out.append((x + "O", *units[i - 1]))
        if i + 3 < n:
            out.append((x + "S", *units[i + 3]))
        if i + 2 < n:
            out.append((x + "R", *units[i + 2]))
        out.append((x + "V", *u))
    return out + [(x + "O", *units[-1])]


def steps():
    out = [("load",), ("norm", 0), ("first_weights",), ("nb", 0), ("hn", "ssm")]
    proj = {g: [("proj", g, i) for i in range(10)] for g in range(GROUPS)}
    sout = {g: [("sout", g, m) for m in range(KD)] for g in range(GROUPS)}
    out += proj[0][:2] + [("dtl",), proj[0][2], ("dt",), proj[0][3], proj[0][4], ("cum",)] + proj[0][5:]
    for g in range(GROUPS):
        scan = [("ssd0", g), ("ssd1", g, 0), ("ssd1", g, 1), ("ssd2", g, 0), ("ssd1", g, 2), ("ssd2", g, 1),
                ("ssd1", g, 3), ("ssd2", g, 2), ("ssd2", g, 3)]
        if g < 2:
            nxt = proj[g + 1]
            fill = nxt[:2] + (sout[g - 1] if g else []) + nxt[2:6]
            between, after = [[], nxt[6:7], nxt[7:8], nxt[8:9]], nxt[9:]
        elif g == 2:
            nxt, so = proj[3], sout[1]
            fill = nxt[:2] + so[:4] + nxt[2:6]
            between, after = [so[4 + m:5 + m] for m in range(GT)], nxt[6:7]
        else:
            nxt, so = proj[3], sout[2]
            fill = nxt[7:8] + so[:2] + nxt[8:9] + so[2:4] + nxt[9:] + [("psp", 0)]
            between, after = [so[4:6], [("pp", 0, 0)], [("pp", 0, 1)], [("pp", 0, 2)]], [("pp", 0, 3)] + so[6:]
        k = 0
        for i, x in enumerate(scan):
            out.append(x)
            while k < len(fill) and k * len(scan) < (i + 1) * len(fill):
                out.append(fill[k])
                k += 1
        out += fill[k:]
        for m in range(GT):
            out.append(("yt", g, m))
            out += between[m]
        out += [("gn", g)] + after[:1] + [("gb", g)] + after[1:]
    def early(name, m):
        return [("he", name, m)]

    def gated(i, ver, first):
        name = f"ple{i}"
        x = early(name, 5) + [("pp", i, m) for m in range(first, KD - 2)] + [("norm", ver)]
        return x + [("pp", i, KD - 2), ("pp", i, KD - 1)] + early(name, 6) + early(name, 7) + [("nb", ver)]

    for m in range(KD):
        out.append(sout[GROUPS - 1][m])
        if 2 <= m < 7:
            out += early("ple0", m - 2)
    out += gated(0, 1, 4)
    for m in range(KD):
        out += [("ple", 0, m)] + (early("kv", m - 1) if m else []) + ([("rope_tables",)] if m == 1 else [])
    out += early("kv", 7)
    out += [("kv", 0), ("norm", 2), ("kv", 1), ("nb", 2), ("hn", "attn"), ("kv", 2), ("kv", 3)]
    ro = {s: [("ro", s, t) for t in range(NT)] for s in range(3)}
    out += ro[0][:2] + [("gate", 0)] + ro[0][2:] + [("gate", 1), ("kT",)] + [("q", 0, b) for b in range(4)]
    out += ro[1][:1] + [("gate", 2)] + ro[1][1:3] + [("gate", 3)] + ro[1][3:] + [("gate", 4), ("qT", 0)]
    out += [("q", 1, b) for b in range(4)] + ro[2][:2] + [("gate", 5)] + ro[2][2:] + [("gate", 6), ("qT", 1)]
    units = [(n, g) for n in range(NT) for g in range(KV_HEADS)]
    swa = pipeline("a", units, [x for x in units if x[1] % 2 == 1])
    out += swa[:7] + [("gate", 7)] + swa[7:]
    out += [("out", 3, 0), ("out", 3, 1), ("psp", 1)]
    for m in range(2, KD):
        out += [("out", 3, m)] + (early("ple1", m - 2) if m < 7 else [])
    out += gated(1, 3, 0)
    for m in range(KD):
        out += [("ple", 1, m)] + (early("ln1", m - 1) if m else [])
    out += early("ln1", 7)
    out += [("avg", 0), ("norm", 4), ("avg", 1), ("nb", 4), ("avg", 2), ("avg", 3)] + [("cmp_in", 0), ("mif",), ("mrow",), ("cmp_in", 1)]
    out += [("mlog",), ("mv", 0), ("mscan",), ("mv", 1), ("mexp",), ("mv", 2), ("mv", 3)]
    lin = [("mq", m) for m in range(4)] + [("mk", m) for m in range(4)]
    lin += [("aq", m) for m in range(4)] + [("ak", 0), ("ak", 1)] + [("mo", m) for m in range(3)]
    for i, x in enumerate(lin):
        out.append(x)
        if i == 3:
            out.append(("mrcol",))
        if 1 <= i <= 4:
            out.append(("cmpq", 0, i - 1))
        if i == 6:
            out.append(("cmp", 0))
        if 7 <= i <= 10:
            out.append(("cmpq", 1, i - 7))
        if i == 12:
            out.append(("cmp", 1))
        if i == 14:
            out.append(("cmp2",))
    out += [("mA",)] + [("mB", h) for h in range(M_HEADS)]
    seq = [(i, g, b) for i in range(NT) for g in range(2) for b in "csw"]
    nsa = pipeline("n", seq, [x for x in seq if x[1:] == (1, "w")])
    out += nsa[:2] + [("mfac",)] + nsa[2:7] + [("mo", 3)]
    rest, h = nsa[7:], 0
    for x in rest:
        out.append(x)
        if x[0] == "nV" and h < M_HEADS:
            out.append(("mg", h))
            h += 1
    for m in range(KD):
        out += [("out", 5, m)] + (early("ln2", m - 2) if m >= 2 else [])
    out += early("ln2", 6) + early("ln2", 7)
    out += [("L", "upg", 0), ("norm", 5), ("L", "upv", 0), ("nb", 5)]
    for m in range(FT + 4):
        if m < FT:
            out.append(("upg", m))
            if m:
                out.append(("fh", m - 1))
            out.append(("upv", m))
        if m == FT - 1:
            out.append(("fh", m))
        if m >= 4:
            for j in range(2):
                c = 2 * (m % 4) + j
                out.append(("dn", m // 4 - 1, c))
                if m >= FT and 2 <= c < 7:
                    out += early("ple2", c - 2)
        if m == FT - 1:
            out.append(("psp", 2))
    out += gated(2, 6, 0)
    out += [("ple", 2, m) for m in range(KD)]
    out += [("norm", 7), ("nb", 7), ("hn", "final")]
    return out


STEPS = steps()
SWAP = STEPS.index(("avg", 0))


def jobs_of(step):
    k, a = step[0], step[1:]
    if k == "L":
        return [a]
    if step in (("upg", 0), ("upv", 0)):
        return []
    if k in ("dtl", "dt", "cum", "upg", "upv", "proj", "pp", "out", "sout", "dn", "gate", "mq", "mk", "mo", "aq", "ak", "cmp_in", "gn", "gb", "yt", "mg"):
        return [step]
    if k == "ple":
        return [step]
    if k == "ssd0":
        return [("cb", *a), ("bt", *a)]
    if k == "ssd1":
        return [("xt", *a), ("seg", *a, 0), ("seg", *a, 1)]
    if k == "ssd2":
        g, c = a
        return [("yd", g, c)] + ([("yo", g, c)] if c else []) + ([("st", g, c)] if c < NT - 1 else [])
    if k in ("kv", "mv", "avg", "q"):
        return [(k, *a[:-1], t) for t in range(NT)] if a[-1] == 0 else []
    if k == "kT":
        return [("kT", t) for t in range(NT)]
    if k == "qT":
        return [("qT", a[0], t) for t in range(NT)]
    if k == "aS":
        return [("aS", *a, j) for j in range(1 if a[0] == 0 else 2)]
    if k == "aT":
        return [("aPT", *a, kt) for kt in range(1 if a[0] == 0 else 2)]
    if k == "mif":
        return [("mi",), ("mf",)]
    if k == "mrcol":
        return [("mrcol",)]
    if k == "mA":
        return [("ecol",), ("Mb", 0)] + [("KQ", 0, s) for s in range(NT)]
    if k == "mB":
        h = a[0]
        if h + 1 == M_HEADS:
            return [("num", h)]
        return [("Mb", h + 1), ("num", h)] + [("KQ", h + 1, s) for s in range(NT)]
    if k == "cmp2":
        return [("ckT",), ("cv",)]
    if k == "nS":
        return [("nS", *a, r) for r in range(1 if a[2] == "c" else 4)]
    if k == "nT":
        return [("nPT", *a, kt) for kt in range(1 if a[2] == "c" else a[0] + 1)]
    return []


JOBS = [j for s in STEPS for j in jobs_of(s)]
JOBNO = {j: i for i, j in enumerate(JOBS)}


def accs_of(step):
    k, a = step[0], step[1:]
    if k == "cmpq" and a[1] == 0:
        return [("chid", a[0])]
    if k == "aV" and a[1] % 2 == 0:
        return [("aO", a[0], a[1] // 2)]
    if k == "mA":
        return [("dtok",)]
    if k == "norm":
        return [("ss", a[0])]
    if k == "nb":
        return [("rb", a[0])]
    if k == "nV" and a[1:] == (0, "c"):
        return [("nO", a[0])]
    return []


ACCS = [j for s in STEPS for j in accs_of(s)]
ACCNO = {j: i for i, j in enumerate(ACCS)}


def blocks_of(step):
    k, a = step[0], step[1:]
    if k == "L":
        return [(*a, 0)]
    if step in (("upg", 0), ("upv", 0)):
        return []
    if k == "proj":
        g, i = a
        t = [("ssm_in", 32 + g), ("ssm_in", 36 + g)] + [("ssm_in", 16 + GT * g + m) for m in range(GT)]
        t += [("ssm_in", GT * g + m) for m in range(GT)]
        return [(*t[i], 0)]
    if k == "pp":
        return [("ple_proj", a[0], a[1] // 4)] if a[1] % 4 == 0 else []
    if k == "psp":
        return [("p", a[0])]
    if k == "out":
        return [({3: "attn_out", 5: "w_out"}[a[0]], a[1], 0)]
    if k in ("sout", "dn"):
        return [(k, a[0], a[1] // 2)] if a[1] % 2 == 0 else []
    if k == "dtl":
        return [("dt",)]
    if k == "ple":
        return [("ple_gate", a[0], a[1])]
    if k == "q":
        return [("attn_q", *a)]
    if k == "gate":
        return [("attn_gate", a[0], 0)]
    if k in ("kv", "mv", "avg"):
        return [step]
    if k in ("mq", "mk", "mo", "aq", "ak", "cmp_in"):
        return [(k, a[0], 0)]
    if k == "cmpq":
        return [("cmp_w1", *a)]
    if k in ("upg", "upv"):
        return [(k, a[0], 0)]
    return []


BLOCKS = [b for s in STEPS for b in blocks_of(s)]
BLKNO = {b: i for i, b in enumerate(BLOCKS)}
SPLIT = [b for b in BLOCKS if b[0] not in ("cmp_w1", "p")]
SPLITNO = {b: i for i, b in enumerate(SPLIT)}


def h_update(step):
    k, a = step[0], step[1:]
    if k == "out":
        return a[0]
    if k == "sout":
        return 1 if a[0] == GROUPS - 1 else None
    if k == "dn":
        return 6 if a[0] == 3 else None
    return None


def last_uses(step):
    k, a = step[0], step[1:]
    if k in ("sout", "dn"):
        return [(k, a[0], a[1] // 2)] if a[1] % 2 else []
    if k == "pp":
        return [("ple_proj", a[0], a[1] // 4)] if a[1] % 4 == 3 else []
    return [b for b in blocks_of(step) if b in SPLITNO]


def splits_at(step):
    if step[0] == "first_weights":
        return [(b, SPLITNO[b]) for b in SPLIT[:NSET]]
    res = [(b, None) for b in blocks_of(step) if b[0] == "p"]
    for b in last_uses(step):
        n = SPLITNO[b] + NSET
        if n < len(SPLIT):
            res.append((SPLIT[n], n))
    return res


class Events:

    def __init__(self, nc, ctx, known):
        self.nc, self.ctx, self.known = nc, ctx, known
        self.sems, self.count, self.seen = {}, {}, {}

    def sem(self, name):
        if name not in self.sems:
            self.sems[name] = self.ctx.enter_context(self.nc.semaphore(name))
            self.count[name] = 0
        return self.sems[name]

    def done(self, name, *events, inc=1):
        s = self.sem(name)
        self.count[name] += inc
        for e in events:
            assert e not in self.seen, e
            self.seen[e] = (name, self.count[name])
        return s, inc

    def at(self, *event):
        if self.known is None:
            return self.sem("first_pass"), 1
        name, value = self.known[event]
        return self.sem(name), value


def build(nc, ins, out, known):
    ctx = ExitStack()
    with ctx:
        ev = Events(nc, ctx, known)
        done, at = ev.done, ev.at

        def sb(name, shape, dt=F32):
            return ctx.enter_context(nc.sbuf_tensor(name, shape, dt))

        h = sb("h", [P, KD, SEQ])
        parts = [(sb(f"parts{i}h", [P, KD, SEQ], F32R), sb(f"parts{i}l", [P, KD, SEQ], F32R)) for i in range(2)]

        def roles(number):
            return parts if number < SWAP else parts[::-1]

        wsh = [sb(f"wsh{i}", [P, BLK], F32R) for i in range(NSET)]
        wsl = [sb(f"wsl{i}", [P, BLK], F32R) for i in range(NSET)]
        ring = sb("ring", [P, NSLOT, BLK])
        con = sb("con", [P, NCON])
        vec = sb("vec", [P, NV])
        rowb = sb("rowb", [P, NR])
        w2c = sb("w2c", [P, 2, HD])
        peT = sb("peT", [P, 2, CMP_BLOCK])
        mbias = sb("mbias", [4, 2])
        pos = sb("pos", [P, NT], I32)
        eps = sb("eps", [P, 1])
        halfpi = sb("halfpi", [P, 1])
        sq = sb("sq", [P, 3, SEQ])
        ssacc = sb("ssacc", [P, SEQ])
        rt = sb("rt", [P, SEQ])
        NAR = 40
        arena = sb("arena", [P, NAR * SEQ])
        bank = [ctx.enter_context(nc.psum_tensor(f"bank{i}", [P, SEQ], F32)) for i in range(8)]

        def ar(unit, *dims):
            n = int(np.prod(dims))
            lo = int(unit * SEQ)
            assert lo + n <= NAR * SEQ
            v = arena[:, lo:lo + n]
            if len(dims) == 2:
                v = v.rearrange("p (a b) -> p a b", a=dims[0])
            if len(dims) == 3:
                v = v.rearrange("p (a b c) -> p a b c", a=dims[0], b=dims[1])
            return v

        ident, tri, upper, ones = (con[:, c:c + P] for c in (C_ID, C_T, C_U, C_ONE))
        swa = con[:, C_SWA:C_SWA + 256]
        rowvalid = con[:, C_RV:C_RV + 1]

        def ps(job):
            return bank[JOBNO[job] % NROT]

        def acc(job):
            return bank[NROT + ACCNO[job] % 2]

        def tok(t):
            return slice(t * P, (t + 1) * P)

        def over(ap, n, axis):
            a = ap.unsqueeze(axis)
            return a.broadcast_to([n if i == axis else d for i, d in enumerate(a.shape)])

        xs = [ar(8 * b, GT, SEQ) for b in range(2)]
        bcT = [ar(8 * b + 4, 2, SEQ) for b in range(2)]
        cva = [ar(6 + b, SEQ) for b in range(2)]
        btok = ar(14, NT, P)
        cbm = ar(15, NT, P)
        zs = ar(16, GT, SEQ)
        xdt = [ar(20 + b, HPG, HD) for b in range(2)]
        xde = [ar(22 + b, HPG, HD) for b in range(2)]
        dtf = ar(24, SEQ)[0:HEADS]
        dat = ar(24, HPG, P)
        dec = [ar(26 + 2 * b, HPG, P) for b in range(2)]
        ytok = ar(30, NT, SEQ)
        prev = [ar(34 + b, HPG, HD) for b in range(2)]
        yoe = ar(36, HPG, HD)
        ysq = ar(37, SEQ)
        yac = ar(38, SEQ)
        ysq2 = ar(36, SEQ)
        dtb = ar(39, NT, HEADS)
        da = ar(39.25, NT, HEADS)
        dtmp = ar(39.5, NT, HEADS)
        dtmp2 = ar(39.75, NT, HEADS)
        cums = sb("cums", [P, 3, NT * HEADS])
        aneg = sb("aneg", [P, HEADS])

        pp = [ar(0, KD, SEQ), ar(4, KD, SEQ), ar(8, KD, SEQ)]
        gsig = [ar(16 + b, SEQ) for b in range(2)]
        rtb = ar(38, SEQ)
        rtb1 = ar(35, SEQ)
        hf = [ar(20 + b, SEQ) for b in range(4)]
        hf2 = [ar(35 + b, SEQ) for b in range(4)]
        hf3 = [ar(30 + b, SEQ) for b in range(4)]

        def normed_tiles(name):
            return {"ssm": hf2, "kv": hf3, "attn": hf3}.get(name, hf)


        vtok = ar(0, NT, 256)
        kT = ar(2, 2, SEQ)
        qT = ar(4, KD, SEQ)
        qr = ar(12, NT, 1024)
        kr = ar(20, NT, 256)
        ctab = ar(22, 4, 256)
        rtmp = ar(24, 8, P)
        qsq = [ar(26 + b, SEQ) for b in range(2)]
        qn = [ar(28 + b, SEQ) for b in range(2)]
        ra = [ar(30 + b, SEQ) for b in range(2)]
        rb = [ar(24 + b, SEQ) for b in range(2)]
        PTb = [ar(20 + 2 * b, 2, SEQ) for b in range(2)]
        gs = ar(32, KD, SEQ)
        Sb = [ar(12 + 2 * b, 4, 256) for b in range(3)]
        ogf = [ar(18 + b, 4, P) for b in range(2)]
        small = sb("small", [P, 12, 16])
        flat = small[:, :, :].rearrange("p a b -> p (a b)")
        tiny = sb("tiny", [P, 1])
        nrm = sb("nrm", [P, 4, NT])
        mst = cums[:, 0, 0:6 * M_HEADS * NT].rearrange("p (a b) -> p a b", a=6)
        negsink = sb("negsink", [P, ATT_HEADS])

        mqT = ar(0, 4, SEQ)
        moT = ar(4, 4, SEQ)
        mkT = ar(8, 4, SEQ)
        mvt = ar(12, NT, SEQ)
        aqT = ar(16, 4, SEQ)
        akT = ar(20, 2, SEQ)
        avt = ar(22, NT, 256)
        ckv = ar(24, 2, SEQ)
        chid = ar(24, 2, 64)
        ctm = ar(24.25, 3, 64)
        vct = ar(24.75, 2, HD)[0:NC_BLK]
        scb = [ar(25 + b / 4, 4, NC_BLK) for b in range(2)]
        kcT = ar(25.5, NC_BLK)
        cblk = [ar(26 + 4 * b, CMP_BLOCK, 2 * NC_BLK) for b in range(2)]
        wt = [ar(26 + b, SEQ) for b in range(2)]
        wk = [ar(28 + b, SEQ) for b in range(2)]
        Mneg = [ar(30, SEQ), ar(36, SEQ)]
        hm = ar(31, 4, SEQ)
        mdiag = [rt[:, :], ssacc[:, :]]
        sel = ar(37, 4, P)
        cmpbf = ar(38, NCMP)
        cmpb = cmpbf.rearrange("p (n h c) -> p n h c", n=NT, h=A_HEADS)
        alibi = ar(8, A_HEADS, SEQ)
        nSb = [ar(26, 4, SEQ), ar(0, 4, SEQ)]
        nPb = [ar(b, SEQ) for b in (30, 35, 36, 37)]
        mrow = [sq[0:4, 0, :], sq[0:4, 1, :], sq[0:4, 2, :], ssacc[0:4, :], rt[0:4, :]]
        gat = sb("gat", [P, NT, 24])
        gif = sb("gif", [P, NT, 8])
        rcol = sb("rcol", [P, NT, 4])
        fca = [ar(22 + b, SEQ) for b in range(2)]
        fg = [ar(26 + b, SEQ) for b in range(2)]
        fsl = [ar(24 + b, SEQ) for b in range(2)]
        res = ar(0, KD, SEQ)

        block = ctx.enter_context(nc.Block())

        @block.sync
        def _(sp):
            for m in range(0, KD, 4):
                sp.dma_start(h[:, m:m + 2, :], ins["xT"][:, m:m + 2, :])\
                    .then_inc(*done(f"xin{m}", ("h", 0, m), ("h", 0, m + 1), inc=16))
            sp.wait_ge(*at("h", 0, 4))
            for L, b in enumerate(BLOCKS):
                if L >= NSLOT:
                    sp.wait_ge(*at("slot_free", L - NSLOT))
                sp.dma_start(ring[:, L % NSLOT, :], ins["wstream"][L]).then_inc(*done(f"loaded{L % NSLOT}", ("loaded", L), inc=16))
            for m in range(KD):
                sp.wait_ge(*at("result", m))
                sp.dma_start(out[m], res[:, m, :]).then_inc(*done("stored", ("stored", m), inc=16))
            sp.wait_ge(*at("stored", KD - 1))

        @block.gpsimd
        def _(pool):
            nc.gpsimd.memset(eps[:, :], EPS)
            nc.gpsimd.memset(halfpi[:, :], float(np.pi / 2)).then_inc(*done("eps_set", ("eps",)))

            def low(dst, src, hi):
                return nc.gpsimd.tensor_tensor(dst, src, hi.bitcast(F32), ALU.subtract)

            for number, step in enumerate(STEPS):
                (hnh, hnl), (xgh, xgl) = roles(number)
                k, a = step[0], step[1:]
                for b, n in splits_at(step):
                    L = BLKNO[b]
                    src = ring[:, L % NSLOT, :]
                    if n is not None:
                        pool.wait_ge(*at("high", L))
                        low(wsl[n % NSET][:, :], src, wsh[n % NSET][:, :])\
                            .then_inc(*done("split", ("split", L), ("slot_free", L)))
                if k == "hn" and a[0] != "final":
                    for name in a:
                        hi, lo = (xgh, xgl) if name == "kv" else (hnh, hnl)
                        buf = normed_tiles(name)
                        for m in range(1, KD, 2):
                            pool.wait_ge(*at("hnhi", name, m))
                            low(lo[:, m, :], buf[m % 4], hi[:, m, :]).then_inc(*done("hn", ("hn", name, m)))
                if k == "he" and a[1] % 2:
                    name, m = a
                    pool.wait_ge(*at("hnhi", name, m))
                    hi, lo = (xgh, xgl) if name in ("kv", "ln1") else (hnh, hnl)
                    low(lo[:, m, :], normed_tiles(name)[m % 4], hi[:, m, :]).then_inc(*done("hn", ("hn", name, m)))
                if k == "gb":
                    g = a[0]
                    for m in range(1, GT, 2):
                        pool.wait_ge(*at("ynhi", g, m))
                        low(xgl[:, GT * (g % 2) + m, :], xs[g % 2][:, m, :], xgh[:, GT * (g % 2) + m, :]).then_inc(*done("yn", ("yn", g, m)))
                if k == "aO":
                    n, G2 = a[0], a[1] // 2
                    pool.wait_ge(*at("oghi", n, G2))
                    low(xgl[:, 4 * G2:4 * G2 + 4, tok(n)], ogf[G2], xgh[:, 4 * G2:4 * G2 + 4, tok(n)])\
                        .then_inc(*done("og", ("og", n, G2)))
                if k == "fh":
                    m = a[0]
                    pool.wait_ge(*at("ffhi", m))
                    low(xgl[:, m % 8, :], fsl[m % 2], xgh[:, m % 8, :]).then_inc(*done("ff", ("ff", m)))

                def masked(n):
                    g, c = divmod(n, NT)
                    if n >= 1:
                        pool.wait_ge(*at("mm", "seg", (n - 1) // NT, (n - 1) % NT, 1))
                    nc.gpsimd.tensor_tensor(dat, over(tri, HPG, 1),
                                            over(da[:, c, g * HPG:(g + 1) * HPG], P, 2), ALU.mult)\
                        .then_inc(*done("dat", ("dat", g, c)))

                if k == "cum":
                    pool.wait_ge(*at("consts"))
                    pool.wait_ge(*at("da"))
                    masked(0)
                if k == "ssd1":
                    g, c = a
                    pool.wait_ge(*at("xdt", g, c))
                    pool.wait_ge(*at("cums"))
                    if c < NT - 1:
                        nc.gpsimd.tensor_tensor(xde[c % 2], xdt[c % 2],
                                                over(cums[:, 1, c * HEADS + g * HPG:c * HEADS + (g + 1) * HPG], HD, 2),
                                                ALU.mult).then_inc(*done("xde", ("xde", g, c)))
                    if g * NT + c + 1 < GROUPS * NT:
                        masked(g * NT + c + 1)
                if k == "ssd2":
                    g, c = a
                    if 1 <= c < NT - 1:
                        pool.wait_ge(*at("prev", g, c))
                        nc.gpsimd.tensor_tensor(prev[(c + 1) % 2], prev[c % 2],
                                                over(cums[:, 2, c * HEADS + g * HPG:c * HEADS + (g + 1) * HPG], HD, 2),
                                                ALU.mult).then_inc(*done("pdec", ("pdec", g, c)))
                if k == "norm" and a[0] == 3:
                    for j in range(2):
                        nc.gpsimd.memset(cblk[j], 0.0).then_inc(*done("czero", ("czero", j)))
                if k == "ro":
                    stage, t = a
                    b = t % 2
                    nh = 8 if stage else 4
                    cs = ctab[:, 0 if stage else 2, :].rearrange("p (t d) -> p t d", t=NT)[:, t, :]
                    pool.wait_ge(*at("qn", *a))
                    nc.gpsimd.tensor_tensor(ra[b][:, 0:nh * HD].rearrange("p (h d) -> p h d", h=nh),
                                            qn[b][:, 0:nh * HD].rearrange("p (h d) -> p h d", h=nh),
                                            over(cs, nh, 1), ALU.mult).then_inc(*done("ropea", ("ropea", *a)))
                if k == "aR":
                    n, g = a
                    u = n * KV_HEADS + g
                    w = P if n == 0 else 256
                    pool.wait_ge(*at("arec", n, g))
                    s = Sb[u % 3][:, :, 0:w]
                    nc.gpsimd.tensor_tensor(s, s, over(small[:, 4 * (u % 3) + 3, 0:4], w, 2), ALU.mult)\
                        .then_inc(*done("aprob", ("aprob", n, g)))
                if k == "mB":
                    for s in range(NT):
                        pool.wait_ge(*at("wt", a[0], s))
                        b = (a[0] * NT + s) % 2
                        nc.gpsimd.tensor_tensor(wk[b][:, 0:P], wk[b][:, 0:P], tri, ALU.mult)\
                            .then_inc(*done("wtm", ("wtm", a[0], s)))
                if k == "mg":
                    h_ = a[0]
                    pool.wait_ge(*at("mixhi", h_))
                    low(xgl[:, h_, :], hm[:, h_, :], xgh[:, h_, :]).then_inc(*done("mix", ("mix", h_)))
                if k == "nR" and a[2] != "c":
                    u = NSEQ[a]
                    w = P * (a[0] + 1)
                    pool.wait_ge(*at("nrec", *a))
                    s = nSb[u % 2][:, :, 0:w]
                    nc.gpsimd.tensor_tensor(s, s, over(small[:, 4 * "csw".index(a[2]) + 3, 0:4], w, 2), ALU.mult)\
                        .then_inc(*done("nprob", ("nprob", *a)))

        @block.scalar
        def _(act):
            for m in range(2, KD, 4):
                act.dma_start(h[:, m:m + 2, :], ins["xT"][:, m:m + 2, :])\
                    .then_inc(*done(f"xin{m}", ("h", 0, m), ("h", 0, m + 1), inc=16))
            for i, (dst, name) in enumerate([(con[:, :], "con"), (vec[:, :], "vec"), (rowb[:, :], "rowb"),
                                             (w2c[:, :, :], "w2c"),
                                             (peT[:, :, :], "peT"), (mbias[:, :], "mbias"), (pos[:, :], "pos")]):
                act.dma_start(dst, ins[name]).then_inc(*done("consts", *([("consts",)] if i == 6 else []), inc=16))
            chain = [0]

            def link(ins_):
                chain[0] += 1
                ins_.then_inc(*done("act_step", ("act_step", chain[0])))
                act.wait_ge(*at("act_step", chain[0]))

            def square(ver, m):
                n = KD * ver + m
                if n >= 3:
                    v, q = divmod(n - 3, KD)
                    if q == KD - 1:
                        act.wait_ge(*at("mm", "ss", v))
                    else:
                        act.wait_ge(*at("ssadd", v, max(q, 1)))
                act.wait_ge(*at("h", ver, m))
                nc.scalar.activation(sq[:, n % 3, :], h[:, m, :], ACT.Square).then_inc(*done("sq", ("sq", ver, m)))

            conv_open = []

            def silu_open():
                if conv_open:
                    g, i = conv_open.pop()
                    act.wait_ge(*at("conv", g, i))
                    if g >= 2:
                        if i < 2:
                            act.wait_ge(*at("mm", "yd", g - 2, 3))
                        else:
                            act.wait_ge(*at("yn", g - 2, i - 2))
                    dst = bcT[g % 2][:, i, :] if i < 2 else xs[g % 2][:, i - 2, :]
                    nc.scalar.activation(dst, cva[(g * 6 + i) % 2], ACT.Silu)\
                        .then_inc(*done("silu", ("xbc", g, i), ("conv_used", g * 6 + i)))

            for number, step in enumerate(STEPS):
                (hnh, hnl), (xgh, xgl) = roles(number)
                k, a = step[0], step[1:]
                if k == "ple" and a[1]:
                    square(2 * a[0] + 2 if a[0] < 2 else 7, a[1] - 1)
                for b, n in splits_at(step):
                    L = BLKNO[b]
                    act.wait_ge(*at("loaded", L))
                    src = ring[:, L % NSLOT, :]
                    if n is None:
                        act.wait_ge(*at("mm", *[("proj", 3, 9), ("gate", KD - 1), ("upv", FT - 1)][b[1]]))
                        nc.scalar.activation(hnh[:, 6:8, :], src.rearrange("p (a b) -> p a b", a=2), ACT.Copy)\
                            .then_inc(*done("high", ("high", L)))
                    else:
                        if n >= NSET:
                            act.wait_ge(*at("set_free", n - NSET))
                        nc.scalar.activation(wsh[n % NSET][:, :], src, ACT.Copy).then_inc(*done("high", ("high", L)))
                if k == "load":
                    for m in range(KD):
                        square(0, m)
                    act.wait_ge(*at("eps"))
                    act.wait_ge(*at("consts"))
                if k == "norm" and a[0] == 4:
                    act.wait_ge(*at("h", 4, KD - 1))
                    act.dma_start(cmpbf, ins["cmpb"]).then_inc(*done("cmp_in_dma", inc=16))
                    act.dma_start(sel[0:4, :, :], ins["sel"]).then_inc(*done("cmp_in_dma", ("cmpb",), inc=16))
                if k == "norm":
                    link(nc.scalar.activation(tiny[:, :], eps[:, :], ACT.Sqrt))
                    act.wait_ge(*at("mm", "ss", a[0]))
                    nc.scalar.activation(nrm[:, 0, :], acc(("ss", a[0]))[:, 0:NT], ACT.Sqrt, bias=eps[:, 0:1], scale=1.0 / D)\
                        .then_inc(*done("rms", ("rms", a[0]), ("accfree", "ss", a[0])))
                if k == "hn" and a[0] != "final":
                    for name in a:
                        hi = xgh if name == "kv" else hnh
                        buf = normed_tiles(name)
                        for m in range(KD):
                            act.wait_ge(*at("hf", name, m))
                            nc.scalar.activation(hi[:, m, :], buf[m % 4], ACT.Copy).then_inc(*done("hnhi", ("hnhi", name, m)))
                if k == "he":
                    name, m = a
                    act.wait_ge(*at("hf", name, m))
                    if name[:3] == "ple" and m == 6:
                        act.wait_ge(*at("mm", "pp", int(name[3]), KD - 1))
                    hi = xgh if name in ("kv", "ln1") else hnh
                    nc.scalar.activation(hi[:, m, :], normed_tiles(name)[m % 4], ACT.Copy)\
                        .then_inc(*done("hnhi", ("hnhi", name, m)))
                if k == "proj":
                    g, i = a
                    b = ps(step)
                    act.wait_ge(*at("mm", *step))
                    if i < 6:
                        ch = [16 + g, 20 + g][i] if i < 2 else GT * g + i - 2
                        n = g * 6 + i
                        if n >= 2:
                            act.wait_ge(*at("conv_used", n - 2))
                        nc.scalar.activation(cva[n % 2], b[:, :], ACT.Identity, bias=vec[:, V_CB + ch:V_CB + ch + 1],
                                             scale=vec[:, V_CW + 3 * 24 + ch:V_CW + 3 * 24 + ch + 1])\
                            .then_inc(*done("conv0", ("conv0", g, i)))
                        silu_open()
                        conv_open.append((g, i))
                    else:
                        silu_open()
                        if g >= 1:
                            act.wait_ge(*at("ygated", g - 1, i - 6))
                        nc.scalar.activation(zs[:, i - 6, :], b[:, :], ACT.Silu)\
                            .then_inc(*done("zs", ("zs", g, i - 6), ("free", *step)))
                if k == "dtl":
                    act.wait_ge(*at("mm", "dtl"))
                    nc.scalar.activation(dtf, ps(step)[0:HEADS, :], ACT.Copy).then_inc(*done("dtf", ("dtf",), ("free", "dtl")))
                if k == "dt":
                    nc.scalar.activation(aneg[:, :], rowb[:, R_ALOG:R_ALOG + HEADS], ACT.Exp).then_inc(*done("aexp", ("aexp",)))
                    act.wait_ge(*at("dtabs"))
                    link(nc.scalar.activation(dtmp2, dtmp2, ACT.Exp))
                    nc.scalar.activation(dtmp2, dtmp2, ACT.Ln, bias=1.0).then_inc(*done("dtln", ("dtln",)))
                if k == "cum":
                    act.wait_ge(*at("mm", "cum"))
                    nc.scalar.activation(cums[:, :, :], ps(("cum",))[:, 0:3 * P].rearrange("p (a b) -> p a b", a=3), ACT.Exp)\
                        .then_inc(*done("cums", ("cums",), ("free", "cum")))
                if k == "ssd0":
                    act.wait_ge(*at("mm", "bt", *a))
                    if a[0] >= 1:
                        act.wait_ge(*at("mm", "st", a[0] - 1, 2))
                    nc.scalar.activation(btok, ps(("bt", *a))[:, :].rearrange("p (a b) -> p a b", a=NT), ACT.Copy)\
                        .then_inc(*done("btok", ("btok", *a), ("free", "bt", *a)))
                if k == "ssd1":
                    g, c = a
                    n = g * NT + c
                    for j in range(2):
                        act.wait_ge(*at("mm", "seg", g, c, j))
                        if n >= 2:
                            act.wait_ge(*at("mm", "yd", (n - 2) // NT, (n - 2) % NT))
                        nc.scalar.activation(dec[c % 2][:, 4 * j:4 * j + 4, :],
                                             ps(("seg", g, c, j))[:, :].rearrange("p (a b) -> p a b", a=4), ACT.Exp)\
                            .then_inc(*done("dec", ("dec", g, c, j), ("free", "seg", g, c, j)))
                if k == "ssd2" and a[1] == 0:
                    g, c = a
                    act.wait_ge(*at("mm", "yd", g, 0))
                    if g >= 1:
                        act.wait_ge(*at("mm", "yt", g - 1, 3))
                    nc.scalar.activation(ytok[:, 0, :], ps(("yd", g, 0))[:, :], ACT.Copy)\
                        .then_inc(*done("ytok0", ("ytok", g, 0), ("free", "yd", g, 0)))
                    act.wait_ge(*at("mm", "st", g, 0))
                    if g >= 1:
                        act.wait_ge(*at("mm", "yo", g - 1, 3))
                    nc.scalar.activation(prev[1], ps(("st", g, 0))[:, :].rearrange("p (a b) -> p a b", a=HPG), ACT.Copy)\
                        .then_inc(*done("prev1", ("prev", g, 1), ("free", "st", g, 0)))
                if k == "yt":
                    g, m = a
                    act.wait_ge(*at("ygated", g, m))
                    if m == 3:
                        act.wait_ge(*at("yadd", g, 1))
                    nc.scalar.activation([yac, ysq, ysq2, ysq][m], xs[g % 2][:, m, :], ACT.Square)\
                        .then_inc(*done("ysq", ("ysq", g, m)))
                if k == "gn":
                    g = a[0]
                    link(nc.scalar.activation(tiny[:, :], eps[:, :], ACT.Sqrt))
                    act.wait_ge(*at("mm", "gn", g))
                    nc.scalar.activation(nrm[:, 2, :], ps(step)[:, 0:NT], ACT.Sqrt, bias=eps[:, 0:1], scale=1.0 / 512)\
                        .then_inc(*done("grms", ("grms", g), ("free", *step)))
                if k == "gb":
                    g = a[0]
                    if g >= 2:
                        act.wait_ge(*at("mm", "sout", g - 2, KD - 1))
                    for m in range(GT):
                        act.wait_ge(*at("ynf", g, m))
                        nc.scalar.activation(xgh[:, GT * (g % 2) + m, :], xs[g % 2][:, m, :], ACT.Copy).then_inc(*done("ynhi", ("ynhi", g, m)))
                if k == "pp":
                    i, m = a
                    act.wait_ge(*at("mm", *step))
                    if i == 0 and m == 0:
                        act.wait_ge(*at("yn", 2, 3))
                    nc.scalar.activation(pp[i][:, m, :], ps(step)[:, :], ACT.Copy)\
                        .then_inc(*done("pp", ("pp", i, m), ("free", *step)))
                if h_update(step):
                    square(h_update(step), a[1])
                if k == "ple":
                    i, m = a
                    act.wait_ge(*at("gscaled", i, m))
                    nc.scalar.activation(gsig[m % 2], gsig[m % 2], ACT.Sigmoid).then_inc(*done("gsig", ("gsig", i, m)))
                    if m == KD - 1:
                        square(2 * i + 2 if i < 2 else 7, m)
                if k == "rope_tables":
                    act.wait_ge(*at("angles"))
                    nc.scalar.activation(rtmp[:, 4, :], rtmp[:, 2, :], ACT.Sin).then_inc(*done("sincos", ("sin",)))
                    nc.scalar.activation(rtmp[:, 5, :], rtmp[:, 3, :], ACT.Sin, scale=-1.0, bias=halfpi[:, 0:1])\
                        .then_inc(*done("sincos", ("cos",)))
                if k in ("kv", "q") and a[-1] == 3:
                    w = 256 if k == "kv" else 512
                    stage = 0 if k == "kv" else 1 + a[0]
                    act.wait_ge(*at("ndiag", 2))
                    for t in range(NT):
                        key = (k, *a[:-1], t)
                        root = nrm[:, 1, t:t + 1] if k == "kv" else 1.0
                        act.wait_ge(*at("mm", *key))
                        n = stage * NT + t
                        if n >= 2:
                            act.wait_ge(*at("qss", n - 2))
                        if k == "kv":
                            nc.scalar.activation(vtok[:, t, :], ps(key)[:, 256:512], ACT.Identity, scale=root)
                        nc.scalar.activation(qsq[t % 2][:, 0:w], ps(key)[:, 0:w], ACT.Square, scale=root)\
                            .then_inc(*done("qsq", ("qsq", *key)))
                    act.wait_ge(*at("qss", stage * NT + NT - 1))
                    lo, nh = 96 * (stage % 2), NT * w // HD
                    nc.scalar.activation(flat[:, lo + 32:lo + 32 + nh], flat[:, lo:lo + nh], ACT.Sqrt,
                                         bias=eps[:, 0:1], scale=1.0 / HD).then_inc(*done("qrms", ("qrms", stage)))
                if k == "kT":
                    for t in range(NT):
                        act.wait_ge(*at("mm", "kT", t))
                        nc.scalar.activation(kT[:, :, tok(t)], ps(("kT", t))[:, 0:256].rearrange("p (a b) -> p a b", a=2),
                                             ACT.Copy).then_inc(*done("kT", ("kT", t), ("free", "kT", t)))
                if k == "qT":
                    for t in range(NT):
                        key = ("qT", a[0], t)
                        act.wait_ge(*at("mm", *key))
                        nc.scalar.activation(qT[:, 4 * a[0]:4 * a[0] + 4, tok(t)],
                                             ps(key)[:, :].rearrange("p (a b) -> p a b", a=4), ACT.Copy,
                                             scale=HD ** -0.5).then_inc(*done("qT", key, ("free", *key)))
                if k == "gate":
                    act.wait_ge(*at("mm", *step))
                    nc.scalar.activation(gs[:, a[0], :], ps(step)[:, :], ACT.Silu)\
                        .then_inc(*done("gs", ("gs", a[0]), ("free", *step)))
                if k == "aE":
                    n, g = a
                    u = n * KV_HEADS + g
                    w = P if n == 0 else 256
                    act.wait_ge(*at("anegm", n, g))
                    sm = small[:, 4 * (u % 3):4 * (u % 3) + 4, :]
                    for r in range(4):
                        last = nc.scalar.activation(Sb[u % 3][:, r, 0:w], Sb[u % 3][:, r, 0:w], ACT.Exp,
                                                    bias=sm[:, 1, r:r + 1], accum_out=sm[:, 2, r:r + 1])
                    last.then_inc(*done("aexpd", ("aexpd", n, g)))
                    nc.scalar.activation(sm[:, 1, 8:12], sm[:, 1, 4:8], ACT.Exp).then_inc(*done("aexpd", ("aesink", n, g)))
                if k == "aT":
                    n, g = a
                    u = n * KV_HEADS + g
                    act.wait_ge(*at("mm", "aPT", n, g, 0))
                    if u >= 2:
                        act.wait_ge(*at("pv", *divmod(u - 2, KV_HEADS)))
                    nc.scalar.activation(PTb[u % 2][:, 0, :], ps(("aPT", n, g, 0))[:, :], ACT.Copy)\
                        .then_inc(*done("aPT_act", ("aPT", n, g, 0), ("free", "aPT", n, g, 0)))
                if k == "aO":
                    n, G2 = a[0], a[1] // 2
                    act.wait_ge(*at("ogf", n, G2))
                    nc.scalar.activation(xgh[:, 4 * G2:4 * G2 + 4, tok(n)], ogf[G2], ACT.Copy)\
                        .then_inc(*done("oghi", ("oghi", n, G2)))
                if k == "mlog":
                    act.wait_ge(*at("mfabs"))
                    link(nc.scalar.activation(mrow[2], mrow[2], ACT.Exp))
                    nc.scalar.activation(mrow[2], mrow[2], ACT.Ln, bias=1.0)\
                        .then_inc(*done("mfln", ("mfln",)))
                if k == "mexp":
                    act.wait_ge(*at("mmt"))
                    nc.scalar.activation(mrow[4], mrow[2], ACT.Exp, scale=-1.0)\
                        .then_inc(*done("mexp", ("men",)))
                if k == "mrcol":
                    act.wait_ge(*at("mm", "mrcol"))
                    nc.scalar.activation(rcol[:, :, :], ps(("mrcol",))[:, 0:16].rearrange("p (a b) -> p a b", a=4), ACT.Copy)\
                        .then_inc(*done("rcol", ("rcol",), ("free", "mrcol")))
                if k in ("mv", "avg") and a[0] == 3:
                    act.wait_ge(*at("ndiag", 4))
                    for t in range(NT):
                        root = nrm[:, 1, t:t + 1]
                        act.wait_ge(*at("mm", k, t))
                        if k == "mv":
                            nc.scalar.activation(mvt[:, t, :], ps((k, t))[:, :], ACT.Identity, scale=root)\
                                .then_inc(*done("mv", ("mv", t), ("free", k, t)))
                        else:
                            nc.scalar.activation(avt[:, t, :], ps((k, t))[:, 0:256], ACT.Identity, scale=root)
                            nc.scalar.activation(gif[:, t, :], ps((k, t))[:, 280:288], ACT.Identity, scale=root)
                            nc.scalar.activation(gat[:, t, :], ps((k, t))[:, 256:280], ACT.Sigmoid, scale=root)\
                                .then_inc(*done("avg", ("avg", t), ("free", k, t)))
                if k == "mo":
                    act.wait_ge(*at("scaled", *step))
                    nc.scalar.activation(moT[:, a[0], :], moT[:, a[0], :], ACT.Sigmoid).then_inc(*done("mo", ("done", *step)))
                if k == "cmp":
                    act.wait_ge(*at("gelu_in", a[0]))
                    nc.scalar.activation(ctm[:, 1, :], ctm[:, 1, :], ACT.Tanh, scale=float(np.sqrt(2 / np.pi)))\
                        .then_inc(*done("ctanh", ("ctanh", a[0])))
                if k == "cmp2":
                    act.wait_ge(*at("mm", "ckT"))
                    nc.scalar.activation(kcT[:, :], ps(("ckT",))[:, 0:NC_BLK], ACT.Copy).then_inc(*done("kcT", ("kcT",), ("free", "ckT")))
                    act.wait_ge(*at("mm", "cv"))
                    nc.scalar.activation(vct[:, :, :], ps(("cv",))[0:NC_BLK, 0:128].rearrange("p (a b) -> p a b", a=2), ACT.Copy)\
                        .then_inc(*done("vct", ("vct",), ("free", "cv")))

                def negated(h_):
                    act.wait_ge(*at("mm", "Mb", h_))
                    if h_ >= 2:
                        act.wait_ge(*at("marg", h_ - 2, NT - 1))
                    nc.scalar.activation(Mneg[h_ % 2], ps(("Mb", h_))[:, :], ACT.Copy, scale=-1.0)\
                        .then_inc(*done("Mneg", ("Mneg", h_), ("free", "Mb", h_)))

                def mexp(n):
                    h_, s = divmod(n, NT)
                    if h_ < M_HEADS:
                        act.wait_ge(*at("marg", h_, s))
                        nc.scalar.activation(wt[n % 2][:, 0:SEQ - P * s], wt[n % 2][:, 0:SEQ - P * s], ACT.Exp)\
                            .then_inc(*done("mexpd", ("mexpd", h_, s)))

                if k == "mA":
                    act.wait_ge(*at("mm", "ecol"))
                    nc.scalar.activation(mst[:, 0, :].rearrange("p (h t) -> p t h", t=NT),
                                         ps(("ecol",))[:, 0:16].rearrange("p (t h) -> p t h", t=NT), ACT.Copy)\
                        .then_inc(*done("ecol", ("ecol",), ("free", "ecol")))
                    negated(0)
                    mexp(0)
                if k == "mB":
                    h_ = a[0]
                    if h_ + 1 < M_HEADS:
                        negated(h_ + 1)
                    for s in range(NT):
                        mexp(h_ * NT + s + 1)
                    if h_ == M_HEADS - 1:
                        act.wait_ge(*at("mm", "KQ", h_, NT - 1))
                        act.dma_start(alibi[:, 0:4, :], ins["alibi"][:, 0:4, :]).then_inc(*done("alibi_in0", ("alibi", 0), inc=16))
                    act.wait_ge(*at("mden", h_))
                    if h_ == M_HEADS - 1:
                        act.dma_start(alibi[:, 4:8, :], ins["alibi"][:, 4:8, :]).then_inc(*done("alibi_in1", ("alibi", 1), inc=16))
                    nc.scalar.activation(mqT[:, h_, :], ps(("num", h_))[:, :], ACT.Square).then_inc(*done("msq", ("msq", h_)))
                    nc.scalar.activation(hm[:, h_, :], ps(("num", h_))[:, :], ACT.Copy)\
                        .then_inc(*done("hm", ("hm", h_), ("free", "num", h_)))
                if k == "mfac":
                    act.wait_ge(*at("mvar"))
                    nc.scalar.activation(mst[:, 4, :], mst[:, 3, :], ACT.Sqrt, bias=eps[:, 0:1], scale=1.0 / P)\
                        .then_inc(*done("mrms", ("mrms",)))
                if k == "mg":
                    h_ = a[0]
                    act.wait_ge(*at("mgated", h_))
                    nc.scalar.activation(xgh[:, h_, :], hm[:, h_, :], ACT.Copy).then_inc(*done("mixhi", ("mixhi", h_)))
                if k == "nE":
                    i, g, br = a
                    u = NSEQ[a]
                    act.wait_ge(*at("nnegm", *a))
                    q = 4 * "csw".index(br)
                    sm = small[:, q:q + 4, :]
                    if br == "c":
                        nc.scalar.activation(scb[g][:, :, :], scb[g][:, :, :], ACT.Exp).then_inc(*done("nexp", ("nexp", *a)))
                    else:
                        w = P * (i + 1)
                        for r in range(4):
                            last = nc.scalar.activation(nSb[u % 2][:, r, 0:w], nSb[u % 2][:, r, 0:w], ACT.Exp,
                                                        bias=sm[:, 1, r:r + 1], accum_out=sm[:, 2, r:r + 1])
                        last.then_inc(*done("nexp", ("nexp", *a)))
                if k == "nT":
                    for kt in range(1 if a[2] == "c" else a[0] + 1):
                        n = NPT[(*a, kt)]
                        if n % 2 == 0:
                            act.wait_ge(*at("mm", "nPT", *a, kt))
                            if n >= 4:
                                act.wait_ge(*at("npv", n - 4))
                            rows = NC_BLK if a[2] == "c" else P
                            nc.scalar.activation(nPb[n % 4][0:rows, :], ps(("nPT", *a, kt))[0:rows, :], ACT.Copy)\
                                .then_inc(*done("nPT_act", ("nPT", *a, kt), ("free", "nPT", *a, kt)))
                if k == "nO":
                    act.wait_ge(*at("nO", a[0]))
                    nc.scalar.activation(xgh[:, 4:8, tok(a[0])], acc(("nO", a[0]))[:, :].rearrange("p (a b) -> p a b", a=4),
                                         ACT.Copy).then_inc(*done("noghi", ("noghi", a[0])))
                if k == "upg":
                    m = a[0]
                    act.wait_ge(*at("fscaled", m))
                    if m >= 2:
                        act.wait_ge(*at("fsilu", m - 2))
                    nc.scalar.activation(fca[m % 2], fg[m % 2], ACT.Identity, bias=vec[:, V_C2B + m:V_C2B + m + 1],
                                         scale=vec[:, V_C2W + 2 * FT + m:V_C2W + 2 * FT + m + 1])\
                        .then_inc(*done("fconv0", ("fconv0", m)))
                if k == "upv":
                    m = a[0]
                    act.wait_ge(*at("fconv", m))
                    if m >= 2:
                        act.wait_ge(*at("ff", m - 2))
                    nc.scalar.activation(fsl[m % 2], fca[m % 2], ACT.Silu).then_inc(*done("fsilu", ("fsilu", m)))
                if k == "fh":
                    m = a[0]
                    act.wait_ge(*at("fff", m))
                    if m >= 8:
                        act.wait_ge(*at("mm", "dn", m // 4 - 2, KD - 1))
                    nc.scalar.activation(xgh[:, m % 8, :], fsl[m % 2], ACT.Copy).then_inc(*done("ffhi", ("ffhi", m)))

        @block.tensor
        def _(pe):
            pe.wait_ge(*at("consts"))

            def open_bank(job):
                n = JOBNO[job]
                if n >= NROT:
                    pe.wait_ge(*at("free", *JOBS[n - NROT]))
                return ps(job)

            def open_acc(job):
                n = ACCNO[job]
                if n >= 2:
                    pe.wait_ge(*at("accfree", *ACCS[n - 2]))
                return acc(job)

            def weights(name):
                pe.wait_ge(*at("split", BLKNO[name]))
                n = SPLITNO[name] % NSET
                return wsh[n], wsl[n]

            def used(name, *more):
                return done("mm", ("set_free", SPLITNO[name]), *more)

            def mm(*args, **kw):
                return nc.tensor.matmul(*args, **kw)

            def mm3(o, w, x, start, stop):
                mm(o, w[0], x[0], start=start, stop=False)
                mm(o, w[0], x[1], start=False, stop=False)
                return mm(o, w[1], x[0], start=False, stop=stop)

            def column_sums(b, lo, src, start=True, stop=True):
                for t in range(NT):
                    last = mm(b[:, lo + t:lo + t + 1], src[:, tok(t)], ones[:, 0:1], start=start and t == 0, stop=stop,
                              skip_group_check=True)
                return last

            def linear(job, name, src, normed=None):
                b = open_bank(job)
                w = weights(name)
                for kt in range(KD):
                    if normed:
                        pe.wait_ge(*at("hn", normed, kt))
                    last = mm3(b[:, :], [q[:, tok(kt)] for q in w], [q[:, kt, :] for q in src], kt == 0, kt == KD - 1)
                last.then_inc(*used(name, ("mm", *job)))

            def quarter(job, name, src, lo, m):
                b = open_bank(job)
                w = weights(name)
                for kt in range(4):
                    last = mm3(b[:, :], [q[:, kt * 256 + (m % 2) * P:kt * 256 + (m % 2 + 1) * P] for q in w],
                               [q[:, lo + kt, :] for q in src], kt == 0, kt == 3)
                if m % 2:
                    last.then_inc(*used(name, ("mm", *job)))
                else:
                    last.then_inc(*done("mm", ("mm", *job)))

            def token_major(jobs, i, name, src, width=SEQ, normed=None):
                bs = [open_bank(j) if i == 0 else ps(j) for j in jobs]
                w = weights(name)
                for k2 in range(2):
                    if normed:
                        pe.wait_ge(*at("hn", normed, 2 * i + k2))
                    for t in range(NT):
                        fin = i == 3 and k2 == 1
                        last = mm3(bs[t][:, 0:width], [q[:, 2 * i + k2, tok(t)] for q in src],
                                   [q[:, k2 * SEQ:k2 * SEQ + width] for q in w], i + k2 == 0, fin)
                        free = k2 == 1 and t == NT - 1
                        if free:
                            last.then_inc(*used(name, *([("mm", *jobs[t])] if fin else [])))
                        elif fin:
                            last.then_inc(*done("mm", ("mm", *jobs[t])))

            for number, step in enumerate(STEPS):
                hn, xg = roles(number)
                k, a = step[0], step[1:]
                if k == "norm":
                    b = open_acc(("ss", a[0]))
                    pe.wait_ge(*at("ssadd", a[0], KD - 2))
                    column_sums(b, 0, ssacc, stop=False)
                    pe.wait_ge(*at("sq", a[0], KD - 1))
                    column_sums(b, 0, sq[:, (KD * a[0] + KD - 1) % 3, :], start=False).then_inc(*done("mm", ("mm", "ss", a[0])))
                if k == "nb":
                    b = open_acc(("rb", a[0]))
                    pe.wait_ge(*at("ndiag", a[0]))
                    mm(b[:, :], ones, rt[:, :], start=True, stop=True).then_inc(*done("mm", ("mm", "rb", a[0])))
                if k == "proj":
                    linear(step, blocks_of(step)[0], hn, "ssm" if a == (0, 0) else None)
                if k == "dtl":
                    linear(step, ("dt",), hn)
                if k == "dt":
                    b = open_bank(("dt",))
                    pe.wait_ge(*at("dtf"))
                    for t in range(NT):
                        last = nc.tensor.transpose(b[:, t * HEADS:(t + 1) * HEADS], dtf[:, tok(t)], ident[0:HEADS, 0:HEADS])
                    last.then_inc(*done("mm", ("mm", "dt")))
                if k == "cum":
                    b = open_bank(("cum",))
                    pe.wait_ge(*at("da"))
                    daf = da.rearrange("p a b -> p (a b)")
                    mm(b[:, 0:P], tri, daf, start=True, stop=True)
                    mm(b[:, P:2 * P], upper, daf, start=True, stop=True)
                    mm(b[:, 2 * P:3 * P], ones, daf, start=True, stop=True).then_inc(*done("mm", ("mm", "cum")))
                if k == "ssd0":
                    g = a[0]
                    b = open_bank(("cb", g))
                    pe.wait_ge(*at("xbc", g, 1))
                    bc = bcT[g % 2]
                    for c in range(NT):
                        last = mm(b[:, tok(c)], bc[:, 0, tok(c)], bc[:, 1, tok(c)], start=True, stop=True)
                    last.then_inc(*done("mm", ("mm", "cb", g)))
                    b = open_bank(("bt", g))
                    for c in range(NT):
                        last = nc.tensor.transpose(b[:, tok(c)], bc[:, 0, tok(c)], ident)
                    last.then_inc(*done("mm", ("mm", "bt", g)))
                if k == "ssd1":
                    g, c = a
                    b = open_bank(("xt", g, c))
                    pe.wait_ge(*at("xbc", g, 5))
                    for m in range(GT):
                        last = nc.tensor.transpose(b[:, tok(m)], xs[g % 2][:, m, tok(c)], ident)
                    last.then_inc(*done("mm", ("mm", "xt", g, c)))
                    pe.wait_ge(*at("dat", g, c))
                    for j in range(2):
                        b = open_bank(("seg", g, c, j))
                        mm(b[:, :], upper, dat[:, 4 * j:4 * j + 4, :], start=True, stop=True)\
                            .then_inc(*done("mm", ("mm", "seg", g, c, j)))
                if k == "ssd2":
                    g, c = a
                    b = open_bank(("yd", g, c))
                    pe.wait_ge(*at("decm", g, c))
                    for r in range(HPG):
                        last = mm(b[:, r * HD:(r + 1) * HD], dec[c % 2][:, r, :], xdt[c % 2][:, r, :], start=True, stop=True)
                    last.then_inc(*done("mm", ("mm", "yd", g, c)))
                    if c:
                        b = open_bank(("yo", g, c))
                        pe.wait_ge(*at("prev", g, c))
                        mm(b[:, :], bcT[g % 2][:, 1, tok(c)], prev[c % 2], start=True, stop=True)\
                            .then_inc(*done("mm", ("mm", "yo", g, c)))
                    if c < NT - 1:
                        b = open_bank(("st", g, c))
                        pe.wait_ge(*at("btok", g))
                        pe.wait_ge(*at("xde", g, c))
                        mm(b[:, :], btok[:, c, :], xde[c % 2], start=True, stop=True)\
                            .then_inc(*done("mm", ("mm", "st", g, c)))
                if k == "yt":
                    g, m = a
                    b = open_bank(step)
                    for c in range(NT):
                        pe.wait_ge(*at("ytok", g, c))
                        last = nc.tensor.transpose(b[:, tok(c)], ytok[:, c, tok(m)], ident)
                    last.then_inc(*done("mm", ("mm", *step)))
                if k == "gn":
                    b = open_bank(step)
                    pe.wait_ge(*at("yadd", a[0], 3))
                    column_sums(b, 0, yac).then_inc(*done("mm", ("mm", *step)))
                if k == "gb":
                    b = open_bank(step)
                    pe.wait_ge(*at("gdiag", a[0]))
                    mm(b[:, :], ones, ysq, start=True, stop=True).then_inc(*done("mm", ("mm", *step)))
                if k == "pp":
                    i, m = a
                    b = open_bank(step)
                    if m == 0:
                        pe.wait_ge(*at("split", BLKNO[("p", i)]))
                    w = weights(("ple_proj", i, m // 4))
                    for kt in range(2):
                        last = mm3(b[:, :], [q[:, kt * SEQ + (m % 4) * P:kt * SEQ + (m % 4 + 1) * P] for q in w],
                                   [q[:, 6 + kt, :] for q in hn], kt == 0, kt == 1)
                    if m % 4 == 3:
                        last.then_inc(*used(("ple_proj", i, m // 4), ("mm", *step)))
                    else:
                        last.then_inc(*done("mm", ("mm", *step)))
                if k == "sout":
                    g, m = a
                    if m == 0:
                        for q in range(GT):
                            pe.wait_ge(*at("yn", g, q))
                    quarter(step, ("sout", g, m // 2), xg, GT * (g % 2), m)
                if k == "dn":
                    q, m = a
                    if m == 0:
                        pe.wait_ge(*at("ff", 4 * q + 3))
                    quarter(step, ("dn", q, m // 2), xg, 4 * (q % 2), m)
                if k == "out":
                    if a == (3, 0):
                        pe.wait_ge(*at("og", NT - 1, 1))
                    if a == (5, 0):
                        pe.wait_ge(*at("mix", 3))
                        pe.wait_ge(*at("nog", NT - 1))
                    linear(step, blocks_of(step)[0], xg)
                if k == "ple":
                    linear(step, blocks_of(step)[0], hn, ["ple0", "ple1", "ple2"][a[0]] if a[1] == 0 else None)
                if k == "kv":
                    token_major([("kv", t) for t in range(NT)], a[0], step, xg, SEQ, "kv")
                if k == "q":
                    token_major([("q", a[0], t) for t in range(NT)], a[1], blocks_of(step)[0], hn)
                if k == "kT":
                    for t in range(NT):
                        b = open_bank(("kT", t))
                        pe.wait_ge(*at("roped", "kv", t))
                        for j in range(2):
                            last = nc.tensor.transpose(b[:, tok(j)], kr[:, t, tok(j)], ident)
                        last.then_inc(*done("mm", ("mm", "kT", t)))
                if k == "qT":
                    for t in range(NT):
                        b = open_bank(("qT", a[0], t))
                        pe.wait_ge(*at("roped", "q", a[0], t))
                        for j in range(4):
                            last = nc.tensor.transpose(b[:, tok(j)], qr[:, t, a[0] * SEQ + j * P:a[0] * SEQ + (j + 1) * P], ident)
                        last.then_inc(*done("mm", ("mm", "qT", a[0], t)))
                if k == "gate":
                    linear(step, blocks_of(step)[0], hn, None if a[0] else "attn")
                if k == "aS":
                    n, g = a
                    lo = HD * (g % 2)
                    if g == 0:
                        pe.wait_ge(*at("kT", n))
                        pe.wait_ge(*at("qT", 1, n))
                    w = P if n == 0 else 256
                    keys = slice(0, P) if n == 0 else slice((n - 1) * P, (n + 1) * P)
                    per = SEQ // w
                    for j in range(4 // per):
                        b = open_bank(("aS", n, g, j))
                        for r in range(per * j, per * (j + 1)):
                            last = mm(b[:, (r % per) * w:(r % per + 1) * w], qT[lo:lo + HD, 4 * (g // 2) + r, tok(n)],
                                      kT[lo:lo + HD, g // 2, keys], start=True, stop=True)
                        last.then_inc(*done("mm", ("mm", "aS", n, g, j)))
                if k == "aT":
                    n, g = a
                    u = n * KV_HEADS + g
                    nk = 1 if n == 0 else 2
                    pe.wait_ge(*at("aprob", n, g))
                    for kt in range(nk):
                        b = open_bank(("aPT", n, g, kt))
                        for r in range(4):
                            last = nc.tensor.transpose(b[:, tok(r)], Sb[u % 3][:, r, tok(kt)], ident)
                        last.then_inc(*done("mm", ("mm", "aPT", n, g, kt)))
                if k == "aV":
                    n, g = a
                    u = n * KV_HEADS + g
                    lo = HD * (g % 2)
                    nk = 1 if n == 0 else 2
                    o = open_acc(("aO", n, g // 2)) if g % 2 == 0 else acc(("aO", n, g // 2))
                    for kt in range(nk):
                        pe.wait_ge(*at("aPT", n, g, kt))
                        last = mm(o[lo:lo + HD, :], vtok[:, n - nk + 1 + kt, g * HD:(g + 1) * HD], PTb[u % 2][:, kt, :],
                                  start=(kt == 0), stop=(kt == nk - 1))
                    last.then_inc(*done("mm", ("pv", n, g)))
                if k == "mif":
                    pe.wait_ge(*at("avg", NT - 1))
                    for j, name in enumerate(("mi", "mf")):
                        b = open_bank((name,))
                        for t in range(NT):
                            last = nc.tensor.transpose(b[0:4, tok(t)], gif[:, t, 4 * j:4 * j + 4], ident)
                        last.then_inc(*done("mm", ("mm", name)))
                if k in ("mq", "mk", "mo", "aq", "ak", "cmp_in"):
                    linear(step, blocks_of(step)[0], hn)
                if k in ("mv", "avg"):
                    token_major([(k, t) for t in range(NT)], a[0], step, hn, SEQ if k == "mv" else 288,
                                "ln1" if k == "avg" else None)
                if k == "mrcol":
                    b = open_bank(("mrcol",))
                    pe.wait_ge(*at("mrrow"))
                    for t in range(NT):
                        last = nc.tensor.transpose(b[:, 4 * t:4 * t + 4], sq[0:4, 0, tok(t)], ident[0:4, 0:4])
                    last.then_inc(*done("mm", ("mm", "mrcol")))
                if k == "cmpq":
                    j, q = a
                    b = open_acc(("chid", j)) if q == 0 else acc(("chid", j))
                    pe.wait_ge(*at("cblk", j))
                    L = BLKNO[("cmp_w1", j, q)]
                    pe.wait_ge(*at("loaded", L))
                    w = ring[:, L % NSLOT, :]
                    for l in range(8):
                        last = mm(b[:, 0:2 * NC_BLK], w[:, l * P:(l + 1) * P], cblk[j][:, 8 * q + l, :],
                                  start=(q == 0 and l == 0), stop=(q == 3 and l == 7))
                    last.then_inc(*done("mm", ("slot_free", L), *([("mm", "chid", j)] if q == 3 else [])))
                if k == "cmp2":
                    b = open_bank(("ckT",))
                    pe.wait_ge(*at("gelu", 1))
                    for g in range(2):
                        last = mm(b[HD * g:HD * (g + 1), 0:NC_BLK], w2c[:, 0, :], chid[:, 0, 32 * g:32 * g + NC_BLK],
                                  start=True, stop=True)
                    last.then_inc(*done("mm", ("mm", "ckT")))
                    b = open_bank(("cv",))
                    for g in range(2):
                        last = mm(b[0:NC_BLK, HD * g:HD * (g + 1)], chid[:, 1, 32 * g:32 * g + NC_BLK], w2c[:, 1, :],
                                  start=True, stop=True)
                    last.then_inc(*done("mm", ("mm", "cv")))

                def stab(h_):
                    mm(open_bank(("Mb", h_))[:, :], sel[0:4, h_, :], mrow[1], start=True, stop=True)\
                        .then_inc(*done("mm", ("mm", "Mb", h_)))

                def keyquery(h_, s):
                    b = open_bank(("KQ", h_, s))
                    if s == 0:
                        pe.wait_ge(*at("done", "mk", h_))
                        pe.wait_ge(*at("done", "mq", h_))
                    mm(b[:, 0:SEQ - P * s], mkT[:, h_, tok(s)], mqT[:, h_, P * s:SEQ], start=True, stop=True)\
                        .then_inc(*done("mm", ("mm", "KQ", h_, s)))

                def meansq(h_):
                    pe.wait_ge(*at("msq", h_))
                    column_sums(acc(("dtok",)), NT * (M_HEADS + h_), mqT[:, h_, :], start=False).then_inc(*done("mm", ("mss", h_)))

                if k == "mA":
                    pe.wait_ge(*at("cmpb"))
                    pe.wait_ge(*at("mmt"))
                    pe.wait_ge(*at("men"))
                    b = open_bank(("ecol",))
                    for t in range(NT):
                        last = nc.tensor.transpose(b[:, 4 * t:4 * t + 4], mrow[4][:, tok(t)], ident[0:4, 0:4])
                    last.then_inc(*done("mm", ("mm", "ecol")))
                    open_acc(("dtok",))
                    stab(0)
                    for s in range(NT):
                        keyquery(0, s)
                if k == "mB":
                    h_ = a[0]
                    more = h_ + 1 < M_HEADS
                    if more:
                        stab(h_ + 1)
                    num, den = open_bank(("num", h_)), acc(("dtok",))
                    for s in range(NT):
                        if s == 2 and h_:
                            meansq(h_ - 1)
                        pe.wait_ge(*at("wtm", h_, s))
                        pe.wait_ge(*at("mv", s))
                        wb = wk[(h_ * NT + s) % 2][:, 0:SEQ - P * s]
                        mm(num[:, P * s:SEQ], mvt[:, s, h_ * P:(h_ + 1) * P], wb, start=(s == 0), stop=(s == NT - 1),
                           skip_group_check=True)
                        for t in range(s, NT):
                            last = mm(den[:, NT * h_ + t:NT * h_ + t + 1], wb[:, tok(t - s)], ones[:, 0:1],
                                      start=(h_ + s + t == 0), stop=(s == t), skip_group_check=True)
                        last.then_inc(*done("mm", ("numden", h_, s), *([("mden", h_)] if s == NT - 1 else [])))
                        if more:
                            keyquery(h_ + 1, s)
                if k == "mfac":
                    meansq(M_HEADS - 1)
                if k == "mg":
                    b = open_bank(step)
                    pe.wait_ge(*at("mdiag", a[0]))
                    mm(b[:, :], ones, mdiag[a[0] % 2], start=True, stop=True).then_inc(*done("mm", ("mm", *step)))
                if k == "nS":
                    i, g, br = a
                    lo = HD * g
                    pe.wait_ge(*at("kcT"))
                    pe.wait_ge(*at("done", "ak", 1))
                    if br == "c":
                        b = open_bank(("nS", *a, 0))
                        for r in range(4):
                            last = mm(b[:, 32 * r:32 * r + NC_BLK], aqT[lo:lo + HD, r, tok(i)], kcT[lo:lo + HD, :],
                                      start=True, stop=True)
                        last.then_inc(*done("mm", ("mm", "nS", *a, 0)))
                    else:
                        w = P * (i + 1)
                        for r in range(4):
                            b = open_bank(("nS", *a, r))
                            mm(b[:, 0:w], aqT[lo:lo + HD, r, tok(i)], akT[lo:lo + HD, "sw".index(br), 0:w],
                               start=True, stop=True).then_inc(*done("mm", ("mm", "nS", *a, r)))
                if k == "nT":
                    i, g, br = a
                    u = NSEQ[a]
                    pe.wait_ge(*at("nprob", *a))
                    for kt in range(1 if br == "c" else i + 1):
                        b = open_bank(("nPT", *a, kt))
                        for r in range(4):
                            if br == "c":
                                last = nc.tensor.transpose(b[0:NC_BLK, tok(r)], scb[g][:, r, :], ident)
                            else:
                                last = nc.tensor.transpose(b[:, tok(r)], nSb[u % 2][:, r, tok(kt)], ident)
                        last.then_inc(*done("mm", ("mm", "nPT", *a, kt)))
                if k == "nV":
                    i, g, br = a
                    lo = HD * g
                    o = open_acc(("nO", i)) if (g, br) == (0, "c") else acc(("nO", i))
                    nk = 1 if br == "c" else i + 1
                    for kt in range(nk):
                        pe.wait_ge(*at("nPT", *a, kt))
                        n = NPT[(*a, kt)]
                        if br == "c":
                            pe.wait_ge(*at("vct"))
                            last = mm(o[lo:lo + HD, :], vct[:, g, :], nPb[n % 4][0:NC_BLK, :], start=True, stop=False)
                        else:
                            v = avt[:, kt, P * "sw".index(br) + HD * g:P * "sw".index(br) + HD * (g + 1)]
                            last = mm(o[lo:lo + HD, :], v, nPb[n % 4][:, :], start=False, stop=(br == "w" and kt == nk - 1))
                        last.then_inc(*done("mm", ("npv", n), *([("nO", i)] if (g, br, kt) == (1, "w", nk - 1) else [])))
                if k in ("upg", "upv"):
                    if blocks_of(step):
                        linear(step, blocks_of(step)[0], hn)
                if k == "L":
                    linear(a, blocks_of(step)[0], hn, "ln2" if a == ("upg", 0) else None)

        @block.vector
        def _(dve):
            chain = [0]

            def link(ins_):
                chain[0] += 1
                ins_.then_inc(*done("dve_step", ("dve_step", chain[0])))
                dve.wait_ge(*at("dve_step", chain[0]))

            def ssadd(ver, m):
                dve.wait_ge(*at("sq", ver, m))
                n = KD * ver + m
                if m == 1:
                    nc.vector.tensor_tensor(ssacc[:, :], sq[:, (n - 1) % 3, :], sq[:, n % 3, :], ALU.add)\
                        .then_inc(*done("ssadd", ("ssadd", ver, m)))
                else:
                    dve.wait_ge(*at("ssadd", ver, m - 1))
                    nc.vector.tensor_tensor(ssacc[:, :], ssacc[:, :], sq[:, n % 3, :], ALU.add)\
                        .then_inc(*done("ssadd", ("ssadd", ver, m)))

            def low(dst, src, hi):
                return nc.vector.tensor_tensor(dst, src, hi.bitcast(F32), ALU.subtract)

            for number, step in enumerate(STEPS):
                (hnh, hnl), (xgh, xgl) = roles(number)
                k, a = step[0], step[1:]
                if k == "psp":
                    L = BLKNO[("p", a[0])]
                    dve.wait_ge(*at("high", L))
                    low(hnl[:, 6:8, :], ring[:, L % NSLOT, :].rearrange("p (a b) -> p a b", a=2), hnh[:, 6:8, :])\
                        .then_inc(*done("split_p", ("split", L), ("slot_free", L)))
                if k == "load":
                    for m in range(1, KD - 1):
                        ssadd(0, m)
                    dve.wait_ge(*at("consts"))
                    nc.vector.tensor_scalar(negsink[:, :], rowb[:, R_SINK:R_SINK + ATT_HEADS], -1.0, None, ALU.mult)
                if k == "norm":
                    ver = a[0]
                    dve.wait_ge(*at("rms", ver))
                    link(nc.vector.reciprocal(nrm[:, 1, :], nrm[:, 0, :]))
                    nc.vector.tensor_tensor(rt[:, :].rearrange("p (a b) -> p a b", a=NT), over(ident, NT, 1),
                                            over(nrm[:, 1, :], P, 2), ALU.mult).then_inc(*done("ndiag", ("ndiag", ver)))
                if k == "he":
                    name, m = a
                    hi, lo = (xgh, xgl) if name in ("kv", "ln1") else (hnh, hnl)
                    buf = normed_tiles(name)
                    if m % 2:
                        dve.wait_ge(*at("hnhi", name, m - 1))
                        low(lo[:, m - 1, :], buf[(m - 1) % 4], hi[:, m - 1, :]).then_inc(*done("hn_dve", ("hn", name, m - 1)))
                    dve.wait_ge(*at("h", VERSION_OF[name], m))
                    if m >= 4:
                        dve.wait_ge(*at("hn", name, m - 4))
                    nc.vector.tensor_scalar(buf[m % 4], h[:, m, :], vec[:, V_NORM[name] + m:V_NORM[name] + m + 1], None, ALU.mult)\
                        .then_inc(*done("hf", ("hf", name, m)))
                if k == "nb" and a[0] in (1, 3, 4, 5, 6):
                    dve.wait_ge(*at("mm", "rb", a[0]))
                    nc.vector.tensor_copy(rtb1 if a[0] == 4 else rtb, acc(("rb", a[0]))[:, :]).then_inc(*done("rtb", ("rtb", a[0]), ("accfree", "rb", a[0])))
                if k == "hn":
                    ver = VERSION_OF[a[0]]
                    dve.wait_ge(*at("mm", "rb", ver))
                    for name in a:
                        hi, lo = (xgh, xgl) if name == "kv" else (hnh, hnl)
                        buf = normed_tiles(name)
                        for m in range(KD):
                            if m >= 4 and ver < 7:
                                dve.wait_ge(*at("hn", name, m - 4))
                            elif name == "attn":
                                dve.wait_ge(*at("hn", "kv", KD - 4 + m))
                            dst = res[:, m, :] if ver == 7 else buf[m % 4]
                            nc.vector.scalar_tensor_tensor(dst, h[:, m, :],
                                                           vec[:, V_NORM[name] + m:V_NORM[name] + m + 1],
                                                           acc(("rb", ver))[:, :],
                                                           ALU.mult, ALU.mult)\
                                .then_inc(*done("hf", ("result", m) if ver == 7 else ("hf", name, m),
                                                *([("accfree", "rb", ver)] if m == KD - 1 and name != "kv" else [])))
                            if ver < 7 and m % 2:
                                dve.wait_ge(*at("hnhi", name, m - 1))
                                low(lo[:, m - 1, :], buf[(m - 1) % 4], hi[:, m - 1, :])\
                                    .then_inc(*done("hn_dve", ("hn", name, m - 1)))
                if k == "proj" and a[1] < 6:
                    g, i = a
                    ch = [16 + g, 20 + g][i] if i < 2 else GT * g + i - 2
                    c = cva[(g * 6 + i) % 2]
                    b = ps(step)
                    dve.wait_ge(*at("conv0", g, i))
                    for s in range(1, TAPS):
                        w = vec[:, V_CW + (3 - s) * 24 + ch:V_CW + (3 - s) * 24 + ch + 1]
                        x = nc.vector.scalar_tensor_tensor(c[:, s:SEQ], b[:, 0:SEQ - s], w, c[:, s:SEQ], ALU.mult, ALU.add)
                        if s < TAPS - 1:
                            link(x)
                        else:
                            x.then_inc(*done("conv", ("conv", g, i), ("free", *step)))
                if k == "dt":
                    dve.wait_ge(*at("mm", "dt"))
                    b = ps(("dt",))[:, 0:P].rearrange("p (a b) -> p a b", a=NT)
                    link(nc.vector.tensor_tensor(dtmp, b, over(rowb[:, R_DTB:R_DTB + HEADS], NT, 1), ALU.add))
                    nc.vector.scalar_tensor_tensor(dtmp2, dtmp, -1.0, dtmp, ALU.mult, ALU.min)\
                        .then_inc(*done("dtabs", ("dtabs",), ("free", "dt")))
                    dve.wait_ge(*at("dtln"))
                    link(nc.vector.scalar_tensor_tensor(dtb, dtmp, 0.0, dtmp2, ALU.max, ALU.add))
                    dve.wait_ge(*at("aexp"))
                    link(nc.vector.tensor_tensor(da, dtb, over(aneg[:, :], NT, 1), ALU.mult))
                    nc.vector.tensor_scalar(da, da, -1.0, None, ALU.mult).then_inc(*done("da", ("da",)))
                if k == "ssd0":
                    g = a[0]
                    dve.wait_ge(*at("mm", "cb", g))
                    nc.vector.tensor_tensor(cbm, ps(("cb", g))[:, :].rearrange("p (a b) -> p a b", a=NT), over(tri, NT, 1),
                                            ALU.mult).then_inc(*done("cbm", ("cbm", g), ("free", "cb", g)))
                if k == "ssd1":
                    g, c = a
                    n = g * NT + c
                    dve.wait_ge(*at("mm", "xt", g, c))
                    if n >= 2:
                        q = ((n - 2) // NT, (n - 2) % NT)
                        dve.wait_ge(*at("mm", "yd", *q))
                        if q[1] < NT - 1:
                            dve.wait_ge(*at("xde", *q))
                    nc.vector.tensor_tensor(xdt[c % 2], ps(("xt", g, c))[:, :].rearrange("p (a b) -> p a b", a=HPG),
                                            over(dtb[:, c, g * HPG:(g + 1) * HPG], HD, 2), ALU.mult)\
                        .then_inc(*done("xdt", ("xdt", g, c), ("free", "xt", g, c)))
                    dve.wait_ge(*at("dec", g, c, 1))
                    dve.wait_ge(*at("cbm", g))
                    nc.vector.tensor_tensor(dec[c % 2], dec[c % 2], over(cbm[:, c, :], HPG, 1), ALU.mult)\
                        .then_inc(*done("decm", ("decm", g, c)))
                if k == "ssd2":
                    g, c = a
                    if c:
                        dve.wait_ge(*at("mm", "yo", g, c))
                        dve.wait_ge(*at("cums"))
                        link(nc.vector.tensor_tensor(yoe, ps(("yo", g, c))[:, :].rearrange("p (a b) -> p a b", a=HPG),
                                                     over(cums[:, 0, c * HEADS + g * HPG:c * HEADS + (g + 1) * HPG], HD, 2),
                                                     ALU.mult))
                        if g >= 1:
                            dve.wait_ge(*at("mm", "yt", g - 1, 3))
                        nc.vector.tensor_tensor(ytok[:, c, :].rearrange("p (a b) -> p a b", a=HPG), yoe,
                                                ps(("yd", g, c))[:, :].rearrange("p (a b) -> p a b", a=HPG), ALU.add)\
                            .then_inc(*done("ytok", ("ytok", g, c), ("free", "yd", g, c), ("free", "yo", g, c)))
                    if 1 <= c < NT - 1:
                        dve.wait_ge(*at("mm", "st", g, c))
                        dve.wait_ge(*at("pdec", g, c))
                        pn = prev[(c + 1) % 2]
                        nc.vector.tensor_tensor(pn, pn, ps(("st", g, c))[:, :].rearrange("p (a b) -> p a b", a=HPG), ALU.add)\
                            .then_inc(*done("prev", ("prev", g, c + 1), ("free", "st", g, c)))
                if k == "yt":
                    g, m = a
                    ti = GT * g + m
                    dve.wait_ge(*at("mm", *step))
                    nc.vector.scalar_tensor_tensor(xs[g % 2][:, m, :], xs[g % 2][:, m, :], vec[:, V_D + ti:V_D + ti + 1], ps(step)[:, :],
                                                   ALU.mult, ALU.add).then_inc(*done("yskip", ("yskip", g, m), ("free", *step)))
                    dve.wait_ge(*at("yskip", g, m))
                    dve.wait_ge(*at("zs", g, m))
                    nc.vector.tensor_tensor(xs[g % 2][:, m, :], xs[g % 2][:, m, :], zs[:, m, :], ALU.mult)\
                        .then_inc(*done("ygated", ("ygated", g, m)))

                def yadd(g, m):
                    dve.wait_ge(*at("ysq", g, m))
                    if m >= 2:
                        dve.wait_ge(*at("yadd", g, m - 1))
                    nc.vector.tensor_tensor(yac, yac, ysq2 if m == 2 else ysq, ALU.add).then_inc(*done("yadd", ("yadd", g, m)))

                if k == "yt" and a[1] >= 2:
                    yadd(a[0], a[1] - 1)
                if k == "gn":
                    yadd(a[0], 3)
                if k == "gn":
                    g = a[0]
                    dve.wait_ge(*at("grms", g))
                    link(nc.vector.reciprocal(nrm[:, 3, :], nrm[:, 2, :]))
                    nc.vector.tensor_tensor(ysq.rearrange("p (a b) -> p a b", a=NT), over(ident, NT, 1),
                                            over(nrm[:, 3, :], P, 2), ALU.mult).then_inc(*done("gdiag", ("gdiag", g)))
                if k == "gb":
                    g = a[0]
                    dve.wait_ge(*at("mm", "gb", g))
                    for m in range(GT):
                        ti = GT * g + m
                        nc.vector.scalar_tensor_tensor(xs[g % 2][:, m, :], xs[g % 2][:, m, :], vec[:, V_GN + ti:V_GN + ti + 1],
                                                       ps(step)[:, :], ALU.mult, ALU.mult)\
                            .then_inc(*done("ynf", ("ynf", g, m), *([("free", *step)] if m == GT - 1 else [])))
                        if m >= 2:
                            q = 2 * (m - 2)
                            dve.wait_ge(*at("ynhi", g, q))
                            x = GT * (g % 2) + q
                            low(xgl[:, x, :], xs[g % 2][:, q, :], xgh[:, x, :]).then_inc(*done("yn_dve", ("yn", g, q)))
                if k in ("sout", "dn") and a[0] < 3:
                    m = a[1]
                    dve.wait_ge(*at("mm", *step))
                    if a[0]:
                        dve.wait_ge(*at("hadd", k, a[0] - 1, m))
                    nc.vector.tensor_tensor(h[:, m, :], h[:, m, :], ps(step)[:, :], ALU.add)\
                        .then_inc(*done("hadd", ("hadd", *step), ("free", *step)))
                if h_update(step):
                    ver, m = h_update(step), a[1]
                    if m >= 2:
                        ssadd(ver, m - 1)
                    dve.wait_ge(*at("mm", *step))
                    if k != "out":
                        dve.wait_ge(*at("hadd", k, 2, m))
                    nc.vector.tensor_tensor(h[:, m, :], h[:, m, :], ps(step)[:, :], ALU.add)\
                        .then_inc(*done("h", ("h", ver, m), ("free", *step)))
                if k == "ple":
                    i, m = a
                    ver = 2 * i + 2 if i < 2 else 7
                    gb = gsig[m % 2]
                    if m >= 2:
                        ssadd(ver, m - 1)
                    dve.wait_ge(*at("rtb", [1, 3, 6][i]))
                    dve.wait_ge(*at("mm", *step))
                    if m >= 2:
                        dve.wait_ge(*at("h", ver, m - 2))
                    nc.vector.tensor_tensor(gb, ps(step)[:, :], rtb, ALU.mult)\
                        .then_inc(*done("gscaled", ("gscaled", i, m), ("free", *step)))
                    dve.wait_ge(*at("gsig", i, m))
                    dve.wait_ge(*at("pp", i, m))
                    link(nc.vector.tensor_tensor(gb, gb, pp[i][:, m, :], ALU.mult))
                    nc.vector.tensor_tensor(h[:, m, :], h[:, m, :], gb, ALU.add).then_inc(*done("h", ("h", ver, m)))
                if k == "rope_tables":
                    for m in range(KD - 4, KD):
                        dve.wait_ge(*at("hn", "ple0", m))
                    posf = small[:, 0, 0:NT]
                    link(nc.vector.tensor_copy(posf, pos[:, :]))
                    ang = rtmp[:, 0, :]
                    a3 = ang.rearrange("p (t f) -> p t f", t=NT)
                    link(nc.vector.tensor_tensor(a3, over(posf, 32, 2), over(rowb[:, R_FREQ:R_FREQ + 32], NT, 1), ALU.mult))
                    big = float(1.5 * 2 ** 23)
                    link(nc.vector.tensor_scalar(rtmp[:, 1, :], ang, float(1 / (2 * np.pi)), big, ALU.mult, ALU.add))
                    link(nc.vector.tensor_scalar(rtmp[:, 1, :], rtmp[:, 1, :], -big, None, ALU.add))
                    c1 = 6.28125
                    c2 = float(np.float32(2 * np.pi - c1))
                    c3 = float(2 * np.pi - c1 - c2)
                    for c in (c1, c2, c3):
                        link(nc.vector.scalar_tensor_tensor(ang, rtmp[:, 1, :], -c, ang, ALU.mult, ALU.add))
                    pi = 3.1415925
                    link(nc.vector.tensor_scalar(rtmp[:, 2, :], ang, pi, -pi, ALU.min, ALU.max))
                    nc.vector.scalar_tensor_tensor(rtmp[:, 3, :], rtmp[:, 2, :], -1.0, rtmp[:, 2, :], ALU.mult, ALU.max)\
                        .then_inc(*done("angles", ("angles",)))
                    dve.wait_ge(*at("cos"))
                    for j, (w, ws) in enumerate(((R_QN, R_QNS), (R_KN, R_KNS))):
                        for half in range(2):
                            cd = ctab[:, 2 * j, :].rearrange("p (t d) -> p t d", t=NT)[:, :, 32 * half:32 * half + 32]
                            sd = ctab[:, 2 * j + 1, :].rearrange("p (t d) -> p t d", t=NT)[:, :, 32 * half:32 * half + 32]
                            cs = rtmp[:, 5, :].rearrange("p (t d) -> p t d", t=NT)
                            sn = rtmp[:, 4, :].rearrange("p (t d) -> p t d", t=NT)
                            link(nc.vector.tensor_tensor(cd, cs, over(rowb[:, w + 32 * half:w + 32 * half + 32], NT, 1), ALU.mult))
                            link(nc.vector.tensor_tensor(sd, sn, over(rowb[:, ws + 32 * half:ws + 32 * half + 32], NT, 1), ALU.mult))
                        link(nc.vector.tensor_scalar(
                            ctab[:, 2 * j + 1, :].rearrange("p (t d) -> p t d", t=NT)[:, :, 0:32],
                            ctab[:, 2 * j + 1, :].rearrange("p (t d) -> p t d", t=NT)[:, :, 0:32], -1.0, None, ALU.mult))
                if k in ("kv", "q") and a[-1] == 3:
                    nh = 4 if k == "kv" else 8
                    w = nh * HD
                    stage = 0 if k == "kv" else 1 + a[0]
                    lo = 96 * (stage % 2)
                    for t in range(NT):
                        key = (k, *a[:-1], t)
                        dve.wait_ge(*at("qsq", *key))
                        nc.vector.tensor_reduce(flat[:, lo + t * nh:lo + (t + 1) * nh],
                                                qsq[t % 2][:, 0:w].rearrange("p (h d) -> p h d", h=nh), AXX,
                                                ALU.add).then_inc(*done("qss", ("qss", stage * NT + t)))
                    dve.wait_ge(*at("qrms", stage))
                    link(nc.vector.reciprocal(flat[:, lo + 64:lo + 64 + NT * nh], flat[:, lo + 32:lo + 32 + NT * nh]))
                    if k == "kv":
                        inv = flat[:, lo + 64:lo + 64 + NT * nh].rearrange("p (t h) -> p t h", t=NT)
                        link(nc.vector.tensor_tensor(inv, inv, over(nrm[:, 1, :], nh, 2), ALU.mult))
                if k == "ro":
                    stage, t = a
                    key = ("q", stage - 1, t) if stage else ("kv", t)
                    n = stage * NT + t
                    b = t % 2
                    nh = 8 if stage else 4
                    w = nh * HD
                    lo = 96 * (stage % 2)
                    q3 = qn[b][:, 0:w].rearrange("p (h d) -> p h d", h=nh)
                    nc.vector.tensor_tensor(q3, ps(key)[:, 0:w].rearrange("p (h d) -> p h d", h=nh),
                                            over(flat[:, lo + 64 + t * nh:lo + 64 + (t + 1) * nh], HD, 2), ALU.mult)\
                        .then_inc(*done("qn", ("qn", *a), ("free", *key)))
                    dve.wait_ge(*at("qn", *a))
                    sn = ctab[:, 1 if stage else 3, :].rearrange("p (t d) -> p t d", t=NT)[:, t, :]
                    r3 = rb[b][:, 0:w].rearrange("p (h d) -> p h d", h=nh)
                    nc.vector.tensor_tensor(r3[:, :, 0:32], q3[:, :, 32:64], over(sn[:, 0:32], nh, 1), ALU.mult)
                    link(nc.vector.tensor_tensor(r3[:, :, 32:64], q3[:, :, 0:32], over(sn[:, 32:64], nh, 1), ALU.mult))
                    dve.wait_ge(*at("ropea", *a))
                    if stage == 0:
                        dst = kr[:, t, :].rearrange("p (o h d) -> p o h d", o=1, h=4)
                        v = [x[b][:, 0:256].rearrange("p (o h d) -> p o h d", o=1, h=4) for x in (ra, rb)]
                    else:
                        dst = qr[:, t, (stage - 1) * SEQ:stage * SEQ].rearrange("p (j o d) -> p o j d", o=2, j=4)
                        v = [x[b][:, :].rearrange("p (o j d) -> p o j d", o=2, j=4) for x in (ra, rb)]
                    nc.vector.tensor_tensor(dst, v[0], v[1], ALU.add).then_inc(*done("roped", ("roped", *key)))
                if k == "aS":
                    n, g = a
                    u = n * KV_HEADS + g
                    w = P if n == 0 else 256
                    per = SEQ // w
                    s = Sb[u % 3]
                    mask = swa[:, P:256] if n == 0 else swa
                    sm = small[:, 4 * (u % 3):4 * (u % 3) + 4, :]
                    if u >= 3:
                        dve.wait_ge(*at("mm", "aPT", *divmod(u - 3, KV_HEADS), 0 if u - 3 < KV_HEADS else 1))
                    for j in range(4 // per):
                        dve.wait_ge(*at("mm", "aS", n, g, j))
                        nc.vector.tensor_tensor(s[:, per * j:per * (j + 1), 0:w],
                                                ps(("aS", n, g, j))[:, :].rearrange("p (a b) -> p a b", a=per),
                                                over(mask, per, 1), ALU.add)\
                            .then_inc(*done("amask", ("amask", n, g, j), ("free", "aS", n, g, j)))
                    dve.wait_ge(*at("amask", n, g, 4 // per - 1))
                    link(nc.vector.tensor_reduce(sm[:, 0, 0:4], s[:, :, 0:w], AXX, ALU.max))
                    link(nc.vector.scalar_tensor_tensor(sm[:, 1, 0:4], sm[:, 0, 0:4], -1.0, negsink[:, 4 * g:4 * g + 4],
                                                        ALU.mult, ALU.min))
                    nc.vector.tensor_tensor(sm[:, 1, 4:8], sm[:, 1, 0:4], rowb[:, R_SINK + 4 * g:R_SINK + 4 * g + 4],
                                            ALU.add).then_inc(*done("anegm", ("anegm", n, g)))
                if k == "aR":
                    n, g = a
                    u = n * KV_HEADS + g
                    sm = small[:, 4 * (u % 3):4 * (u % 3) + 4, :]
                    dve.wait_ge(*at("aesink", n, g))
                    link(nc.vector.tensor_tensor(sm[:, 3, 4:8], sm[:, 2, 0:4], sm[:, 1, 8:12], ALU.add))
                    nc.vector.reciprocal(sm[:, 3, 0:4], sm[:, 3, 4:8]).then_inc(*done("arec", ("arec", n, g)))
                if k == "aT":
                    n, g = a
                    u = n * KV_HEADS + g
                    if n:
                        dve.wait_ge(*at("mm", "aPT", n, g, 1))
                        if u >= 2:
                            dve.wait_ge(*at("pv", *divmod(u - 2, KV_HEADS)))
                        nc.vector.tensor_copy(PTb[u % 2][:, 1, :], ps(("aPT", n, g, 1))[:, :])\
                            .then_inc(*done("aPT_dve", ("aPT", n, g, 1), ("free", "aPT", n, g, 1)))
                if k == "aO":
                    n, g = a
                    G2 = g // 2
                    dve.wait_ge(*at("pv", n, g))
                    dve.wait_ge(*at("gs", KD - 1))
                    if n:
                        dve.wait_ge(*at("og", n - 1, G2))
                    nc.vector.tensor_tensor(ogf[G2],
                                            acc(("aO", n, G2))[:, :].rearrange("p (a b) -> p a b", a=4),
                                            gs[:, 4 * G2:4 * G2 + 4, tok(n)], ALU.mult)\
                        .then_inc(*done("ogf", ("ogf", n, G2), ("accfree", "aO", n, G2)))
                if k == "mrow":
                    dve.wait_ge(*at("mm", "mi"))
                    nc.vector.tensor_scalar(mrow[0], ps(("mi",))[0:4, :], mbias[:, 0:1], None, ALU.add)\
                        .then_inc(*done("mi", ("mi_row",), ("free", "mi")))
                    dve.wait_ge(*at("mm", "mf"))
                    nc.vector.tensor_scalar(mrow[1], ps(("mf",))[0:4, :], mbias[:, 1:2], None, ALU.add)\
                        .then_inc(*done("mf", ("mf_row",), ("free", "mf")))
                    dve.wait_ge(*at("mf_row"))
                    nc.vector.scalar_tensor_tensor(mrow[2], mrow[1], -1.0, mrow[1], ALU.mult, ALU.min)\
                        .then_inc(*done("mfabs", ("mfabs",)))
                    link(nc.vector.memset(mrow[4], 0.0))
                if k == "mscan":
                    dve.wait_ge(*at("mfln"))
                    link(nc.vector.scalar_tensor_tensor(mrow[1], mrow[1], 0.0, mrow[2],
                                                        ALU.min, ALU.subtract))
                    link(nc.vector.tensor_tensor_scan(mrow[3], mrow[1], mrow[4], 0.0, ALU.add, ALU.add))
                    nc.vector.tensor_tensor(mrow[0], mrow[0], mrow[3], ALU.subtract)\
                        .then_inc(*done("mrrow", ("mrrow",)))
                    dve.wait_ge(*at("mrrow"))
                    link(nc.vector.tensor_tensor_scan(mrow[1], mrow[0], mrow[0], 0.0, ALU.max, ALU.max))
                    nc.vector.tensor_tensor(mrow[2], mrow[1], mrow[3], ALU.add)\
                        .then_inc(*done("mmt", ("mmt",)))
                if k in ("mq", "mk", "aq", "ak", "cmp_in", "mo"):
                    dst = {"mq": mqT, "mk": mkT, "aq": aqT, "ak": akT, "cmp_in": ckv, "mo": moT}[k][:, a[0], :]
                    dve.wait_ge(*at("rtb", 4))
                    dve.wait_ge(*at("mm", *step))
                    nc.vector.scalar_tensor_tensor(dst, ps(step)[:, :], {"mq": P ** -0.5, "aq": HD ** -0.5}.get(k, 1.0), rtb1,
                                                   ALU.mult, ALU.mult)\
                        .then_inc(*done("scaled", ("scaled" if k == "mo" else "done", *step), ("free", *step)))
                if k == "cmp_in":
                    j = a[0]
                    dve.wait_ge(*at("done", *step))
                    dve.wait_ge(*at("czero", j))
                    for g in range(2):
                        rows = slice(HD * g, HD * (g + 1))
                        raw = ckv[rows, j, :]
                        src = bass.AP(tensor=ckv.tensor, offset=raw.offset,
                                      ap=[list(raw.ap[0]), [1, CMP_BLOCK], [CMP_STRIDE, NC_BLK]])
                        last = nc.vector.tensor_tensor(cblk[j][rows, :, NC_BLK * g:NC_BLK * (g + 1)], src,
                                                       over(peT[rows, j, :], NC_BLK, 2), ALU.add)
                    last.then_inc(*done("cblk", ("cblk", j)))
                if k == "cmp":
                    j = a[0]
                    x = ctm[:, 0, :].rearrange("p (g n) -> p g n", g=2)[:, :, 0:NC_BLK]
                    y = ctm[:, 1, :].rearrange("p (g n) -> p g n", g=2)[:, :, 0:NC_BLK]
                    z = ctm[:, 2, :].rearrange("p (g n) -> p g n", g=2)[:, :, 0:NC_BLK]
                    if j == 0:
                        dve.wait_ge(*at("cblk", 1))
                        link(nc.vector.memset(ctm[:, :, :], 0.0))
                    dve.wait_ge(*at("mm", "chid", j))
                    nc.vector.tensor_copy(x, acc(("chid", j))[:, 0:2 * NC_BLK].rearrange("p (g n) -> p g n", g=2))\
                        .then_inc(*done("chidc", ("chidc", j), ("accfree", "chid", j)))
                    dve.wait_ge(*at("chidc", j))
                    link(nc.vector.tensor_tensor(y, x, x, ALU.mult))
                    link(nc.vector.tensor_scalar(y, y, 0.044715, 1.0, ALU.mult, ALU.add))
                    nc.vector.tensor_tensor(y, y, x, ALU.mult).then_inc(*done("gelu_in", ("gelu_in", j)))
                    dve.wait_ge(*at("ctanh", j))
                    link(nc.vector.tensor_scalar(z, y, 1.0, 0.5, ALU.add, ALU.mult))
                    nc.vector.tensor_tensor(chid[:, j, :].rearrange("p (g n) -> p g n", g=2)[:, :, 0:NC_BLK], z, x, ALU.mult)\
                        .then_inc(*done("gelu", ("gelu", j)))
                    dve.wait_ge(*at("gelu", j))

                def marg(n):
                    h_, s = divmod(n, NT)
                    if h_ == M_HEADS:
                        return
                    if s == 0:
                        dve.wait_ge(*at("Mneg", h_))
                    if n >= 2:
                        dve.wait_ge(*at("wt", *divmod(n - 2, NT)))
                    nc.vector.tensor_scalar(wt[n % 2][:, 0:SEQ - P * s], Mneg[h_ % 2][:, P * s:SEQ], rcol[:, s, h_:h_ + 1], 0.0,
                                            ALU.add, ALU.min).then_inc(*done("marg", ("marg", h_, s)))

                if k == "mA":
                    dve.wait_ge(*at("rcol"))
                    marg(0)
                if k == "mB":
                    h_ = a[0]
                    for s in range(NT):
                        n = h_ * NT + s
                        marg(n + 1)
                        w = SEQ - P * s
                        dve.wait_ge(*at("mexpd", h_, s))
                        dve.wait_ge(*at("mm", "KQ", h_, s))
                        if n >= 2:
                            dve.wait_ge(*at("numden", *divmod(n - 2, NT)))
                        nc.vector.tensor_tensor(wk[n % 2][:, 0:w], wt[n % 2][:, 0:w], ps(("KQ", h_, s))[:, 0:w], ALU.mult)\
                            .then_inc(*done("wt", ("wt", h_, s), ("free", "KQ", h_, s)))
                if k == "mfac":
                    n = M_HEADS * NT
                    dt_ = acc(("dtok",))
                    dve.wait_ge(*at("mss", M_HEADS - 1))
                    dve.wait_ge(*at("ecol"))
                    link(nc.vector.tensor_copy(mst[:, 1, :], dt_[:, 0:n]))
                    link(nc.vector.scalar_tensor_tensor(mst[:, 1, :], mst[:, 1, :], -1.0, mst[:, 1, :], ALU.mult, ALU.max))
                    link(nc.vector.tensor_tensor(mst[:, 1, :], mst[:, 1, :], mst[:, 0, :], ALU.max))
                    link(nc.vector.reciprocal(mst[:, 2, :], mst[:, 1, :]))
                    nc.vector.tensor_tensor(mst[:, 3, :], dt_[:, n:2 * n], mst[:, 2, :], ALU.mult)\
                        .then_inc(*done("mcol", ("mcol",), ("accfree", "dtok")))
                    dve.wait_ge(*at("mcol"))
                    nc.vector.tensor_tensor(mst[:, 3, :], mst[:, 3, :], mst[:, 2, :], ALU.mult).then_inc(*done("mvar", ("mvar",)))
                    dve.wait_ge(*at("mrms"))
                    link(nc.vector.reciprocal(mst[:, 5, :], mst[:, 4, :]))
                    link(nc.vector.tensor_tensor(mst[:, 5, :], mst[:, 5, :], mst[:, 2, :], ALU.mult))

                def mdiagonal(h_):
                    if h_ >= 2:
                        dve.wait_ge(*at("mm", "mg", h_ - 2))
                    nc.vector.tensor_tensor(mdiag[h_ % 2].rearrange("p (a b) -> p a b", a=NT), over(ident, NT, 1),
                                            over(mst[:, 5, NT * h_:NT * (h_ + 1)], P, 2), ALU.mult)\
                        .then_inc(*done("mdiag", ("mdiag", h_)))

                if k == "mfac":
                    mdiagonal(0)
                if k == "mg":
                    h_ = a[0]
                    if h_ + 1 < M_HEADS:
                        mdiagonal(h_ + 1)
                    dve.wait_ge(*at("hm", h_))
                    dve.wait_ge(*at("mm", *step))
                    nc.vector.scalar_tensor_tensor(hm[:, h_, :], hm[:, h_, :], vec[:, V_MN + h_:V_MN + h_ + 1],
                                                   ps(step)[:, :], ALU.mult, ALU.mult)\
                        .then_inc(*done("mnormed", ("mnormed", h_), ("free", *step)))
                    dve.wait_ge(*at("mnormed", h_))
                    dve.wait_ge(*at("done", "mo", h_))
                    nc.vector.tensor_tensor(hm[:, h_, :], hm[:, h_, :], moT[:, h_, :], ALU.mult)\
                        .then_inc(*done("mgated", ("mgated", h_)))
                if k == "nS":
                    i, g, br = a
                    u = NSEQ[a]
                    q = 4 * "csw".index(br)
                    sm = small[:, q:q + 4, :]
                    h0 = 4 * g
                    if br == "c":
                        s = scb[g]
                        dve.wait_ge(*at("cmpb"))
                        if i:
                            dve.wait_ge(*at("mm", "nPT", i - 1, g, "c", 0))
                        dve.wait_ge(*at("mm", "nS", *a, 0))
                        nc.vector.tensor_tensor(s[:, :, :], ps(("nS", *a, 0))[:, 0:P].rearrange("p (r c) -> p r c", r=4)[:, :, 0:NC_BLK],
                                                cmpb[:, i, h0:h0 + 4, :], ALU.add)\
                            .then_inc(*done("nmask", ("nmask", *a), ("free", "nS", *a, 0)))
                        dve.wait_ge(*at("nmask", *a))
                        link(nc.vector.tensor_reduce(sm[:, 0, 0:4], s[:, :, :], AXX, ALU.max))
                        nc.vector.tensor_tensor(s[:, :, :], s[:, :, :], over(sm[:, 0, 0:4], NC_BLK, 2), ALU.subtract)\
                            .then_inc(*done("nnegm", ("nnegm", *a)))
                    else:
                        w = P * (i + 1)
                        s = nSb[u % 2]
                        if i == 0:
                            dve.wait_ge(*at("alibi", g))
                        if NPREV[a] is not None:
                            dve.wait_ge(*at("mm", "nPT", *NPREV[a], NPREV[a][0]))
                        for r in range(4):
                            dve.wait_ge(*at("mm", "nS", *a, r))
                            nc.vector.tensor_tensor_reduce(out=s[:, r, 0:w], in0=ps(("nS", *a, r))[:, 0:w],
                                                           in1=alibi[:, h0 + r, SEQ - w:SEQ], scale=1.0, scalar=-3e38,
                                                           op0=ALU.add, op1=ALU.max, accum_out=sm[:, 0, r:r + 1])\
                                .then_inc(*done("nmask", ("nmask", *a, r), ("free", "nS", *a, r)))
                        dve.wait_ge(*at("nmask", *a, 3))
                        nc.vector.tensor_scalar(sm[:, 1, 0:4], sm[:, 0, 0:4], -1.0, None, ALU.mult)\
                            .then_inc(*done("nnegm", ("nnegm", *a)))
                if k == "nR":
                    i, g, br = a
                    q = 4 * "csw".index(br)
                    sm = small[:, q:q + 4, :]
                    h0 = 4 * g
                    gcol = gat[:, i, :].rearrange("p (h b) -> p b h", b=3)[:, "csw".index(br), h0:h0 + 4]
                    dve.wait_ge(*at("nexp", *a))
                    if br == "c":
                        s = scb[g]
                        link(nc.vector.tensor_reduce(sm[:, 2, 0:4], s[:, :, :], AXX, ALU.add))
                        link(nc.vector.reciprocal(sm[:, 3, 4:8], sm[:, 2, 0:4]))
                        if i == 0:
                            link(nc.vector.tensor_scalar(sm[:, 3, 4:8], sm[:, 3, 4:8], rowvalid, None, ALU.mult))
                        dve.wait_ge(*at("avg", i))
                        link(nc.vector.tensor_tensor(sm[:, 3, 0:4], sm[:, 3, 4:8], gcol, ALU.mult))
                        nc.vector.tensor_tensor(s[:, :, :], s[:, :, :], over(sm[:, 3, 0:4], NC_BLK, 2), ALU.mult)\
                            .then_inc(*done("nprobc", ("nprob", *a)))
                    else:
                        link(nc.vector.reciprocal(sm[:, 3, 4:8], sm[:, 2, 0:4]))
                        nc.vector.tensor_tensor(sm[:, 3, 0:4], sm[:, 3, 4:8], gcol, ALU.mult)\
                            .then_inc(*done("nrec", ("nrec", *a)))
                if k == "nT":
                    i, g, br = a
                    for kt in range(1 if br == "c" else i + 1):
                        n = NPT[(*a, kt)]
                        if n % 2 == 1:
                            dve.wait_ge(*at("mm", "nPT", *a, kt))
                            if n >= 4:
                                dve.wait_ge(*at("npv", n - 4))
                            rows = NC_BLK if br == "c" else P
                            nc.vector.tensor_copy(nPb[n % 4][0:rows, :], ps(("nPT", *a, kt))[0:rows, :])\
                                .then_inc(*done("nPT_dve", ("nPT", *a, kt), ("free", "nPT", *a, kt)))
                if k == "nO":
                    i = a[0]
                    dve.wait_ge(*at("noghi", i))
                    nc.vector.tensor_tensor(xgl[:, 4:8, tok(i)], acc(("nO", i))[:, :].rearrange("p (a b) -> p a b", a=4),
                                            xgh[:, 4:8, tok(i)].bitcast(F32), ALU.subtract)\
                        .then_inc(*done("nog", ("nog", i), ("accfree", "nO", i)))
                if k == "upg":
                    m = a[0]
                    b = fg[m % 2]
                    c = fca[m % 2]
                    dve.wait_ge(*at("rtb", 5))
                    dve.wait_ge(*at("mm", "upg", m))
                    if m >= 2:
                        dve.wait_ge(*at("fconv", m - 2))
                    nc.vector.tensor_tensor(b, ps(("upg", m))[:, :], rtb, ALU.mult)\
                        .then_inc(*done("fscaled", ("fscaled", m), ("free", "upg", m)))
                    dve.wait_ge(*at("fscaled", m))
                    dve.wait_ge(*at("fconv0", m))
                    for s in range(1, 3):
                        w = vec[:, V_C2W + (2 - s) * FT + m:V_C2W + (2 - s) * FT + m + 1]
                        x = nc.vector.scalar_tensor_tensor(c[:, s:SEQ], b[:, 0:SEQ - s], w, c[:, s:SEQ], ALU.mult, ALU.add)
                        if s == 1:
                            link(x)
                        else:
                            x.then_inc(*done("fconv", ("fconv", m)))
                if k == "upv":
                    m = a[0]
                    dve.wait_ge(*at("mm", "upv", m))
                    dve.wait_ge(*at("fsilu", m))
                    nc.vector.tensor_tensor(fsl[m % 2], fsl[m % 2], ps(("upv", m))[:, :], ALU.mult)\
                        .then_inc(*done("fprod", ("fprod", m), ("free", "upv", m)))
                    dve.wait_ge(*at("fprod", m))
                    nc.vector.tensor_tensor(fsl[m % 2], fsl[m % 2], rtb, ALU.mult).then_inc(*done("fff", ("fff", m)))
    return ev.seen


NSEQ, NPREV, NPT = {}, {}, {}
for _s in STEPS:
    if _s[0] == "nS":
        _a = _s[1:]
        _big = [x for x in NSEQ if x[2] != "c"]
        NSEQ[_a] = len(_big)
        if _a[2] != "c":
            NPREV[_a] = _big[-2] if len(_big) >= 2 else None
    if _s[0] == "nT":
        for _k in range(1 if _s[3] == "c" else _s[1] + 1):
            NPT[(*_s[1:], _k)] = len(NPT)


def pack(v):
    f = {k: np.asarray(x) for k, x in v.items()}

    def cols(w, order):
        return w[:, order]

    pair16 = np.concatenate([np.arange(64) + 64 * hh for G in range(2) for r in range(4) for hh in (8 * G + r, 8 * G + 4 + r)])
    pair8 = np.concatenate([np.arange(64) + 64 * hh for r in range(4) for hh in (r, 4 + r)])
    wi = f["w_in_2"][0]
    o = np.cumsum([0, 512, 512, 512, 512, 4, 4, 512] + [128] * 6 + [24])
    mq, mk, mv, mo, mi, mf, aq, akc, avc, aks, avs, akw, avw, ag = (wi[:, o[i]:o[i + 1]] for i in range(14))
    stationary = {
        "ssm_in": f["ssm_in_w"][0], "attn_out": f["attn_out_w"][0][pair16],
        "attn_gate": cols(f["attn_in_w"][0][:, 1024:], pair16),
        "w_out": np.concatenate([f["w_out_2"][0][:512], f["w_out_2"][0][512:][pair8]]),
        "mq": mq, "mk": mk, "mo": mo, "aq": cols(aq, pair8), "ak": np.concatenate([aks, akw], 1),
        "cmp_in": np.concatenate([akc, avc], 1), "upg": f["w_up_2"][0][:, :D_FF], "upv": f["w_up_2"][0][:, D_FF:],
    }
    moving = {
        "kv": f["kv_w"], "attn_q": f["attn_in_w"][0][:, :1024], "mv": mv,
        "avg": np.concatenate([avs, avw, ag, mi, mf, np.zeros((D, SEQ - 288), np.float32)], 1),
    }
    gates = [f["ple_gate_w"][0], f["ple_gate_w"][1], f["w_ple_gate_2"][0]]
    projs = [f["ple_proj_w"][0], f["ple_proj_w"][1], f["w_ple_proj_2"][0]]
    ps_ = [f["p"][0, 0], f["p"][1, 0], f["p_2"][0, 0]]
    w1 = [f["cmp_k_w1_2"][0], f["cmp_v_w1_2"][0]]

    def block(b):
        k = b[0]
        if k == "p":
            return ps_[b[1]].T.reshape(2, P, SEQ).transpose(1, 0, 2)
        if k == "ple_proj":
            return projs[b[1]][:, b[2] * SEQ:(b[2] + 1) * SEQ].reshape(2, P, SEQ).transpose(1, 0, 2)
        if k == "ple_gate":
            return gates[b[1]][:, b[2] * P:(b[2] + 1) * P].reshape(KD, P, P).transpose(1, 0, 2)
        if k == "cmp_w1":
            w = w1[b[1]].reshape(CMP_BLOCK, HD, P)[8 * b[2]:8 * b[2] + 8].transpose(1, 0, 2)
            return np.concatenate([w, w], 0)
        if k == "dt":
            w = np.concatenate([f["ssm_in_w"][0][:, -HEADS:], np.zeros((D, P - HEADS), np.float32)], 1)
            return w.reshape(KD, P, P).transpose(1, 0, 2)
        if k in ("sout", "dn"):
            w = {"sout": f["ssm_out_w"][0], "dn": f["w_down_2"][0]}[k][512 * b[1]:512 * (b[1] + 1), 256 * b[2]:256 * (b[2] + 1)]
            return w.reshape(4, P, 256).transpose(1, 0, 2)
        if k in moving:
            w = moving[k][:, (b[1] * SEQ if k == "attn_q" else 0):][:, :SEQ]
            return w[256 * b[-1]:256 * (b[-1] + 1)].reshape(2, P, SEQ).transpose(1, 0, 2)
        w = stationary[k][D * b[2]:D * (b[2] + 1), b[1] * P:(b[1] + 1) * P]
        return w.reshape(KD, P, P).transpose(1, 0, 2)

    res = {"wstream": np.stack([block(b).reshape(P, BLK) for b in BLOCKS])}
    res["xT"] = f["x"][0].T.reshape(KD, P, SEQ).transpose(1, 0, 2)

    def tiles(x):
        return x.reshape(-1, P).T

    norms = [f["ssm_norm_w"], f["kv_norm_w"], f["attn_norm_w"], f["ple_norm_w"][0], f["ple_norm_w"][1], f["ln1_g_2"],
             f["ln2_g_2"], f["ple_norm_g_2"], f["final_g_2"]]
    vec = [tiles(x) for x in norms] + [tiles(f["ssm_conv_w"]), tiles(f["ssm_conv_b"]), tiles(f["ssm_gnorm_w"]),
                                       tiles(np.repeat(f["ssm_d"][0], HD)), tiles(f["conv_w_2"]), tiles(f["conv_b_2"]),
                                       tiles(f["mlstm_norm_g_2"])]
    res["vec"] = np.concatenate(vec, 1)
    assert res["vec"].shape == (P, NV)
    qw, kw = f["q_norm_w"][0], f["k_norm_w"]
    half = 32
    inv_freq = (10000.0 ** (-(np.arange(half, dtype=np.float32) * 2.0 / HD))).astype(np.float32)
    row = np.concatenate([f["ssm_dt_bias"][0], f["ssm_a_log"][0], qw, qw[half:], qw[:half], kw, kw[half:], kw[:half],
                          f["attn_sinks"][0], inv_freq])
    res["rowb"] = np.broadcast_to(row, (P, NR))
    res["w2c"] = np.stack([f["cmp_k_w2_2"][0], f["cmp_v_w2_2"][0]], 1)
    pe = np.stack([f["cmp_pos_k_2"][0].T, f["cmp_pos_v_2"][0].T], 1)
    res["peT"] = np.concatenate([pe, pe], 0)
    res["mbias"] = f["mlstm_gate_bias_2"][0].reshape(2, 4).T
    res["pos"] = f["positions"][0].reshape(NT, P).T.astype(np.int32)
    res.update(constants())
    return {k: np.ascontiguousarray(x) for k, x in res.items()}


def constants():
    i = np.arange(P)
    con = np.zeros((P, NCON), np.float32)
    con[:, C_ID:C_ID + P] = np.eye(P)
    con[:, C_T:C_T + P] = i[:, None] <= i[None, :]
    con[:, C_U:C_U + P] = i[:, None] > i[None, :]
    con[:, C_ONE:C_ONE + P] = 1.0
    c = np.arange(256)
    con[:, C_SWA:C_SWA + 256] = np.where((c[None, :] - P <= i[:, None]) & (c[None, :] > i[:, None]), 0.0, NEG)
    slope = 2.0 ** -(np.arange(A_HEADS) + 1.0)
    t = np.arange(SEQ).reshape(NT, P).T
    end = CMP_STRIDE * np.arange(NC_BLK) + CMP_BLOCK - 1
    dist = t[:, :, None, None] - end[None, None, None, :]
    cb = np.where(dist >= 0, -slope[None, None, :, None] * dist, NEG)
    con[:, C_RV] = i >= CMP_BLOCK - 1
    sel = np.zeros((4, 4, P), np.float32)
    for h in range(4):
        sel[h, h] = 1.0
    d = 384 + i[:, None, None] - np.arange(SEQ)[None, None, :]
    ali = np.where(d >= 0, -slope[None, :, None] * d, NEG).astype(np.float32)
    return {"con": con, "alibi": ali, "cmpb": cb.reshape(P, -1).astype(np.float32), "sel": sel}


def kernel(**inputs):
    import concourse.bacc as bacc
    from concourse.bass_utils import run_bass_kernel_spmd as run

    arrays = pack(inputs)
    known = None
    for _ in range(2):
        nc = bacc.Bacc("TRN2", target_bir_lowering=False, num_devices=1)
        aps = {k: nc.dram_tensor("in_" + k, x.shape, mybir.dt.from_np(x.dtype), kind="ExternalInput").ap()
               for k, x in arrays.items()}
        out = nc.dram_tensor("outT", (KD, P, SEQ), F32, kind="ExternalOutput").ap()
        known = build(nc, aps, out, known)
    r = run(nc, [{"in_" + k: x for k, x in arrays.items()}], core_ids=[0])
    return r.results[0]["outT"].reshape(D, SEQ).T[None]
```
